# Optimizing a Trainium2 kernel written in Bass

```python
import numpy as np
import jax
import jax.numpy as jnp
from jax import lax

D_MODEL = 2048
BATCH = 1
SEQ = 256
DEPTH = 2
DEC_BATCH = 8
DEC_SEQ = 1
PAST_LEN = 2048
PAGE_SIZE = 128

N_A_LAYERS = DEPTH // 2
N_B_LAYERS = DEPTH - N_A_LAYERS
SSM_GROUP = 16
SSM_GROUPS = D_MODEL // SSM_GROUP
SSM_STATE = 64
DT_MIN = 0.001
DT_MAX = 0.1
N_HEADS = 16
HEAD_DIM = D_MODEL // N_HEADS
N_KV_HEADS = 4
GQA_REP = N_HEADS // N_KV_HEADS
CMP_BLOCK = 32
CMP_STRIDE = 16
CMP_PARTS = CMP_BLOCK // CMP_STRIDE
CMP_HIDDEN = HEAD_DIM
SLC_BLOCK = 64
N_SELECT = 16
WINDOW = 512
WIN_QBLOCK = 128
SLC_QBLOCK = 32
ROPE_THETA = 10000.0
ATTN_SCALE = HEAD_DIM ** -0.5
D_FF = -(-8 * D_MODEL // (3 * 256)) * 256
PLE_DIM = 256
NORM_EPS = 1e-6
NEG_INF = -1e30
FORCED_SCORE = 1e9

kernel_name = 'yoco_s5_nsa_decode_step'

def rmsnorm(x, g):
    xf = x.astype(jnp.float32)
    y = xf * lax.rsqrt(jnp.mean(xf * xf, axis=-1, keepdims=True) + NORM_EPS)
    return (y * g.astype(jnp.float32)).astype(x.dtype)

def rope(x, pos):
    half = HEAD_DIM // 2
    inv_freq = ROPE_THETA ** (-jnp.arange(half, dtype=jnp.float32) / half)
    ang = pos.astype(jnp.float32)[:, None] * inv_freq[None, :]
    cos = jnp.cos(ang)[:, None, :]
    sin = jnp.sin(ang)[:, None, :]
    xf = x.astype(jnp.float32)
    x1, x2 = xf[..., :half], xf[..., half:]
    return jnp.concatenate([x1 * cos - x2 * sin, x2 * cos + x1 * sin], axis=-1).astype(x.dtype)

def masked_softmax(s, mask):
    s = jnp.where(mask, s, NEG_INF)
    m = jnp.max(s, axis=-1, keepdims=True)
    p = jnp.exp(s - m) * mask
    return p / jnp.maximum(jnp.sum(p, axis=-1, keepdims=True), 1e-30)

def swiglu(h, wg, wu, wd):
    return (jax.nn.silu(h @ wg) * (h @ wu)) @ wd

def s5_mixer(u, h0_re, h0_im, a_re, a_im, log_dt, b_re, b_im, c_re, c_im, d, w_glu, b_glu):
    bsz, t = u.shape[:2]
    f32 = jnp.float32
    a_re = a_re.astype(f32)
    a_im = a_im.astype(f32)
    dt = jnp.exp(log_dt.astype(f32))[:, None]
    mag = jnp.exp(dt * a_re)
    ab_re, ab_im = mag * jnp.cos(dt * a_im), mag * jnp.sin(dt * a_im)
    den = a_re * a_re + a_im * a_im
    nr, ni = ab_re - 1.0, ab_im
    cf_re = (nr * a_re + ni * a_im) / den
    cf_im = (ni * a_re - nr * a_im) / den
    uf = u.astype(f32).reshape(bsz, t, SSM_GROUPS, SSM_GROUP)
    bu_re = jnp.einsum('btgh,gph->btgp', uf, b_re.astype(f32))
    bu_im = jnp.einsum('btgh,gph->btgp', uf, b_im.astype(f32))
    x_re = cf_re * bu_re - cf_im * bu_im
    x_im = cf_re * bu_im + cf_im * bu_re
    x_re = x_re.at[:, 0].add(ab_re * h0_re - ab_im * h0_im)
    x_im = x_im.at[:, 0].add(ab_re * h0_im + ab_im * h0_re)
    a_t_re = jnp.broadcast_to(ab_re, (1, t, SSM_GROUPS, SSM_STATE))
    a_t_im = jnp.broadcast_to(ab_im, (1, t, SSM_GROUPS, SSM_STATE))

    def combine(e1, e2):
        a1r, a1i, b1r, b1i = e1
        a2r, a2i, b2r, b2i = e2
        return (a2r * a1r - a2i * a1i, a2r * a1i + a2i * a1r,
                a2r * b1r - a2i * b1i + b2r, a2r * b1i + a2i * b1r + b2i)

    _, _, h_re, h_im = lax.associative_scan(combine, (a_t_re, a_t_im, x_re, x_im), axis=1)
    y = (jnp.einsum('btgp,ghp->btgh', h_re, c_re.astype(f32))
         - jnp.einsum('btgp,ghp->btgh', h_im, c_im.astype(f32)))
    y = y.reshape(bsz, t, D_MODEL) + d.astype(f32) * u.astype(f32)
    g = jax.nn.gelu(y)
    z = g @ w_glu.astype(f32) + b_glu.astype(f32)
    out = z[..., :D_MODEL] * jax.nn.sigmoid(z[..., D_MODEL:])
    return out.astype(u.dtype), h_re[:, -1], h_im[:, -1]

def shared_kv_rows(h, pos, norm_kv_g, kv_w):
    bsz, t = h.shape[:2]
    kv = (rmsnorm(h, norm_kv_g) @ kv_w).reshape(bsz, t, 6, N_KV_HEADS, HEAD_DIM)
    ck, cv, sk, sv, wk, wv = [kv[:, :, i] for i in range(6)]
    return ck, cv, rope(sk, pos), sv, rope(wk, pos), wv

def compress_rows(rows, w1, b1, w2):
    bsz, t = rows.shape[:2]
    n_units = t // CMP_STRIDE
    n_cmp = n_units - CMP_PARTS + 1
    units = rows[:, :n_units * CMP_STRIDE].reshape(bsz, n_units, CMP_STRIDE, N_KV_HEADS, HEAD_DIM)
    w1p = w1.reshape(CMP_PARTS, CMP_STRIDE, HEAD_DIM, CMP_HIDDEN)
    h = b1
    for j in range(CMP_PARTS):
        h = h + jnp.einsum('bnsgd,sdh->bngh', units[:, j:j + n_cmp], w1p[j])
    return jax.nn.gelu(h) @ w2

def compress_kv(ck, cv, w):
    k_cmp = compress_rows(ck, w['cmp_k_w1'], w['cmp_k_b1'], w['cmp_k_w2'])
    n_cmp = k_cmp.shape[1]
    k_cmp = rope(k_cmp, jnp.arange(n_cmp, dtype=jnp.int32) * CMP_STRIDE + (CMP_BLOCK - 1))
    v_cmp = compress_rows(cv, w['cmp_v_w1'], w['cmp_v_b1'], w['cmp_v_w2'])
    return k_cmp, v_cmp

def cmp_branch(q, qpos, k_cmp, v_cmp):
    n_cmp = k_cmp.shape[1]
    k_end = jnp.arange(n_cmp, dtype=jnp.int32) * CMP_STRIDE + (CMP_BLOCK - 1)
    s = jnp.einsum('btgrd,bngd->btgrn', q, k_cmp).astype(jnp.float32) * ATTN_SCALE
    mask = (k_end[None, :] <= qpos[:, None])[None, :, None, None, :]
    p = masked_softmax(s, mask)
    o = jnp.einsum('btgrn,bngd->btgrd', p.astype(v_cmp.dtype), v_cmp)
    return o, jnp.sum(p, axis=3)

def cmp_to_slc_matrix(n_cmp, n_slc):
    units = np.arange(n_cmp)[:, None] + np.arange(CMP_PARTS)[None, :]
    sblk = (units * CMP_STRIDE) // SLC_BLOCK
    m = np.zeros((n_cmp, n_slc), np.float32)
    np.add.at(m, (np.repeat(np.arange(n_cmp), CMP_PARTS), sblk.reshape(-1)), 1.0)
    return m

def select_blocks(p_grp, qpos, n_slc):
    n_cmp = p_grp.shape[-1]
    m = jnp.asarray(cmp_to_slc_matrix(n_cmp, n_slc))
    score = jnp.einsum('btgn,nj->btgj', p_grp, m)
    j = jnp.arange(n_slc, dtype=jnp.int32)[None, :]
    cur = (qpos // SLC_BLOCK)[:, None]
    valid = j * SLC_BLOCK <= qpos[:, None]
    forced = (j == 0) | (j == cur) | (j == cur - 1)
    score = jnp.where(valid[None, :, None, :],
                      jnp.where(forced[None, :, None, :], FORCED_SCORE, score), NEG_INF)
    vals, idx = lax.top_k(score, min(N_SELECT, n_slc))
    return idx, vals > 0.5 * NEG_INF

def block_positions(idx):
    pos = idx[..., None] * SLC_BLOCK + jnp.arange(SLC_BLOCK, dtype=jnp.int32)
    return pos.reshape(*idx.shape[:-1], -1)

def gathered_attn(q, qpos, k_g, v_g, kpos, kok):
    s = jnp.einsum('btgrd,btgkd->btgrk', q, k_g).astype(jnp.float32) * ATTN_SCALE
    mask = (kok & (kpos <= qpos[None, :, None, None]))[:, :, :, None, :]
    p = masked_softmax(s, mask)
    return jnp.einsum('btgrk,btgkd->btgrd', p.astype(v_g.dtype), v_g)

def slc_branch_contiguous(q, qpos, idx, ok, sk, sv):
    bsz, t = sk.shape[:2]
    nb = t // SLC_QBLOCK
    bi = jnp.arange(bsz)[:, None, None, None]
    gi = jnp.arange(N_KV_HEADS)[None, None, :, None]

    def to_blocks(a):
        return a.reshape(bsz, nb, SLC_QBLOCK, *a.shape[2:]).swapaxes(0, 1)

    def one(args):
        qb, qpb, ib, okb = args
        kpos = block_positions(ib)
        kc = jnp.minimum(kpos, t - 1)
        return gathered_attn(qb, qpb, sk[bi, kc, gi], sv[bi, kc, gi], kpos,
                             jnp.repeat(okb, SLC_BLOCK, axis=-1))

    out = lax.map(one, (to_blocks(q), qpos.reshape(nb, SLC_QBLOCK), to_blocks(idx), to_blocks(ok)))
    return out.swapaxes(0, 1).reshape(bsz, t, N_KV_HEADS, GQA_REP, HEAD_DIM)

def gather_paged_rows(pool, page_table, new_rows, pos):
    bsz = pos.shape[0]
    past = page_table.shape[1] * PAGE_SIZE
    bi = jnp.arange(bsz)[:, None, None, None]
    gi = jnp.arange(N_KV_HEADS)[None, None, :, None]
    pc = jnp.clip(pos, 0, past - 1)
    page = page_table[bi, pc // PAGE_SIZE]
    from_pool = pool[page, pc % PAGE_SIZE, gi]
    pn = jnp.clip(pos - past, 0, new_rows.shape[1] - 1)
    from_new = new_rows[bi, pn, gi]
    return jnp.where((pos < past)[..., None], from_pool, from_new)

def slc_branch_paged(q, qpos, idx, ok, pool_k, pool_v, page_table, new_k, new_v):
    kpos = block_positions(idx)
    kg = gather_paged_rows(pool_k, page_table, new_k, kpos)
    vg = gather_paged_rows(pool_v, page_table, new_v, kpos)
    return gathered_attn(q, qpos, kg, vg, kpos, jnp.repeat(ok, SLC_BLOCK, axis=-1))

def window_attn(q, qpos, k, v, kpos):
    s = jnp.einsum('bnqgrd,bnkgd->bngrqk', q, k).astype(jnp.float32) * ATTN_SCALE
    dist = qpos[:, :, None] - kpos[:, None, :]
    mask = (kpos[:, None, :] >= 0) & (dist >= 0) & (dist < WINDOW)
    p = masked_softmax(s, mask[None, :, None, None])
    return jnp.einsum('bngrqk,bnkgd->bnqgrd', p.astype(v.dtype), v)

def win_branch_banded(q, qpos, wk, wv):
    bsz, t = q.shape[:2]
    nb = t // WIN_QBLOCK
    span = WINDOW + WIN_QBLOCK
    idx = np.arange(nb)[:, None] * WIN_QBLOCK + np.arange(span)[None, :]
    pad = ((0, 0), (WINDOW, 0), (0, 0), (0, 0))
    kb = jnp.pad(wk, pad)[:, idx]
    vb = jnp.pad(wv, pad)[:, idx]
    kpos = jnp.asarray(idx - WINDOW, dtype=jnp.int32)
    qb = q.reshape(bsz, nb, WIN_QBLOCK, N_KV_HEADS, GQA_REP, HEAD_DIM)
    o = window_attn(qb, qpos.reshape(nb, WIN_QBLOCK), kb, vb, kpos)
    return o.reshape(bsz, t, N_KV_HEADS, GQA_REP, HEAD_DIM)

def win_branch_buffer(q, qpos, kcat, vcat, kpos):
    o = window_attn(q[:, None], qpos[None], kcat[:, None], vcat[:, None], kpos[None])
    return o[:, 0]

def nsa_mixer(hn, pos, kv, w_q, w_gate, b_gate, w_o):
    bsz, t = hn.shape[:2]
    q = rope((hn @ w_q).reshape(bsz, t, N_HEADS, HEAD_DIM), pos)
    q = q.reshape(bsz, t, N_KV_HEADS, GQA_REP, HEAD_DIM)
    gates = jax.nn.sigmoid(hn @ w_gate + b_gate).reshape(bsz, t, 3, N_KV_HEADS, GQA_REP)[..., None]
    o_cmp, p_grp = cmp_branch(q, pos, kv['k_cmp'], kv['v_cmp'])
    idx, ok = select_blocks(p_grp, pos, kv['n_slc'])
    o_slc = kv['slc_fn'](q, pos, idx, ok)
    o_win = kv['win_fn'](q, pos)
    o = gates[:, :, 0] * o_cmp + gates[:, :, 1] * o_slc + gates[:, :, 2] * o_win
    return o.reshape(bsz, t, N_HEADS * HEAD_DIM) @ w_o

def trunk(x, p, pos, h0_re, h0_im, build_kv, w):
    ssm_re, ssm_im = [], []
    kv = None
    for i in range(DEPTH):
        hn = rmsnorm(x, w['norm_mix_g'][i])
        if i < N_A_LAYERS:
            o, hr, hi = s5_mixer(hn, h0_re[i], h0_im[i], w['ssm_a_re'][i], w['ssm_a_im'][i],
                                 w['ssm_log_dt'][i], w['ssm_b_re'][i], w['ssm_b_im'][i],
                                 w['ssm_c_re'][i], w['ssm_c_im'][i], w['ssm_d'][i],
                                 w['ssm_w_glu'][i], w['ssm_b_glu'][i])
            ssm_re.append(hr)
            ssm_im.append(hi)
        else:
            j = i - N_A_LAYERS
            o = nsa_mixer(hn, pos, kv, w['nsa_w_q'][j], w['nsa_w_gate'][j],
                          w['nsa_b_gate'][j], w['nsa_w_o'][j])
        x = x + o
        x = x + swiglu(rmsnorm(x, w['norm_ffn_g'][i]), w['ffn_w_gate'][i],
                       w['ffn_w_up'][i], w['ffn_w_down'][i])
        gate = jax.nn.sigmoid(rmsnorm(x, w['norm_ple_g'][i]) @ w['ple_w_gate'][i])
        x = x + gate * (p[i] @ w['ple_w_proj'][i])
        if i == N_A_LAYERS - 1:
            kv = build_kv(x)
    return rmsnorm(x, w['norm_final_g']), jnp.stack(ssm_re), jnp.stack(ssm_im), kv['new']

def setup_inputs(seed: int = 0) -> dict:
    key = jax.random.key(seed)
    ks = iter(jax.random.split(key, 64))
    f32 = jnp.float32

    def nrm(shape, scale):
        return scale * jax.random.normal(next(ks), shape, f32)

    def gain(shape):
        return 1.0 + nrm(shape, 0.02)

    n_pages = PAST_LEN // PAGE_SIZE
    n_used = DEC_BATCH * n_pages
    n_pool = n_used + (n_used + 3) // 4
    win_buf = min(WINDOW, PAST_LEN)
    kv_pool = (n_pool, PAGE_SIZE, N_KV_HEADS, HEAD_DIM)
    ssm_st = (N_A_LAYERS, DEC_BATCH, SSM_GROUPS, SSM_STATE)
    x_prompt = nrm((BATCH, SEQ, D_MODEL), 1.0)
    x_sample = nrm((DEC_BATCH, DEC_SEQ, D_MODEL), 1.0)
    state_ssm_re = nrm(ssm_st, 0.5)
    state_ssm_im = nrm(ssm_st, 0.5)
    cache_cmp_k = nrm(kv_pool, 1.0)
    cache_cmp_v = nrm(kv_pool, 1.0)
    cache_slc_k = nrm(kv_pool, 1.0)
    cache_slc_v = nrm(kv_pool, 1.0)
    state_win_k = nrm((DEC_BATCH, win_buf, N_KV_HEADS, HEAD_DIM), 1.0)
    state_win_v = nrm((DEC_BATCH, win_buf, N_KV_HEADS, HEAD_DIM), 1.0)
    page_table = jax.random.permutation(next(ks), n_pool)[:n_used].reshape(DEC_BATCH, n_pages).astype(jnp.int32)
    p_prompt = nrm((DEPTH, BATCH, SEQ, PLE_DIM), 1.0)
    p_sample = nrm((DEPTH, DEC_BATCH, DEC_SEQ, PLE_DIM), 1.0)
    a_shape = (N_A_LAYERS, SSM_GROUPS, SSM_STATE)
    n_idx = jnp.arange(SSM_STATE, dtype=f32)
    return {
        'x_prompt': x_prompt, 'x_sample': x_sample,
        'state_ssm_re': state_ssm_re, 'state_ssm_im': state_ssm_im,
        'cache_cmp_k': cache_cmp_k, 'cache_cmp_v': cache_cmp_v,
        'cache_slc_k': cache_slc_k, 'cache_slc_v': cache_slc_v,
        'state_win_k': state_win_k, 'state_win_v': state_win_v,
        'page_table': page_table, 'p_prompt': p_prompt, 'p_sample': p_sample,
        'norm_mix_g': gain((DEPTH, D_MODEL)), 'norm_ffn_g': gain((DEPTH, D_MODEL)),
        'norm_ple_g': gain((DEPTH, D_MODEL)), 'norm_kv_g': gain((D_MODEL,)),
        'norm_final_g': gain((D_MODEL,)),
        'ssm_a_re': -0.5 + nrm(a_shape, 0.01),
        'ssm_a_im': jnp.pi * n_idx + nrm(a_shape, 0.01),
        'ssm_log_dt': jax.random.uniform(next(ks), (N_A_LAYERS, SSM_GROUPS), f32,
                                         float(np.log(DT_MIN)), float(np.log(DT_MAX))),
        'ssm_b_re': nrm((N_A_LAYERS, SSM_GROUPS, SSM_STATE, SSM_GROUP), (2 * SSM_GROUP) ** -0.5),
        'ssm_b_im': nrm((N_A_LAYERS, SSM_GROUPS, SSM_STATE, SSM_GROUP), (2 * SSM_GROUP) ** -0.5),
        'ssm_c_re': nrm((N_A_LAYERS, SSM_GROUPS, SSM_GROUP, SSM_STATE), (2 * SSM_STATE) ** -0.5),
        'ssm_c_im': nrm((N_A_LAYERS, SSM_GROUPS, SSM_GROUP, SSM_STATE), (2 * SSM_STATE) ** -0.5),
        'ssm_d': 1.0 + nrm((N_A_LAYERS, D_MODEL), 0.1),
        'ssm_w_glu': nrm((N_A_LAYERS, D_MODEL, 2 * D_MODEL), D_MODEL ** -0.5),
        'ssm_b_glu': nrm((N_A_LAYERS, 2 * D_MODEL), 0.01),
        'kv_w': nrm((D_MODEL, 6 * N_KV_HEADS * HEAD_DIM), D_MODEL ** -0.5),
        'cmp_k_w1': nrm((CMP_BLOCK, HEAD_DIM, CMP_HIDDEN), (CMP_BLOCK * HEAD_DIM) ** -0.5),
        'cmp_k_b1': nrm((CMP_HIDDEN,), 0.01),
        'cmp_k_w2': nrm((CMP_HIDDEN, HEAD_DIM), CMP_HIDDEN ** -0.5),
        'cmp_v_w1': nrm((CMP_BLOCK, HEAD_DIM, CMP_HIDDEN), (CMP_BLOCK * HEAD_DIM) ** -0.5),
        'cmp_v_b1': nrm((CMP_HIDDEN,), 0.01),
        'cmp_v_w2': nrm((CMP_HIDDEN, HEAD_DIM), CMP_HIDDEN ** -0.5),
        'nsa_w_q': nrm((N_B_LAYERS, D_MODEL, N_HEADS * HEAD_DIM), D_MODEL ** -0.5),
        'nsa_w_gate': nrm((N_B_LAYERS, D_MODEL, 3 * N_HEADS), D_MODEL ** -0.5),
        'nsa_b_gate': nrm((N_B_LAYERS, 3 * N_HEADS), 0.01),
        'nsa_w_o': nrm((N_B_LAYERS, N_HEADS * HEAD_DIM, D_MODEL), (N_HEADS * HEAD_DIM) ** -0.5),
        'ffn_w_gate': nrm((DEPTH, D_MODEL, D_FF), D_MODEL ** -0.5),
        'ffn_w_up': nrm((DEPTH, D_MODEL, D_FF), D_MODEL ** -0.5),
        'ffn_w_down': nrm((DEPTH, D_FF, D_MODEL), D_FF ** -0.5),
        'ple_w_gate': nrm((DEPTH, D_MODEL, D_MODEL), D_MODEL ** -0.5),
        'ple_w_proj': nrm((DEPTH, PLE_DIM, D_MODEL), PLE_DIM ** -0.5),
    }

def reference(x_prompt, x_sample, state_ssm_re, state_ssm_im, cache_cmp_k, cache_cmp_v,
              cache_slc_k, cache_slc_v, state_win_k, state_win_v, page_table, p_prompt, p_sample,
              norm_mix_g, norm_ffn_g, norm_ple_g, norm_kv_g, norm_final_g,
              ssm_a_re, ssm_a_im, ssm_log_dt, ssm_b_re, ssm_b_im, ssm_c_re, ssm_c_im, ssm_d,
              ssm_w_glu, ssm_b_glu, kv_w, cmp_k_w1, cmp_k_b1, cmp_k_w2, cmp_v_w1, cmp_v_b1,
              cmp_v_w2, nsa_w_q, nsa_w_gate, nsa_b_gate, nsa_w_o, ffn_w_gate, ffn_w_up,
              ffn_w_down, ple_w_gate, ple_w_proj):
    w = dict(norm_mix_g=norm_mix_g, norm_ffn_g=norm_ffn_g, norm_ple_g=norm_ple_g,
             norm_final_g=norm_final_g, ssm_a_re=ssm_a_re, ssm_a_im=ssm_a_im,
             ssm_log_dt=ssm_log_dt, ssm_b_re=ssm_b_re, ssm_b_im=ssm_b_im, ssm_c_re=ssm_c_re,
             ssm_c_im=ssm_c_im, ssm_d=ssm_d, ssm_w_glu=ssm_w_glu, ssm_b_glu=ssm_b_glu,
             cmp_k_w1=cmp_k_w1, cmp_k_b1=cmp_k_b1, cmp_k_w2=cmp_k_w2, cmp_v_w1=cmp_v_w1,
             cmp_v_b1=cmp_v_b1, cmp_v_w2=cmp_v_w2, nsa_w_q=nsa_w_q, nsa_w_gate=nsa_w_gate,
             nsa_b_gate=nsa_b_gate, nsa_w_o=nsa_w_o, ffn_w_gate=ffn_w_gate, ffn_w_up=ffn_w_up,
             ffn_w_down=ffn_w_down, ple_w_gate=ple_w_gate, ple_w_proj=ple_w_proj)
    past = page_table.shape[1] * PAGE_SIZE
    pos_p = jnp.arange(x_prompt.shape[1], dtype=jnp.int32)
    pos_s = past + jnp.arange(x_sample.shape[1], dtype=jnp.int32)

    def build_kv_prompt(h):
        ck, cv, sk, sv, wk, wv = shared_kv_rows(h, pos_p, norm_kv_g, kv_w)
        k_cmp, v_cmp = compress_kv(ck, cv, w)
        t = h.shape[1]
        wb = min(WINDOW, t)
        return dict(k_cmp=k_cmp, v_cmp=v_cmp, n_slc=-(-t // SLC_BLOCK),
                    slc_fn=lambda q, qpos, idx, ok: slc_branch_contiguous(q, qpos, idx, ok, sk, sv),
                    win_fn=lambda q, qpos: win_branch_banded(q, qpos, wk, wv),
                    new=(ck, cv, sk, sv, wk[:, t - wb:], wv[:, t - wb:]))

    def build_kv_sample(h):
        ck, cv, sk, sv, wk, wv = shared_kv_rows(h, pos_s, norm_kv_g, kv_w)
        bd, tn = h.shape[:2]
        ck_all = jnp.concatenate(
            [cache_cmp_k[page_table].reshape(bd, past, N_KV_HEADS, HEAD_DIM), ck], axis=1)
        cv_all = jnp.concatenate(
            [cache_cmp_v[page_table].reshape(bd, past, N_KV_HEADS, HEAD_DIM), cv], axis=1)
        k_cmp, v_cmp = compress_kv(ck_all, cv_all, w)
        wb = state_win_k.shape[1]
        kcat = jnp.concatenate([state_win_k, wk], axis=1)
        vcat = jnp.concatenate([state_win_v, wv], axis=1)
        kpos_win = past - wb + jnp.arange(wb + tn, dtype=jnp.int32)
        return dict(k_cmp=k_cmp, v_cmp=v_cmp, n_slc=-(-(past + tn) // SLC_BLOCK),
                    slc_fn=lambda q, qpos, idx, ok: slc_branch_paged(
                        q, qpos, idx, ok, cache_slc_k, cache_slc_v, page_table, sk, sv),
                    win_fn=lambda q, qpos: win_branch_buffer(q, qpos, kcat, vcat, kpos_win),
                    new=(ck, cv, sk, sv, kcat[:, tn:], vcat[:, tn:]))

    h0 = jnp.zeros((N_A_LAYERS, x_prompt.shape[0], SSM_GROUPS, SSM_STATE), jnp.float32)
    y_prompt, sre_p, sim_p, new_p = trunk(x_prompt, p_prompt, pos_p, h0, h0, build_kv_prompt, w)
    y_sample, sre_s, sim_s, new_s = trunk(x_sample, p_sample, pos_s, state_ssm_re, state_ssm_im,
                                          build_kv_sample, w)
    ck_p, cv_p, sk_p, sv_p, wk_p, wv_p = new_p
    ck_s, cv_s, sk_s, sv_s, wk_s, wv_s = new_s
    return (y_prompt, y_sample, sre_p, sim_p, ck_p, cv_p, sk_p, sv_p, wk_p, wv_p,
            sre_s, sim_s, ck_s, cv_s, sk_s, sv_s, wk_s, wv_s)


_drawn_inputs = setup_inputs


def setup_inputs(seed=0):
    import zlib

    import numpy as np

    out = dict(_drawn_inputs(seed))
    spreads = {}
    factors = {'cache_cmp_k': 2.796,
     'cache_slc_k': 3.29,
     'cache_slc_v': 2.668,
     'norm_mix_g': 2.793,
     'norm_ffn_g': 3.171,
     'norm_ple_g': 60.087,
     'norm_kv_g': 8.183,
     'norm_final_g': 7.908,
     'ssm_a_re': 17.13,
     'ssm_b_glu': 8.0,
     'cmp_k_b1': 8.0,
     'cmp_v_b1': 64.0,
     'nsa_b_gate': 46.735}
    for name, (base, spread) in spreads.items():
        noise = np.random.default_rng([zlib.crc32(name.encode()), seed]).standard_normal(out[name].shape)
        drawn = base * np.exp(spread * noise) if base else spread * noise
        out[name] = jnp.asarray(drawn.astype(out[name].dtype))
    for name, factor in factors.items():
        out[name] = (out[name] * factor).astype(out[name].dtype)
    return out
```

```python
from contextlib import ExitStack, contextmanager

import concourse.bass as bass
import numpy as np
from concourse import mybir

F32, F32R, I32 = mybir.dt.float32, mybir.dt.float32r, mybir.dt.int32
ALU, ACT, AX = mybir.AluOpType, mybir.ActivationFunctionType, mybir.AxisListType
ds = bass.ds

P = 128
D, TP, TS, DEPTH = 2048, 256, 8, 2
T = TP + TS
KC = D // P
FF = 5632
PLE = 256
G, HREP, DH, NH = 4, 4, 128, 16
PAGE, PAGES, POOL, PAST = 128, 16, 160, 2048
GRP, ST = 16, 64
NQ = 64
STRIDE, TAPS = 16, 32
NCMP, NCMPP = PAST // STRIDE - 1, TP // STRIDE - 1
WIN = 512
EPS = 1e-6
SCALE = DH ** -0.5
NEG = -1e30
MAGIC = 12582912.0
INV2PI = float(np.float32(1 / (2 * np.pi)))
TWOPI_A = 6.28125
TWOPI_B = float(np.float32(2 * np.pi - 6.28125))
TWOPI_IN = 6.2831845
HALFPI = float(np.float32(np.pi / 2))
RING = 4
UK = 2
UN = 512
FC1, FC2 = 24, 20
SLOT = UK * UN


def shape_constants():
    f = np.float32
    half = DH // 2
    inv = (f(10000.0) ** (-np.arange(half, dtype=f) / f(half))).astype(f)

    def turn(pos):
        ang = pos.astype(f)[None, :] * inv[:, None]
        c, s = np.cos(ang).astype(f), np.sin(ang).astype(f)
        return np.concatenate([c, c]), np.concatenate([-s, s])

    tok = np.concatenate([np.arange(TP), np.full(TS, PAST)])
    out = {}
    out["ident"] = np.eye(P, dtype=f)
    out["ropet"] = np.stack(turn(tok), 1)
    cmp_pos = np.arange(NCMP) * STRIDE + TAPS - 1
    out["ropec"] = np.stack([np.repeat(a, 2, axis=1) for a in turn(cmp_pos)], 1)
    out["ropep"] = np.stack([np.tile(a[:, :NCMPP], (1, G)) for a in turn(cmp_pos)], 1)
    out["iota"] = np.tile(np.arange(16, dtype=f), (P, 1))
    par = (np.arange(P) // GRP) % 2
    cm = np.zeros((P, 2, 2, ST), f)
    cm[np.arange(P), 0, par], cm[np.arange(P), 1, par] = 1, -1
    out["cmask"] = cm.reshape(P, 2, P)
    t, k = np.arange(P)[:, None], np.arange(TP)[None, :]
    out["causal"] = np.stack([np.where(k <= t, 0, NEG), np.where(k <= t + P, 0, NEG)], 1).astype(f)
    vis = np.stack([(cmp_pos[:NCMPP][None, :] <= t + P * qt) for qt in range(2)], 1)
    out["cmpvis"] = np.concatenate([np.where(vis, 0, NEG), vis], 1).astype(f)
    row = np.arange(P) // HREP
    out["bd"] = (row[:, None] == np.arange(P // HREP)[None, :]).astype(f)
    out["same"] = (row[:, None] == row[None, :]).astype(f)
    m = np.zeros((P, 33), f)
    for n in range(NCMP):
        for j in range(2):
            m[n, (n + j) * STRIDE // 64] += 1
    out["toblk"] = m[:, 1:31].copy()
    lt = np.arange(30)
    out["earlier"] = np.broadcast_to((lt[None, None, :] < lt[None, :, None]), (P, 30, 30)).astype(f).copy()
    return out


@contextmanager
def straight(_start, _end):
    yield 0


class Sbuf:

    def __init__(self, nc, base):
        self.nc, self.at = nc, base

    def __call__(self, name, shape, dtype=F32, at=None):
        size = int(np.prod(shape[1:])) * 4
        size = -(-size // 32) * 32
        where = self.at if at is None else at
        if at is None:
            self.at += size
        assert where + size <= 229344, (name, where + size)
        return self.nc.alloc_sbuf_tensor_at(name, list(shape), dtype, offset=where)


def trunk_kernel(nc, io, out):
    const, sem_of = {}, {}
    stack = ExitStack()

    def sem(name):
        if name not in sem_of:
            sem_of[name] = stack.enter_context(nc.semaphore(name))
        return sem_of[name]

    sb = Sbuf(nc, 16512)
    X = sb("x_res", [P, KC, T])
    XH = sb("act_head", [P, KC, T], F32R)
    xl_at = sb.at
    XL = sb("act_rest", [P, KC, T], F32R)
    RAW = sb("w_raw", [P, RING, SLOT])
    WH = sb("w_head", [P, RING, SLOT], F32R)
    WL = sb("w_rest", [P, RING, SLOT], F32R)
    PH = sb("ple_head", [P, DEPTH, 2, T], F32R)
    PL = sb("ple_rest", [P, DEPTH, 2, T], F32R)
    HN = sb("normed", [P, 4, T])
    za_at = sb.at
    ZA = sb("gate_val", [P, 4, T])
    ZB = sb("prod_val", [P, 4, T])
    ssq_at = sb.at
    SSQ = sb("sumsq", [P, 4, T])
    RT = sb("rms", [P, T])
    RSTD = sb("rstd", [P, T])
    GV = sb("gains_t", [P, P])
    GW = sb("biases_t", [P, 50])
    ONES = sb("ones", [P, P])
    IDENT = sb("ident", [P, P])
    ROPET = sb("ropet", [P, 2, T])
    EPSB = sb("eps_bias", [P, 8])
    PT = sb("page_table", [1, P], I32)
    region = sb.at
    NMIX, NFFN, NPLE, NKV_GAIN, NFIN = (0, 1), (2, 3), (4, 5), 6, 7

    RH = sb("rows_head", [P, TAPS // 2, P, 2], F32R)
    rl_at = sb.at
    RL = sb("rows_rest", [P, TAPS // 2, P, 2], F32R)
    W2K = sb("w2k", [P, 2, P])
    W2V = sb("w2v", [P, P])
    GEL = sb("cmp_hidden", [P, 2 * NCMP])
    CMPO = sb("cmp_out", [P, 2 * P])
    RTMP = sb("rope_tmp", [P, 2 * NCMP])
    ROPC = sb("ropec", [P, 2, 2 * NCMP])
    ARGA = sb("turns_hi", [P, NQ + 1, 16])
    ARGB = sb("turns_lo", [P, NQ + 1, 16])
    PR = sb("ssm_par", [P, 16, NQ])
    W0 = sb("carry_in", [P, 2, NQ, TS])
    fin_at = sb.at
    FIN = sb("ssm_last", [P, 2, NQ, 1 + TS])
    BN = sb("b_raw", [P, 2, 4, GRP])
    CN_ = sb("c_raw", [P, 2, ST])
    BP = sb("b_prod", [P, 4, 4, GRP])
    BPAD = sb("b_pad", [P, 2, P])
    CPAD = sb("c_pad", [P, 2, P])
    BCT = sb("bc_t", [P, 4, P])
    CMASK = sb("cmask", [P, 2, P])
    IOTA = sb("iota16", [P, 16])
    T1 = sb("turns", [P, TP])
    KS = sb("round_s", [P, TP])
    KCR = sb("round_c", [P, TP])
    FS = sb("frac_s", [P, TP])
    FCO = sb("frac_c", [P, TP])
    SN = sb("sin_t", [P, 2, TP], at=ssq_at)
    CS = sb("cos_t", [P, 2, TP], at=ssq_at + 2 * TP * 4)
    XRI = sb("x_ri", [P, 2, 2, T])
    SRI = sb("s_ri", [P, 2, TP])
    M12 = sb("prod_pool", [P, 2, TP], at=za_at)
    N12 = sb("prod_dve", [P, 2, TP], at=za_at + 2 * TP * 4)
    H = sb("state", [P, 2, 2, T], at=za_at + 4 * TP * 4)
    OUTS = sb("states_out", [NQ, 2 * (1 + TS), P], at=region)
    XN = sb("x_nat", [P, 2, D], at=region)
    XS = sb("x_nat_s", [TS, D], at=rl_at)
    PN = sb("p_nat", [P, DEPTH, 2, PLE], at=rl_at + 8192)
    PS_ = sb("p_nat_s", [TS, DEPTH, PLE], at=rl_at + 12288)
    VEC = sb("vec_nat", [P, 2, P], at=rl_at + 14336)
    arg_at = rl_at + 16384 + 1536 + 1024 * 3 + 2048
    AN = sb("a_nat", [NQ, 3, P], at=xl_at)
    LD = sb("logdt_nat", [NQ, 2], at=xl_at + 1536)
    S0 = sb("s0_nat", [P, 2, 4, P], at=xl_at + 2048)
    H0 = sb("s0_t", [P, 2, NQ, TS], at=fin_at)
    PTMP = sb("par_tmp", [P, 4, NQ * 16], at=xl_at)
    PSF = sb("par_small", [P, 8, NQ], at=region)
    OTMP = sb("nat_out", [P, 2, P * 4], at=region)

    HH = sb("hid_head", [P, FC1, T], F32R, at=region)
    HL = sb("hid_rest", [P, FC1, T], F32R, at=region + FC1 * T * 4)

    att_at = region + 6 * 4 * T * 4 + KC * T * 4
    KVT = sb("kv_t", [P, 6, G, T], at=region)
    QT = sb("q_t", [P, NH, T], at=region + 6 * 4 * T * 4)
    sb.at = att_at
    VNAT = sb("v_rows", [P, 2, 2, G * DH])
    KCP = sb("k_cmp_p", [P, 64])
    VCP = sb("v_cmp_p", [16, G, DH])
    KS6 = sb("new_t", [P, 6, TS * G])
    SNAT = sb("new_rows", [TS * G, 6, DH])
    GT = sb("gates_t", [P, T])
    GN = sb("gates_rows", [P, 2, 48])
    GNS = sb("gates_rows_s", [TS, 48])
    GSM = sb("gates_s", [P, 8])
    QS = sb("q_s", [P, P])
    SWAP = sb("swap_halves", [P, P])
    BGATE = sb("b_gate", [P, 8])
    SM = sb("soft_small", [P, 64])
    scratch = sb.at
    WGR = sb("wg_raw", [P, KC, 48])
    WGH = sb("wg_head", [P, KC, P], F32R)
    WGL = sb("wg_rest", [P, KC, P], F32R)
    sb.at = scratch
    W1P = sb("taps_p", [P, TAPS, P])
    W2P = sb("w2_p", [P, 3, P])
    GEP = sb("hid_p", [P, 2, 64])
    RTP = sb("rope_p", [P, 64])
    sb.at = scratch
    SP2 = sb("scores_p", [P, 2, HREP, TP])
    PTP = sb("probs_t_p", [P, 2, 2, HREP * P])
    sb.at = scratch
    S2 = sb("scores_s", [P, PAST])
    SCT = sb("scores_st", [P, PAGES, P])
    KT = sb("k_t", [P, 2, G * P])
    NAT = sb("rows_out", [P, 2, G * DH], at=za_at)
    at = sb.at
    sb.at = 16512 + KC * T * 4
    CAUS = sb("causal", [P, 2, TP])
    CMPV = sb("cmpvis", [P, 4, NCMPP])
    ROPP = sb("ropep", [P, 2, G * NCMPP])
    BD = sb("own_head", [P, TS * G])
    SAME = sb("same_group", [P, P])
    TOB = sb("to_block", [P, 30])
    EARL = sb("earlier", [P, 30, 30])
    S2W = sb("scores_w", [P, WIN])
    STW = sb("scores_wt", [P, 4, P])
    PCS = sb("cmp_probs", [P, 3, P])
    assert sb.at <= xl_at
    W1Q = sb("taps_v", [P, TAPS, P], at=xl_at)
    KCS = sb("cmp_rows", [P, TS * 2, 2 * NCMP], at=xl_at)
    RTW = sb("new_scores", [P, 2, TS * G], at=region + 8192)
    RTK = sb("new_probs_t", [32, 2, P], at=region + 4 * T * 4 * 3)
    ZERO = sb("zeros", [P, P], at=region + 4 * T * 4 * 3 + 1024)
    BLK = sb("block_mask", [P, 32], at=region + 4 * T * 4 * 3 + 1536)
    YN = sb("y_rows", [P, 2, D], at=region)
    YS = sb("y_rows_s", [TS, D], at=region + 2 * D * 4)
    VCS = sb("cmp_rows_v", [P, TS * 2, 2 * P], at=xl_at)
    RK = sb("rank_pairs", [P, 2, 30, 30], at=region)
    sb.at = at

    PSUM = stack.enter_context(nc.psum_tensor("psum", [P, 8, 512], F32))
    kscr = nc.dram_tensor("cmp_k_scratch", [TS, 2, P, 2 * NCMP], F32).ap()
    vscr = nc.dram_tensor("cmp_v_scratch", [TS, 2, NCMP, 2 * P], F32).ap()

    class Phase:

        def __init__(self, name, steps, ka, kb, unrolled=False):
            self.name, self.steps, self.ka, self.kb, self.unrolled = name, steps, ka, kb, unrolled
            self.per = ka + kb

        def loop(self, eng):
            return eng.Fori(0, self.steps) if not self.unrolled else None

    phases = [Phase("glu", 4, 8, 8)]

    def layer_tail(l):
        return [Phase(f"gu1{l}", FC1 // 4, 8, 8), Phase(f"dn1{l}", 2, FC1 // 2, FC1 // 2),
                Phase(f"gu2{l}", FC2 // 4, 8, 8), Phase(f"dn2{l}", 2, FC2 // 2, FC2 // 2),
                Phase(f"ple{l}", 4, 8, 1, True)]

    phases += layer_tail(0) + [Phase("kv", 3, 8, 8), Phase("q", 2, 8, 8), Phase("o", 2, 8, 8)] + layer_tail(1)
    TAP_UNITS = 2 * RING
    s, ngr = TAP_UNITS, 0
    for ph in phases:
        ph.base, ph.groups = s, ngr
        s += ph.per * ph.steps
        ngr += ph.steps
    NUNITS = s
    by_name = {ph.name: ph for ph in phases}
    nsq = 4
    for ph in phases:
        ph.sq = nsq
        if ph.name in ("glu", "o") or ph.name[:3] in ("dn2", "ple"):
            nsq += 4

    def steps_of(ph, eng, body):
        if ph.unrolled:
            for i in range(ph.steps):
                body(i)
        else:
            with eng.Fori(0, ph.steps) as i:
                body(i)

    class Unit:

        def __init__(self, base, per=0, i=0, c=0):
            if isinstance(i, int):
                n = base + per * i + c
                self.n, self.slot, self.turn = n, n % RING, n // RING + 1
            else:
                self.n, self.slot = per * i + (base + c), (base + c) % RING
                self.turn = (per // RING) * i + ((base + c) // RING + 1)
            self.known = isinstance(i, int)

    raw_ready = [sem(f"raw_ready{k}") for k in range(RING)]
    units_used, head_done, rest_done = sem("units_used"), sem("head_done"), sem("rest_done")
    free_a, free_b = sem("free_a"), sem("free_b")
    x_done, sq_done, ssq_done = sem("x_done"), sem("sq_done"), sem("ssq_done")
    norm_sum, rt_done, rstd_done = sem("norm_sum"), sem("rt_done"), sem("rstd_done")
    hn_done, xh_done, xl_done = sem("hn_done"), sem("xh_done"), sem("xl_done")
    glu_sig, prod_done, hh_done, hl_done = (sem(n) for n in ("glu_sig", "prod_done", "hh_done", "hl_done"))
    tp_done, tp_evac = sem("tp_done"), sem("tp_evac")
    ld = {n: sem("ld_" + n) for n in ("const", "vec", "x", "ssm", "p", "late")}
    pt_used, ph_done, par_act, par_dve = sem("pt_used"), sem("ph_done"), sem("par_act"), sem("par_dve")
    page_ready = [sem(f"page_ready{k}") for k in range(RING)]
    page_used, bc_loaded, bc_ready, bct_tp, bct_done = (sem(n) for n in ("page_used", "bc_loaded", "bc_ready", "bct_tp", "bct_done"))
    cmp_tp, cmp_head, cmp_rest, cmp_acc, cmp_gelu, cmp_mm2, cmp_out, cmp_kept, rope_part = (
        sem(n) for n in ("cmp_tp", "cmp_head", "cmp_rest", "cmp_acc", "cmp_gelu", "cmp_mm2", "cmp_out", "cmp_kept", "rope_part"))
    pool_t1, dve_ks, dve_kc, dve_fc, pool_fs, act_tab = (sem(n) for n in ("pool_t1", "dve_ks", "dve_kc", "dve_fc", "pool_fs", "act_tab"))
    hn_chunk, pe_bu, act_x, pool_rot, dve_n, dve_rot, dve_scan, pool_der, dve_n2, dve_h, pe_y, pool_fin = (
        sem(n) for n in ("hn_chunk", "pe_bu", "act_x", "pool_rot", "dve_n", "dve_rot", "dve_scan", "pool_der", "dve_n2", "dve_h", "pe_y", "pool_fin"))
    y_sum, y_gelu, b_prod, arg_ready, stored, out_nat = (sem(n) for n in ("y_sum", "y_gelu", "b_prod", "arg_ready", "stored", "out_nat"))

    def load_unit(sp, u, src, first=False):
        if not (u.known and u.n < RING) and not first:
            sp.wait_ge(rest_done, u.n - (RING - 1))
        sp.dma_start(RAW[:, u.slot, :].rearrange("p (k n) -> p k n", k=src.shape[1]), src).then_inc(raw_ready[u.slot], 16)

    def split_head(act, u):
        act.wait_ge(raw_ready[u.slot], 16 * u.turn)
        if not (u.known and u.n < TAP_UNITS + RING):
            act.wait_ge(units_used, u.n - (RING - 1) - TAP_UNITS)
        nc.scalar.activation(WH[:, u.slot, :], RAW[:, u.slot, :], ACT.Copy).then_inc(head_done, 1)

    def split_rest(dve, u):
        dve.wait_ge(head_done, u.n + 1)
        nc.vector.tensor_tensor(WL[:, u.slot, :], RAW[:, u.slot, :], WH[:, u.slot, :].bitcast(F32),
                                ALU.subtract).then_inc(rest_done, 1)

    def group_matmuls(pe, ph, i, c0, kunits, bank, heads, rests, ready):
        for ku in range(kunits):
            u = Unit(ph.base, ph.per, i, c0 + ku)
            pe.wait_ge(rest_done, u.n + 1)
            for kk in range(UK):
                k = UK * ku + kk
                if ready is not None:
                    ready(k)
                for n in range(4):
                    w = slice(kk * UN + n * P, kk * UN + (n + 1) * P)
                    o = PSUM[:, bank + n, 0:T]
                    nc.tensor.matmul(o, WH[:, u.slot, w], heads[:, k, :], start=k == 0, stop=False)
                    nc.tensor.matmul(o, WH[:, u.slot, w], rests[:, k, :], start=False, stop=False)
                    last = nc.tensor.matmul(o, WL[:, u.slot, w], heads[:, k, :], start=False,
                                            stop=k == UK * kunits - 1)
            last.then_inc(units_used, 1)

    NORMS = {"mix0": 0, "ffn0": 1, "ple0": 2, "kv": 3, "ffn1": 4, "ple1": 5, "fin": 6}
    HNS = {"ffn0": 0, "ple0": 1, "kv": 2, "mix1": 3, "ffn1": 4, "ple1": 5, "fin": 6}
    XLS = {"ffn0": 16, "ple0": 32, "kv": 48, "mix1": 64, "att": 80, "ffn1": 96, "ple1": 112}

    def rms_pe(pe, name):
        k = NORMS[name]
        pe.wait_ge(ssq_done, 4 * (k + 1))
        for j in range(4):
            last = nc.tensor.matmul(PSUM[:, 4, 0:T], ONES[:, :], SSQ[:, j, :], start=j == 0, stop=j == 3)
        last.then_inc(norm_sum, 1)

    def rms_act(act, name):
        k = NORMS[name]
        act.wait_ge(norm_sum, k + 1)
        nc.scalar.activation(RT[:, :], PSUM[:, 4, 0:T], ACT.Sqrt, scale=1.0 / D, bias=EPSB[:, 0:1]).then_inc(rt_done, 1)

    def rms_dve(dve, name):
        k = NORMS[name]
        dve.wait_ge(rt_done, k + 1)
        nc.vector.reciprocal(RSTD[:, :], RT[:, :]).then_inc(rstd_done, 1)
        dve.wait_ge(rstd_done, k + 1)

    def norm_act(act, name, used=None):
        n = 16 * HNS[name]
        if used is not None:
            act.wait_ge(units_used, used)
        for c in range(KC):
            act.wait_ge(hn_done, n + c + 1)
            nc.scalar.activation(XH[:, c, :], HN[:, c % 4, :], ACT.Copy).then_inc(xh_done, 1)

    def norm_dve(dve, name, gain):
        m = XLS.get(name)

        def rest(c):
            dve.wait_ge(xh_done, m + c + 1)
            nc.vector.tensor_tensor(XL[:, c, :], HN[:, c % 4, :], XH[:, c, :].bitcast(F32),
                                    ALU.subtract).then_inc(xl_done, 1)

        for c in range(KC):
            if c >= 4:
                dve.wait_ge(xl_done, m + c - 3)
            nc.vector.scalar_tensor_tensor(out=HN[:, c % 4, :], in0=X[:, c, :], scalar=GV[:, 16 * gain + c:16 * gain + c + 1],
                                           in1=RSTD[:, :], op0=ALU.mult, op1=ALU.mult).then_inc(hn_done, 1)
            if c >= 1:
                rest(c - 1)
        rest(KC - 1)

    def normed_ready(pe, name):
        return lambda k: pe.wait_ge(xl_done, XLS[name] + k + 1)

    def square_act(act, k, chunks, done, count):
        act.wait_ge(done, count)
        act.wait_ge(ssq_done, k)
        nc.scalar.activation(HN[:, :, :], X[:, chunks, :], ACT.Square).then_inc(sq_done, 1)

    def square_dve(dve, k, dst):
        dve.wait_ge(sq_done, k + 1)
        nc.vector.tensor_reduce(dst if len(dst.shape) == 2 else dst.rearrange("p o t -> p (o t)"), HN[:, :, :].rearrange("p c t -> p t c"), AX.X, ALU.add).then_inc(ssq_done, 1)

    def weight(name, i, half):
        def cols(w, at, rows=None):
            w = w if rows is None else w[rows]
            return w.rearrange("(k p) n -> p k n", p=P)[:, :, ds(at, UN)]
        l = int(name[-1]) if name[-1] in "01" else 0
        if name == "glu":
            return cols(io["ssm_w_glu"][0], i * UN + half * D)
        if name[:2] == "gu":
            at = (FC1 * P if name[2] == "2" else 0)
            return cols(io["ffn_w_up" if half else "ffn_w_gate"][l], i * UN + at)
        if name[:2] == "dn":
            rows = slice(0, FC1 * P) if name[2] == "1" else slice(FC1 * P, FF)
            return cols(io["ffn_w_down"][l], i * (2 * UN) + half * UN, rows)
        if name[:3] == "ple":
            return cols(io["ple_w_proj" if half else "ple_w_gate"][l], i * UN)
        w = {"kv": io["kv_w"], "q": io["nsa_w_q"][0], "o": io["nsa_w_o"][0]}[name]
        return cols(w, i * (2 * UN) + half * UN)

    def phase_sp(sp, name, skip=0, only=None):
        ph = by_name[name]
        if only is not None:
            for c in range(only):
                load_unit(sp, Unit(ph.base, ph.per, 0, c), weight(name, 0, 0)[:, UK * c:UK * (c + 1), :])
            return

        def body(i):
            for half, kn, c0 in ((0, ph.ka, 0), (1, ph.kb, ph.ka)):
                src = weight(name, i, half)
                for ku in range(kn):
                    if isinstance(i, int) and i == 0 and c0 + ku < skip:
                        continue
                    load_unit(sp, Unit(ph.base, ph.per, i, c0 + ku), src[:, UK * ku:UK * (ku + 1), :])

        if skip:
            body(0)
            with sp.Fori(1, ph.steps) as i:
                body(i)
        else:
            steps_of(ph, sp, body)

    def phase_pe(pe, name, heads, rests, ready, heads_b=None, rests_b=None):
        ph = by_name[name]

        def body(i, wait=True):
            if wait:
                pe.wait_ge(free_a, i + ph.groups)
            group_matmuls(pe, ph, i, 0, ph.ka, 0, heads, rests, ready)
            if wait:
                pe.wait_ge(free_b, i + ph.groups)
            group_matmuls(pe, ph, i, ph.ka, ph.kb, 4, heads_b or heads, rests_b or rests, None)

        if ph.groups == 0:
            body(0, False)
            with pe.Fori(1, ph.steps) as i:
                body(i)
        else:
            steps_of(ph, pe, body)

    def after_units(eng, name, split, evac_a, evac_b):
        ph = by_name[name]

        def body(i):
            for c in range(ph.per):
                u = Unit(ph.base, ph.per, i, c)
                if c == ph.ka - 1:
                    eng.wait_ge(units_used, u.n + 1 - TAP_UNITS)
                    evac_a(i)
                if c == ph.per - 1:
                    eng.wait_ge(units_used, u.n + 1 - TAP_UNITS)
                    evac_b(i)
                if not (u.known and u.n + RING >= NUNITS):
                    split(eng, Unit(ph.base + RING, ph.per, i, c))

        steps_of(ph, eng, body)

    nothing = lambda i: None
    A4, B4 = PSUM[:, 0:4, 0:T], PSUM[:, 4:8, 0:T]

    def four(t, g):
        return t[:, ds(4 * g, 4), :] if not isinstance(g, int) else t[:, 4 * g:4 * g + 4, :]

    NKV = TS
    caches = [io["cache_cmp_k"], io["cache_cmp_v"]]
    cache_views = [c.rearrange("n r g d -> n r (g d)") for c in caches]
    w1 = [io["cmp_k_w1"], io["cmp_v_w1"]]
    L_CONST = 16 * 2
    L_VEC = 16 * 9
    L_SSM = 16 * 5
    L_LATE = 16 * 8

    def start_sp(sp):
        def rows(x, n):
            return x.rearrange("(c p) -> c p", p=P) if n == 1 else x.rearrange("l (c p) -> (l c) p", p=P)
        sp.dma_start(IDENT[:, :], io["k_ident"]).then_inc(ld["const"], 16)
        sp.dma_start(ROPET[:, :, :], io["k_ropet"]).then_inc(ld["const"], 16)
        for name, at in (("norm_mix_g", 0), ("norm_ffn_g", 32), ("norm_ple_g", 64)):
            sp.dma_start(VEC[at:at + 32, 0, :], rows(io[name], 2)).then_inc(ld["vec"], 16)
        for name, at in (("norm_kv_g", 96), ("norm_final_g", 112)):
            sp.dma_start(VEC[at:at + 16, 0, :], rows(io[name], 1)).then_inc(ld["vec"], 16)
        for name, at, n in (("ssm_d", 0, 16), ("ssm_b_glu", 16, 32)):
            sp.dma_start(VEC[at:at + n, 1, :], rows(io[name], 2)).then_inc(ld["vec"], 16)
        for name, at in (("cmp_k_b1", 48), ("cmp_v_b1", 49)):
            sp.dma_start(VEC[at:at + 1, 1, :], io[name].rearrange("(a p) -> a p", a=1)).then_inc(ld["vec"], 16)
        sp.dma_start(XN[:, :, :], io["x_prompt"][0].rearrange("(q p) d -> p q d", p=P)).then_inc(ld["x"], 16)
        sp.dma_start(XS[:, :], io["x_sample"].rearrange("b o d -> (b o) d")).then_inc(ld["x"], 16)
        for k, name in enumerate(("ssm_a_re", "ssm_a_im")):
            sp.dma_start(AN[:, k, :], io[name][0].rearrange("(q e) p -> q (e p)", e=2)).then_inc(ld["ssm"], 16)
        sp.dma_start(LD[:, :], io["ssm_log_dt"][0].rearrange("(q e) -> q e", e=2)).then_inc(ld["ssm"], 16)
        for k, name in enumerate(("state_ssm_re", "state_ssm_im")):
            sp.dma_start(S0[:, k, :, :], io[name][0].rearrange("(k b) (q e) p -> (b q) k (e p)", b=2, e=2)).then_inc(ld["ssm"], 16)
        for u in range(RING):
            load_taps(sp, 0, u)
        sp.dma_start(PN[:, :, :, :], io["p_prompt"].rearrange("l o (q p) d -> p l (o q) d", p=P)).then_inc(ld["p"], 16)
        sp.dma_start(PS_[:, :, :], io["p_sample"].rearrange("l b o d -> b l (o d)")).then_inc(ld["p"], 16)
        sp.dma_start(PT[:, :], io["page_table"].rearrange("(o b) n -> o (b n)", o=1)).then_inc(ld["late"], 16)
        sp.dma_start(W2K[:, 0, :], io["cmp_k_w2"]).then_inc(ld["late"], 16)
        sp.dma_start(W2K[:, 1, 0:64], io["cmp_k_w2"][:, 64:128]).then_inc(ld["late"], 16)
        sp.dma_start(W2K[:, 1, 64:128], io["cmp_k_w2"][:, 0:64]).then_inc(ld["late"], 16)
        sp.dma_start(W2V[:, :], io["cmp_v_w2"]).then_inc(ld["late"], 16)
        sp.dma_start(ROPC[:, :, :], io["k_ropec"]).then_inc(ld["late"], 16)
        sp.dma_start(CMASK[:, :, :], io["k_cmask"]).then_inc(ld["late"], 16)
        sp.dma_start(IOTA[:, :], io["k_iota"]).then_inc(ld["late"], 16)

    def load_taps(sp, kv, u):
        load_unit(sp, Unit(RING * kv + u), w1[kv][8 * u:8 * u + 8].rearrange("t d h -> d t h"))

    def body_sp(sp, kv, i, first):
        c = i + NKV * kv
        if not (first and kv == 0):
            sp.wait_ge(bc_ready, c)
        for k, name in enumerate(("ssm_b_re", "ssm_b_im")):
            b = io[name][0].rearrange("(c j e) p h -> c (e p) j h", j=4, e=2)
            sp.dma_start(BN[:, k, :, :], b[ds(c, 1)].rearrange("o s j h -> (o s) j h")).then_inc(bc_loaded, 16)
        for k, name in enumerate(("ssm_c_re", "ssm_c_im")):
            cc = io[name][0].rearrange("(c g) h p -> c (g h) p", g=8)
            sp.dma_start(CN_[:, k, :], cc[ds(c, 1)].rearrange("o s p -> (o s) p")).then_inc(bc_loaded, 16)
        for gp in range(2):
            for u in range(4):
                pages = [sp.value_load(PT[0:1, ds(i * PAGES + (4 * u + k), 1)], min_val=0, max_val=POOL - 1) for k in range(4)]
                if first and gp == 0:
                    sp.wait_ge(rest_done, RING * kv + u + 1)
                else:
                    sp.wait_ge(cmp_tp, 8 * (2 * c + gp - 1) + 2 * u + 2)
                for k, page in enumerate(pages):
                    src = cache_views[kv][ds(page, 1), :, 2 * gp * DH:(2 * gp + 2) * DH]
                    sp.dma_start(RAW[:, u, k * 256:(k + 1) * 256], src.rearrange("o r n -> (o r) n")).then_inc(page_ready[u], 16)

    ZPAR = PSUM
    P0_JOBS = 3 + KC + 2 + 4

    def bank_of(j):
        return PSUM[:, j % 8, :]

    def start_pe(pe):
        j = 0

        def job(ins, wait=None):
            nonlocal j
            if wait:
                pe.wait_ge(*wait)
            if j >= 8:
                pe.wait_ge(tp_evac, j - 7)
            for src, at in ins:
                n, m = src.shape[0], int(np.prod(src.shape[1:]))
                last = nc.tensor.transpose(PSUM[0:m, j % 8, at:at + n], src, IDENT[0:n, 0:n])
            last.then_inc(tp_done, 1)
            j += 1

        pe.wait_ge(ld["const"], L_CONST)
        job([(VEC[:, 0, :], 0)], (ld["vec"], L_VEC))
        job([(VEC[0:50, 1, :], 0)])
        pe.wait_ge(ld["ssm"], L_SSM)
        job([(AN[:, k, :], k * NQ) for k in range(3)], (par_dve, 1))
        pe.wait_ge(ld["x"], 32)
        for c in range(KC):
            sl = slice(c * P, (c + 1) * P)
            job([(XN[:, 0, sl], 0), (XN[:, 1, sl], P), (XS[:, sl], 2 * P)])
        for k in range(2):
            job([(S0[:, k, m, :], m * P) for m in range(4)])
        for l in range(DEPTH):
            for c in range(2):
                sl = slice(c * P, (c + 1) * P)
                job([(PN[:, l, 0, sl], 0), (PN[:, l, 1, sl], P), (PS_[:, l, sl], 2 * P)],
                    (ld["p"], 32) if l == c == 0 else None)

    def start_dve(dve):
        nc.vector.memset(ONES[:, :], 1.0)
        nc.vector.memset(EPSB[:, 0:1], EPS)
        nc.vector.memset(EPSB[:, 1:2], HALFPI)
        nc.vector.memset(ARGA[:, NQ:NQ + 1, :], 0.0)
        nc.vector.memset(ARGB[:, NQ:NQ + 1, :], 0.0)
        nc.vector.memset(BPAD[:, :, :], 0.0)
        dve.wait_ge(ld["ssm"], L_SSM)
        nc.vector.tensor_copy(AN[:, 2, :].rearrange("q (e p) -> q e p", e=2),
                              LD[:, :].unsqueeze(2).to_broadcast([NQ, 2, ST])).then_inc(par_dve, 1)
        j = 0

        def evac(dst, src_cols=None, rows=P):
            nonlocal j
            dve.wait_ge(tp_done, j + 1)
            src = bank_of(j)[0:rows]
            src = src_cols(src)
            nc.vector.tensor_copy(dst, src).then_inc(tp_evac, 1)
            j += 1

        evac(GV[:, :], lambda b: b[:, 0:P])
        evac(GW[:, :], lambda b: b[:, 0:50])
        evac(PR[:, 0:3, :], lambda b: b[:, 0:3 * NQ].rearrange("p (k q) -> p k q", k=3))
        for c in range(KC):
            evac(X[:, c, :], lambda b: b[:, 0:T])
        for u in range(RING):
            split_rest(dve, Unit(u))
        for k in range(2):
            evac(H0[:, k, :, :].rearrange("p q b -> p b q"), lambda b: b[:, :].rearrange("p (b q) -> p b q", q=NQ))
        for l in range(DEPTH):
            for c in range(2):
                evac(ZA[:, 2 * l + c, :], lambda b: b[:, 0:T])
        dve.wait_ge(ph_done, 1)
        dve.wait_ge(tp_evac, P0_JOBS)
        nc.vector.tensor_tensor(PL[:, :, :, :].rearrange("p l c t -> p (l c) t"), ZA[:, :, :],
                                PH[:, :, :, :].rearrange("p l c t -> p (l c) t").bitcast(F32), ALU.subtract).then_inc(ph_done, 1)
        for g in range(4):
            square_dve(dve, g, SSQ[:, g, :])
        rms_dve(dve, "mix0")
        ssm_parameters_dve(dve)

    def start_act(act):
        for u in range(RING):
            split_head(act, Unit(u))
        act.wait_ge(tp_evac, P0_JOBS)
        nc.scalar.activation(PH[:, :, :, :].rearrange("p l c t -> p (l c) t"), ZA[:, :, :], ACT.Copy).then_inc(ph_done, 1)
        for g in range(4):
            if g:
                act.wait_ge(ssq_done, g)
            nc.scalar.activation(HN[:, :, :], X[:, 4 * g:4 * g + 4, :], ACT.Square).then_inc(sq_done, 1)
        rms_act(act, "mix0")
        act.wait_ge(tp_evac, 3)
        nc.scalar.activation(PR[:, 3, :], PR[:, 2, :], ACT.Exp).then_inc(par_act, 1)
        act.wait_ge(par_dve, 2)
        nc.scalar.activation(PR[:, 4, :], PSF[:, 0, :], ACT.Exp).then_inc(par_act, 1)
        act.wait_ge(par_dve, 3)
        nc.scalar.activation(PR[:, 5, :], PSF[:, 4, :], ACT.Sin, scale=TWOPI_IN).then_inc(par_act, 1)
        nc.scalar.activation(PR[:, 6, :], PSF[:, 5, :], ACT.Sin, scale=TWOPI_IN).then_inc(par_act, 1)

    def ssm_parameters_dve(dve):
        V = nc.vector
        n = [0]

        def link(ins):
            n[0] += 1
            ins.then_inc(arg_ready, 1)
            dve.wait_ge(arg_ready, n[0])

        def tt(o, a, b, op):
            link(V.tensor_tensor(o, a, b, op))

        def rounded(o, a, tmp):
            link(V.tensor_scalar(tmp, a, MAGIC, -MAGIC, ALU.add, ALU.add))
            tt(o, a, tmp, ALU.subtract)

        s = lambda k: PSF[:, k, :]
        r = lambda k: PR[:, k, :]
        dve.wait_ge(par_act, 1)
        V.tensor_tensor(s(0), r(3), r(0), ALU.mult).then_inc(par_dve, 1)
        tt(s(1), r(3), r(1), ALU.mult)
        link(V.tensor_scalar(s(2), s(1), INV2PI, MAGIC, ALU.mult, ALU.add))
        link(V.tensor_scalar(s(2), s(2), -MAGIC, None, ALU.add))
        link(V.scalar_tensor_tensor(out=s(3), in0=s(2), scalar=-TWOPI_A, in1=s(1), op0=ALU.mult, op1=ALU.add))
        link(V.scalar_tensor_tensor(out=s(3), in0=s(2), scalar=-TWOPI_B, in1=s(3), op0=ALU.mult, op1=ALU.add))
        link(V.tensor_scalar(s(4), s(3), INV2PI, None, ALU.mult))
        link(V.tensor_scalar(s(4), s(4), 0.5, -0.5, ALU.min, ALU.max))
        link(V.tensor_scalar(s(6), s(4), 0.25, None, ALU.add))
        link(V.tensor_scalar(s(7), s(6), MAGIC, -MAGIC, ALU.add, ALU.add))
        V.tensor_tensor(s(5), s(6), s(7), ALU.subtract).then_inc(par_dve, 1)
        it = IOTA[:, :].unsqueeze(1).to_broadcast([P, NQ, 16])
        dve.wait_ge(ld["late"], L_LATE)
        t0 = PTMP[:, 0, :].rearrange("p (q b) -> p q b", b=16)
        t1 = PTMP[:, 1, :].rearrange("p (q b) -> p q b", b=16)
        tt(t0, s(4).unsqueeze(2).to_broadcast([P, NQ, 16]), it, ALU.mult)
        rounded(ARGB[:, 0:NQ, :], t0, t1)
        link(V.tensor_scalar(s(6), s(4), 16.0, None, ALU.mult))
        rounded(s(1), s(6), s(7))
        tt(t0, s(1).unsqueeze(2).to_broadcast([P, NQ, 16]), it, ALU.mult)
        rounded(ARGA[:, 0:NQ, :], t0, t1)
        dve.wait_ge(par_act, 4)
        tt(r(7), r(4), r(6), ALU.mult)
        tt(r(8), r(4), r(5), ALU.mult)
        link(V.tensor_scalar(s(1), r(7), -1.0, None, ALU.add))
        tt(s(2), r(0), r(0), ALU.mult)
        tt(s(3), r(1), r(1), ALU.mult)
        tt(s(2), s(2), s(3), ALU.add)
        link(V.reciprocal(s(2), s(2)))
        tt(s(3), s(1), r(0), ALU.mult)
        tt(s(6), r(8), r(1), ALU.mult)
        tt(s(3), s(3), s(6), ALU.add)
        tt(r(9), s(3), s(2), ALU.mult)
        tt(s(3), r(8), r(0), ALU.mult)
        tt(s(6), s(1), r(1), ALU.mult)
        tt(s(3), s(3), s(6), ALU.subtract)
        tt(r(10), s(3), s(2), ALU.mult)
        re, im = (r(k).unsqueeze(2).to_broadcast([P, NQ, TS]) for k in (7, 8))
        t2 = PTMP[:, 0, 0:NQ * TS].rearrange("p (q b) -> p q b", b=TS)
        t3 = PTMP[:, 1, 0:NQ * TS].rearrange("p (q b) -> p q b", b=TS)
        tt(t2, re, H0[:, 0, :, :], ALU.mult)
        tt(t3, im, H0[:, 1, :, :], ALU.mult)
        tt(W0[:, 0, :, :], t2, t3, ALU.subtract)
        tt(t2, re, H0[:, 1, :, :], ALU.mult)
        tt(t3, im, H0[:, 0, :, :], ALU.mult)
        tt(W0[:, 1, :, :], t2, t3, ALU.add)
        assert n[0] == N_PAR, n[0]
    N_PAR = 39

    def tile(c, j):
        return 4 * c + j

    def page_rows(bank):
        return PSUM[:, bank, :].rearrange("p (g n s) -> p g n s", g=2, s=16)

    def rows_of(tensor, m):
        return tensor[:, :, 16 * m:16 * m + 16, :].rearrange("p s n g -> p g n s")

    def body_pe(pe, kv, i, first, last=False):
        c = i + NKV * kv
        item = lambda gp: 2 * c + gp

        def bct():
            pe.wait_ge(bc_ready, c + 1)
            if not (first and kv == 0):
                pe.wait_ge(bct_done, c)
            for k in range(2):
                nc.tensor.transpose(PSUM[:, 7, k * P:(k + 1) * P], BPAD[:, k, :], IDENT[:, :])
            for k in range(2):
                last_ = nc.tensor.transpose(PSUM[:, 7, (2 + k) * P:(3 + k) * P], CPAD[:, k, :], IDENT[:, :])
            last_.then_inc(bct_tp, 1)

        def bu(j):
            if j == 0:
                pe.wait_ge(bct_done, c + 1)
                pe.wait_ge(hn_chunk, c + 1)
            if not (first and kv == 0 and j == 0):
                pe.wait_ge(act_x, tile(c, j))
            r = slice(32 * j, 32 * j + 32)
            for k in range(2):
                last_ = nc.tensor.matmul(PSUM[:, 4 + k, 0:T], BCT[r, k, :], HN[r, 0, :], start=True, stop=True)
            last_.then_inc(pe_bu, 1)

        def y(j):
            pe.wait_ge(dve_h, tile(c, j) + 1)
            pe.wait_ge(pool_rot, tile(c, j) + 1)
            if j == 0 and not (first and kv == 0):
                pe.wait_ge(y_sum, c)
            r = slice(32 * j, 32 * j + 32)
            nc.tensor.matmul(PSUM[r, 6, 0:T], BCT[:, 2, r], H[:, j % 2, 0, :], start=True, stop=False)
            nc.tensor.matmul(PSUM[r, 6, 0:T], BCT[:, 3, r], H[:, j % 2, 1, :], start=False, stop=True).then_inc(pe_y, 1)

        def tp(gp, lo, hi):
            for m in range(lo, hi):
                u = m // 2
                pe.wait_ge(page_ready[u], 64 * item(gp) + 64)
                n = 8 * item(gp) + m
                if not (first and kv == 0 and gp == 0 and m < 2):
                    pe.wait_ge(cmp_rest, n - 1)
                for g in range(2):
                    for pg in range(2):
                        src = RAW[:, u, (2 * (m % 2) + pg) * 256 + g * DH:(2 * (m % 2) + pg) * 256 + (g + 1) * DH]
                        last_ = nc.tensor.transpose(PSUM[:, m % 2, (2 * g + pg) * P:(2 * g + pg + 1) * P], src, IDENT[:, :])
                last_.then_inc(cmp_tp, 1)

        def mm(gp, part):
            if part == 0:
                pe.wait_ge(cmp_rest, 8 * item(gp) + 8)
                if not (first and kv == 0 and gp == 0):
                    pe.wait_ge(cmp_gelu, item(gp))
                if first and gp == 0:
                    pe.wait_ge(rest_done, RING * kv + RING)
            for t in range(16 * part, 16 * part + 16):
                u, k = t // 8, t % 8
                w = slice(k * P, (k + 1) * P)
                sh = 2 * part
                hi, lo = (r[:, t % 16, :, :].rearrange("p n g -> p (n g)")[:, sh:sh + 2 * NCMP] for r in (RH, RL))
                o = PSUM[:, 2, 0:2 * NCMP]
                nc.tensor.matmul(o, WH[:, u, w], hi, start=t == 0, stop=False)
                nc.tensor.matmul(o, WH[:, u, w], lo, start=False, stop=False)
                last_ = nc.tensor.matmul(o, WL[:, u, w], hi, start=False, stop=t == TAPS - 1)
            if part == 1:
                last_.then_inc(cmp_acc, 1)

        bct()
        bu(0)
        tp(0, 0, 4)
        if not first:
            second_pe(pe, kv, item(0) - 1)
        bu(1)
        y(0)
        tp(0, 4, 8)
        mm(0, 0)
        bu(2)
        y(1)
        mm(0, 1)
        second_pe(pe, kv, item(0), first and kv == 0)
        tp(1, 0, 4)
        bu(3)
        y(2)
        tp(1, 4, 8)
        y(3)
        mm(1, 0)
        mm(1, 1)

    def second_pe(pe, kv, item, very_first=False):
        pe.wait_ge(cmp_gelu, item + 1)
        if not very_first:
            pe.wait_ge(cmp_out, item)
        if kv == 0:
            for k in range(2):
                last = nc.tensor.matmul(PSUM[:, 3, 256 * k:256 * k + 2 * NCMP], W2K[:, k, :], GEL[:, :], start=True, stop=True)
        else:
            for g in range(2):
                hid = GEL[:, :].rearrange("p (n g) -> p g n", g=2)[:, g, :]
                last = nc.tensor.matmul(PSUM[0:NCMP, 3, g * P:(g + 1) * P], hid, W2V[:, :], start=True, stop=True)
        last.then_inc(cmp_mm2, 1)

    def body_act(act, kv, i, first):
        c = i + NKV * kv
        item = lambda gp: 2 * c + gp

        def take_x(j):
            q = tile(c, j)
            act.wait_ge(pe_bu, q + 1)
            if not (first and kv == 0 and j < 2):
                act.wait_ge(dve_rot, q - 1)
                act.wait_ge(pool_rot, q - 1)
            nc.scalar.activation(XRI[:, j % 2, :, :], PSUM[:, 4:6, 0:T], ACT.Copy).then_inc(act_x, 1)

        def heads(gp, lo, hi):
            for m in range(lo, hi):
                n = 8 * item(gp) + m
                act.wait_ge(cmp_tp, n + 1)
                if m == 0 and not (first and kv == 0 and gp == 0):
                    act.wait_ge(cmp_acc, item(gp))
                nc.scalar.activation(rows_of(RH, m), page_rows(m % 2), ACT.Copy).then_inc(cmp_head, 1)

        act.wait_ge(bct_tp, c + 1)
        if not (first and kv == 0):
            act.wait_ge(pe_y, 4 * c)
        nc.scalar.activation(BCT[:, :, :], PSUM[:, 7, :].rearrange("p (k n) -> p k n", k=4), ACT.Copy).then_inc(bct_done, 1)
        take_x(0)
        tables_act(act, tile(c, 1), 1, first and kv == 0)
        heads(0, 0, 4)
        if not first:
            keep_act(act, kv, item(0) - 1, i - 1, 1)
        take_x(1)
        tables_act(act, tile(c, 2), 0)
        heads(0, 4, 8)
        take_x(2)
        tables_act(act, tile(c, 3), 1)
        gelu_act(act, kv, item(0), first and kv == 0)
        heads(1, 0, 4)
        take_x(3)
        tables_act(act, tile(c, 4), 0)
        keep_act(act, kv, item(0), i, 0)
        heads(1, 4, 8)
        act.wait_ge(y_sum, c + 1)
        nc.scalar.activation(HN[:, 3, :], HN[:, 3, :], ACT.Gelu_apprx_tanh).then_inc(y_gelu, 1)
        gelu_act(act, kv, item(1))
        act.wait_ge(y_gelu, c + 1)
        nc.scalar.activation(XH[:, ds(c, 1), :].rearrange("p o t -> p (o t)"), HN[:, 3, :], ACT.Copy).then_inc(xh_done, 1)

    def tables_act(act, q, par_, very_first=False):
        act.wait_ge(pool_fs, q + 1)
        act.wait_ge(dve_fc, q + 1)
        if not very_first:
            act.wait_ge(dve_h, q - 1)
            act.wait_ge(pool_der, q - 1)
        nc.scalar.activation(SN[:, par_, :], FS[:, :], ACT.Sin, scale=TWOPI_IN)
        nc.scalar.activation(CS[:, par_, :], FCO[:, :], ACT.Sin, scale=-TWOPI_IN, bias=EPSB[:, 1:2]).then_inc(act_tab, 1)

    def gelu_act(act, kv, item, very_first=False):
        act.wait_ge(cmp_acc, item + 1)
        if not very_first:
            act.wait_ge(cmp_mm2, item)
        nc.scalar.activation(GEL[:, :], PSUM[:, 2, 0:2 * NCMP], ACT.Gelu_apprx_tanh,
                             bias=GW[:, 48 + kv:49 + kv]).then_inc(cmp_gelu, 1)

    def keep_act(act, kv, item, b, gp):
        if kv == 0:
            act.wait_ge(cmp_out, item + 1)
            src, dst = CMPO[:, 0:2 * NCMP], kscr
        else:
            act.wait_ge(cmp_mm2, item + 1)
            act.wait_ge(cmp_kept, 16 * item)
            nc.scalar.activation(CMPO[0:NCMP, :], PSUM[0:NCMP, 3, 0:2 * P], ACT.Copy).then_inc(cmp_out, 1)
            act.wait_ge(cmp_out, item + 1)
            src, dst = CMPO[0:NCMP, :], vscr
        act.dma_start(dst[ds(b, 1), gp].rearrange("o p n -> (o p) n"), src).then_inc(cmp_kept, 16)

    def turns_dve(dve, q, very_first=False):
        dve.wait_ge(pool_t1, q + 1)
        if not very_first:
            dve.wait_ge(pool_fs, q)
        nc.vector.tensor_scalar(KS[:, :], T1[:, :], MAGIC, -MAGIC, ALU.add, ALU.add).then_inc(dve_ks, 1)
        nc.vector.tensor_scalar(KCR[:, :], T1[:, :], 0.25, MAGIC, ALU.add, ALU.add).then_inc(dve_kc, 1)

    def cosine_dve(dve, q, very_first=False):
        dve.wait_ge(dve_kc, q + 1)
        if not very_first:
            dve.wait_ge(act_tab, q)
        nc.vector.scalar_tensor_tensor(out=FCO[:, :], in0=KCR[:, :], scalar=-MAGIC, in1=T1[:, :],
                                       op0=ALU.add, op1=ALU.subtract).then_inc(dve_fc, 1)

    def prologue_dve(dve):
        turns_dve(dve, 0, True)
        cosine_dve(dve, 0, True)

    def body_dve(dve, kv, i, first):
        c = i + NKV * kv
        V = nc.vector
        item = lambda gp: 2 * c + gp

        if not (first and kv == 0):
            dve.wait_ge(pe_bu, 4 * c)
            dve.wait_ge(y_sum, c)
        V.scalar_tensor_tensor(out=HN[:, 0, :], in0=X[:, ds(c, 1), :].rearrange("p o t -> p (o t)"),
                               scalar=GV[:, ds(c, 1)], in1=RSTD[:, :], op0=ALU.mult, op1=ALU.mult).then_inc(hn_chunk, 1)
        dve.wait_ge(bc_loaded, 64 * c + 64)
        cf = [PR[:, k:k + 1, ds(4 * c, 4)].rearrange("p o q -> p (o q)").unsqueeze(2).to_broadcast([P, 4, GRP]) for k in (9, 10)]
        V.tensor_tensor(BP[:, 0, :, :], cf[0], BN[:, 0, :, :], ALU.mult)
        V.tensor_tensor(BP[:, 1, :, :], cf[1], BN[:, 1, :, :], ALU.mult)
        V.tensor_tensor(BP[:, 2, :, :], cf[0], BN[:, 1, :, :], ALU.mult)
        V.tensor_tensor(BP[:, 3, :, :], cf[1], BN[:, 0, :, :], ALU.mult).then_inc(b_prod, 1)
        dve.wait_ge(b_prod, c + 1)
        if not (first and kv == 0):
            dve.wait_ge(bct_tp, c)
        bp = BPAD[:, :, :].rearrange("p k (j e h) -> p k e j h", j=4, e=2)
        for e in range(2):
            r = slice(ST * e, ST * e + ST)
            V.tensor_tensor(bp[r, 0, e], BP[r, 0], BP[r, 1], ALU.subtract)
            V.tensor_tensor(bp[r, 1, e], BP[r, 2], BP[r, 3], ALU.add)
        for k in range(2):
            last = V.tensor_tensor(CPAD[:, k, :].rearrange("p (e s) -> p e s", e=2), CN_[:, k, :].unsqueeze(1).to_broadcast([P, 2, ST]),
                                   CMASK[:, k, :].rearrange("p (e s) -> p e s", e=2), ALU.mult)
        last.then_inc(bc_ready, 1)

        def state_tile(j):
            q, b = tile(c, j), j % 2
            x, sn, cs = XRI[:, b, :, 0:TP], SN[:, b, :], CS[:, b, :]
            G2 = HN[:, 1:3, 0:TP]
            dve.wait_ge(act_tab, q + 1)
            dve.wait_ge(act_x, q + 1)
            V.tensor_tensor(N12[:, :, :], x, cs.unsqueeze(1).to_broadcast([P, 2, TP]), ALU.mult).then_inc(dve_n, 1)
            dve.wait_ge(dve_n, q + 1)
            dve.wait_ge(pool_rot, q + 1)
            V.tensor_tensor(G2[:, 0], N12[:, 0, :], M12[:, 0, :], ALU.add)
            V.tensor_tensor(G2[:, 1], N12[:, 1, :], M12[:, 1, :], ALU.subtract).then_inc(dve_rot, 1)
            dve.wait_ge(dve_rot, q + 1)
            m = PR[:, 4:5, ds(q, 1)].rearrange("p o q -> p (o q)").to_broadcast([P, TP])
            for k in range(2):
                last_ = V.tensor_tensor_scan(SRI[:, k, :], m, G2[:, k], 0.0, ALU.mult, ALU.add)
            last_.then_inc(dve_scan, 1)
            turns_dve(dve, q + 1)
            dve.wait_ge(dve_scan, q + 1)
            V.tensor_tensor(N12[:, :, :], SRI[:, :, :], cs.unsqueeze(1).to_broadcast([P, 2, TP]), ALU.mult).then_inc(dve_n2, 1)
            cosine_dve(dve, q + 1)
            dve.wait_ge(dve_n2, q + 1)
            dve.wait_ge(pool_der, q + 1)
            if not (first and kv == 0 and j < 2):
                dve.wait_ge(pe_y, q - 1)
                dve.wait_ge(pool_fin, q - 1)
            V.tensor_tensor(H[:, b, 0, 0:TP], N12[:, 0, :], M12[:, 0, :], ALU.subtract)
            V.tensor_tensor(H[:, b, 1, 0:TP], N12[:, 1, :], M12[:, 1, :], ALU.add).then_inc(dve_h, 1)

        def rests(gp, lo, hi):
            for m in range(lo, hi):
                dve.wait_ge(cmp_head, 8 * item(gp) + m + 1)
                V.tensor_tensor(rows_of(RL, m), page_rows(m % 2), rows_of(RH, m).bitcast(F32), ALU.subtract).then_inc(cmp_rest, 1)

        state_tile(0)
        rests(0, 0, 4)
        if not first:
            rotate_dve(dve, kv, item(0) - 1)
        state_tile(1)
        rests(0, 4, 8)
        state_tile(2)
        rests(1, 0, 4)
        rotate_dve(dve, kv, item(0), first and kv == 0)
        state_tile(3)
        rests(1, 4, 8)
        dve.wait_ge(pe_y, 4 * c + 4)
        if not (first and kv == 0):
            dve.wait_ge(xl_done, c)
        V.scalar_tensor_tensor(out=HN[:, 3, :], in0=HN[:, 0, :], scalar=GW[:, ds(c, 1)], in1=PSUM[:, 6, 0:T],
                               op0=ALU.mult, op1=ALU.add).then_inc(y_sum, 1)
        dve.wait_ge(xh_done, c + 1)
        V.tensor_tensor(XL[:, ds(c, 1), :].rearrange("p o t -> p (o t)"), HN[:, 3, :],
                        XH[:, ds(c, 1), :].rearrange("p o t -> p (o t)").bitcast(F32), ALU.subtract).then_inc(xl_done, 1)

    def rotate_dve(dve, kv, item, very_first=False):
        if kv:
            return
        V = nc.vector
        dve.wait_ge(cmp_mm2, item + 1)
        V.tensor_tensor(RTMP[:, :], PSUM[:, 3, 256:256 + 2 * NCMP], ROPC[:, 1, :], ALU.mult)
        if not very_first:
            dve.wait_ge(cmp_kept, 16 * item)
        V.tensor_tensor(CMPO[:, 0:2 * NCMP], PSUM[:, 3, 0:2 * NCMP], ROPC[:, 0, :], ALU.mult).then_inc(rope_part, 1)
        dve.wait_ge(rope_part, item + 1)
        V.tensor_tensor(CMPO[:, 0:2 * NCMP], CMPO[:, 0:2 * NCMP], RTMP[:, :], ALU.add).then_inc(cmp_out, 1)

    def turns_pool(pool, q, very_first=False):
        if not very_first:
            pool.wait_ge(dve_fc, q)
            pool.wait_ge(pool_fs, q)
        shape = [P, 16, 16]
        a = ARGA[:, ds(q, 1), :].rearrange("p o b -> p (o b)").unsqueeze(2).to_broadcast(shape)
        b = ARGB[:, ds(q, 1), :].rearrange("p o b -> p (o b)").unsqueeze(1).to_broadcast(shape)
        nc.gpsimd.tensor_tensor(T1[:, :].rearrange("p (a b) -> p a b", b=16), a, b, ALU.add).then_inc(pool_t1, 1)

    def parts_pool(pool, q, very_first=False):
        pool.wait_ge(dve_ks, q + 1)
        pool.wait_ge(pool_t1, q + 1)
        if not very_first:
            pool.wait_ge(act_tab, q)
        nc.gpsimd.tensor_tensor(FS[:, :], T1[:, :], KS[:, :], ALU.subtract).then_inc(pool_fs, 1)

    def prologue_pool(pool):
        pool.wait_ge(arg_ready, N_PAR)
        turns_pool(pool, 0, True)
        parts_pool(pool, 0, True)

    def body_pool(pool, kv, i, first):
        c = i + NKV * kv
        Q = nc.gpsimd
        for j in range(4):
            q, b = tile(c, j), j % 2
            sn = SN[:, b, :].unsqueeze(1).to_broadcast([P, 2, TP])
            very_first = first and kv == 0
            pool.wait_ge(act_tab, q + 1)
            pool.wait_ge(act_x, q + 1)
            if not (very_first and j == 0):
                pool.wait_ge(dve_h, q)
            if not (very_first and j < 2):
                pool.wait_ge(pe_y, q - 1)
                pool.wait_ge(pool_fin, q - 1)
            Q.tensor_tensor(M12[:, 0, :], XRI[:, b, 1, 0:TP], SN[:, b, :], ALU.mult)
            Q.tensor_tensor(M12[:, 1, :], XRI[:, b, 0, 0:TP], SN[:, b, :], ALU.mult)
            w0 = W0[:, :, ds(q, 1), :].rearrange("p k o b -> p k (o b)")
            Q.tensor_tensor(H[:, b, :, TP:T], w0, XRI[:, b, :, TP:T], ALU.add).then_inc(pool_rot, 1)
            turns_pool(pool, q + 1)
            pool.wait_ge(dve_scan, q + 1)
            Q.tensor_tensor(M12[:, 0, :], SRI[:, 1, :], SN[:, b, :], ALU.mult)
            Q.tensor_tensor(M12[:, 1, :], SRI[:, 0, :], SN[:, b, :], ALU.mult).then_inc(pool_der, 1)
            parts_pool(pool, q + 1)
            pool.wait_ge(dve_h, q + 1)
            pool.wait_ge(pool_rot, q + 1)
            last = H[:, b, :, TP - 1:T]
            Q.tensor_tensor(FIN[:, :, ds(q, 1), :].rearrange("p k o b -> p k (o b)"), last,
                            ONES[:, 0:2 * (1 + TS)].rearrange("p (k b) -> p k b", k=2), ALU.mult).then_inc(pool_fin, 1)

    upto = io.get("_upto", 99)

    def sequences(eng, body):
        def run(kv):
            body(eng, kv, 0, True)
            with eng.Fori(1, NKV) as i:
                body(eng, kv, i, False)
        return run

    def stage1_sp(sp):
        run = sequences(sp, body_sp)
        sp.wait_ge(ld["late"], L_LATE)
        run(0)
        for u in range(RING):
            sp.wait_ge(cmp_tp, 8 * (2 * NKV - 1) + 2 * u + 2)
            load_taps(sp, 1, u)
        run(1)
        for u in range(RING):
            sp.wait_ge(cmp_tp, 8 * (4 * NKV - 1) + 2 * u + 2)
            load_unit(sp, Unit(TAP_UNITS + u), weight("glu", 0, 0)[:, UK * u:UK * (u + 1), :])

    def stage1_pe(pe):
        rms_pe(pe, "mix0")
        run = sequences(pe, body_pe)
        pe.wait_ge(ld["late"], L_LATE)
        for kv in range(2):
            run(kv)
            second_pe(pe, kv, 2 * NKV * (kv + 1) - 1)

    def stage1_act(act):
        tables_act(act, 0, 0, True)
        run = sequences(act, body_act)
        for kv in range(2):
            run(kv)
            n = 2 * NKV * (kv + 1)
            keep_act(act, kv, n - 1, NKV - 1, 1)
            act.wait_ge(cmp_acc, n)
            for u in range(RING):
                split_head(act, Unit(RING * (kv + 1) + u))

    def stage1_dve(dve):
        prologue_dve(dve)
        run = sequences(dve, body_dve)
        for kv in range(2):
            run(kv)
            rotate_dve(dve, kv, 2 * NKV * (kv + 1) - 1)
            for u in range(RING):
                split_rest(dve, Unit(RING * (kv + 1) + u))
        dve.wait_ge(pool_fin, NQ)
        dve.wait_ge(pool_fs, NQ + 1)
        dve.wait_ge(act_tab, NQ + 1)
        dve.wait_ge(cmp_kept, 16 * 4 * NKV)

    def stage1_pool(pool):
        prologue_pool(pool)
        run = sequences(pool, body_pool)
        for kv in range(2):
            run(kv)

    def final_states_pe(pe):
        pass

    V = nc.vector

    X_ADDS = {"glu": 0, "ple0": 4, "ple1": 8}
    HID_USES, at = {}, 1
    for n in ("gu10", "gu20", "gu11", "gu21"):
        HID_USES[n] = at
        at += by_name[n].steps

    def add_to_x(dve, name, i):
        ph = by_name[name]
        xs = X[:, ds(4 * i, 4), :]
        V.tensor_tensor(xs, xs, ZB[:, :, :], ALU.add).then_inc(x_done, 1)
        square_dve(dve, ph.sq + i, SSQ[:, ds(i, 1), :])

    def glu_act(act):
        ph = by_name["glu"]

        def b(i):
            act.wait_ge(free_b, i + 1)
            nc.scalar.activation(ZB[:, :, :], ZB[:, :, :], ACT.Sigmoid).then_inc(glu_sig, 1)
            square_act(act, ph.sq + i, ds(4 * i, 4), x_done, i + 1)
        after_units(act, "glu", split_head, nothing, b)

    def glu_dve(dve):
        def bias(i, half):
            return GW[:, ds(4 * i + (16 + 16 * half), 4)].unsqueeze(2).to_broadcast([P, 4, T])

        def a(i):
            V.tensor_tensor(ZA[:, :, :], A4, bias(i, 0), ALU.add).then_inc(free_a, 1)

        def b(i):
            V.tensor_tensor(ZB[:, :, :], B4, bias(i, 1), ALU.add).then_inc(free_b, 1)
            dve.wait_ge(glu_sig, i + 1)
            V.tensor_tensor(ZB[:, :, :], ZA[:, :, :], ZB[:, :, :], ALU.mult).then_inc(prod_done, 1)
            dve.wait_ge(prod_done, i + 1)
            add_to_x(dve, "glu", i)
        after_units(dve, "glu", split_rest, a, b)

    def gate_act(act, name, func, hidden):
        ph = by_name[name]

        def a(i):
            act.wait_ge(free_b, ph.groups + i)
            nc.scalar.activation(ZA[:, :, :], A4, func).then_inc(free_a, 1)

        def b(i):
            if hidden:
                act.wait_ge(free_b, ph.groups + i + 1)
                nc.scalar.activation(HH[:, ds(4 * i, 4), :], ZB[:, :, :], ACT.Copy).then_inc(hh_done, 1)
            else:
                square_act(act, ph.sq + i, ds(4 * i, 4), x_done, X_ADDS[name] + i + 1)
        after_units(act, name, split_head, a, b)

    def gate_dve(dve, name, hidden):
        ph = by_name[name]

        def b(i):
            if hidden:
                dve.wait_ge(hl_done, HID_USES[name] + i)
            dve.wait_ge(free_a, ph.groups + i + 1)
            V.tensor_tensor(ZB[:, :, :], ZA[:, :, :], B4, ALU.mult).then_inc(free_b, 1)
            if not hidden:
                dve.wait_ge(free_b, ph.groups + i + 1)
                add_to_x(dve, name, i)
        after_units(dve, name, split_rest, nothing, b)

    def hidden_pool(pool, name):
        ph = by_name[name]
        with pool.Fori(0, ph.steps) as i:
            pool.wait_ge(hh_done, HID_USES[name] + i)
            pool.wait_ge(free_b, ph.groups + i + 1)
            nc.gpsimd.tensor_tensor(HL[:, ds(4 * i, 4), :], ZB[:, :, :], HH[:, ds(4 * i, 4), :].bitcast(F32),
                                    ALU.subtract).then_inc(hl_done, 1)

    def add_dve(dve, name, squares):
        ph = by_name[name]

        def part(half, bank, free):
            def f(i):
                xs = X[:, ds(8 * i + 4 * half, 4), :]
                V.tensor_tensor(xs, xs, bank, ALU.add).then_inc(free, 1)
                if squares:
                    square_dve(dve, ph.sq + 2 * i + half, SSQ[:, ds(2 * i + half, 1), :])
            return f
        after_units(dve, name, split_rest, part(0, A4, free_a), part(1, B4, free_b))

    def add_act(act, name, squares):
        ph = by_name[name]

        def part(half, free):
            def f(i):
                if squares:
                    square_act(act, ph.sq + 2 * i + half, ds(8 * i + 4 * half, 4), free, ph.groups + i + 1)
            return f
        after_units(act, name, split_head, part(0, free_a), part(1, free_b))

    def keep_groups_act(act, name, dst):
        def part(half, bank, free):
            return lambda i: nc.scalar.activation(dst(2 * i + half), bank, ACT.Copy).then_inc(free, 1)
        after_units(act, name, split_head, part(0, A4, free_a), part(1, B4, free_b))

    def only_split_dve(dve, name):
        after_units(dve, name, split_rest, nothing, nothing)

    def ffn_sp(sp, l):
        for n in ("gu1", "dn1", "gu2", "dn2", "ple"):
            phase_sp(sp, n + str(l))

    def ffn_pe(pe, l):
        rms_pe(pe, f"ffn{l}")
        for part in "12":
            gu, dn = f"gu{part}{l}", f"dn{part}{l}"
            phase_pe(pe, gu, XH, XL, normed_ready(pe, f"ffn{l}") if part == "1" else None)
            phase_pe(pe, dn, HH, HL, lambda k: pe.wait_ge(hl_done, HID_USES[gu] + k // 4 + 1))
        rms_pe(pe, f"ple{l}")
        phase_pe(pe, f"ple{l}", XH, XL, normed_ready(pe, f"ple{l}"), PH[:, l], PL[:, l])

    def ffn_act(act, l):
        rms_act(act, f"ffn{l}")
        norm_act(act, f"ffn{l}")
        for part in "12":
            gate_act(act, f"gu{part}{l}", ACT.Silu, True)
            add_act(act, f"dn{part}{l}", part == "2")
        rms_act(act, f"ple{l}")
        norm_act(act, f"ple{l}")
        gate_act(act, f"ple{l}", ACT.Sigmoid, False)

    def ffn_dve(dve, l):
        rms_dve(dve, f"ffn{l}")
        norm_dve(dve, f"ffn{l}", NFFN[l])
        for part in "12":
            gate_dve(dve, f"gu{part}{l}", True)
            add_dve(dve, f"dn{part}{l}", part == "2")
        rms_dve(dve, f"ple{l}")
        norm_dve(dve, f"ple{l}", NPLE[l])
        gate_dve(dve, f"ple{l}", False)

    def ffn_pool(pool, l):
        for part in "12":
            hidden_pool(pool, f"gu{part}{l}")

    class Steps:

        def __init__(self, name, steps):
            self.sem, self.steps, self.made = sem(name), steps, 0

        def made_by(self, ins, step):
            assert self.steps[self.made] == step, (step, self.steps[self.made])
            self.made += 1
            ins.then_inc(self.sem, 1)

        def wait(self, eng, step):
            eng.wait_ge(self.sem, self.steps.index(step) + 1)

    fs_tp, fs_used = sem("fs_tp"), sem("fs_used")
    FS_BANKS = 5

    def states_pe(pe):
        pe.wait_ge(pool_fin, NQ)
        pe.wait_ge(y_sum, KC)
        pe.wait_ge(act_x, NQ)
        pe.wait_ge(cmp_out, 4 * NKV)
        pe.wait_ge(cmp_rest, 32 * NKV)
        n = 2 * (1 + TS)
        for j in range(n):
            k, b = divmod(j, 1 + TS)
            last = nc.tensor.transpose(PSUM[0:NQ, j // 4, (j % 4) * P:(j % 4 + 1) * P], FIN[:, k, :, b], IDENT[:, :])
            if j % 4 == 3 or j == n - 1:
                last.then_inc(fs_tp, 1)
        pe.wait_ge(fs_used, FS_BANKS)

    def states_dve(dve):
        for j in range(FS_BANKS):
            m = min(4, 2 * (1 + TS) - 4 * j)
            dve.wait_ge(fs_tp, j + 1)
            V.tensor_copy(OUTS[:, 4 * j:4 * j + m, :], PSUM[0:NQ, j, 0:m * P].rearrange("q (b s) -> q b s", s=P)).then_inc(fs_used, 1)

    def states_sp(sp):
        sp.wait_ge(fs_used, FS_BANKS)
        for k, n in enumerate(("ssm_re", "ssm_im")):
            at = k * (1 + TS)
            view = lambda name: out[name][0].rearrange("b (q e) s -> q b (e s)", e=2)
            sp.dma_start(view(n + "_prompt"), OUTS[:, at:at + 1, :]).then_inc(stored, 16)
            sp.dma_start(view(n + "_sample"), OUTS[:, at + 1:at + 1 + TS, :]).then_inc(stored, 16)
    STATES_STORED = 64

    att_ready = [sem(f"att_ready{k}") for k in range(RING)]
    att_used = sem("att_used")
    ld_gate, ld_masks, ld_taps, ld_kc, ld_vc, gates_moved = (
        sem(n) for n in ("ld_gate", "ld_masks", "ld_taps", "ld_kc", "ld_vc", "gates_moved"))
    rows_stored, shift_stored = sem("rows_stored"), sem("shift_stored")
    SLC_PAGES, WIN_PAGES = TS * PAGES, TS * WIN // PAGE
    BRANCH = {"sk": 0, "wk": SLC_PAGES, "sv": SLC_PAGES + WIN_PAGES, "wv": 2 * SLC_PAGES + WIN_PAGES}
    ATT_PAGES = 2 * (SLC_PAGES + WIN_PAGES)

    def before_kv_sp(sp):
        sp.wait_ge(ssq_done, by_name["ple0"].sq)
        sp.dma_start(WGR[:, :, :], io["nsa_w_gate"][0].rearrange("(k p) n -> p k n", p=P)).then_inc(ld_gate, 16)
        sp.dma_start(BGATE[0:48, 0:1], io["nsa_b_gate"][0].rearrange("(p a) -> p a", a=1)).then_inc(ld_gate, 16)

    def attention_small_sp(sp):
        gate_pe.wait(sp, "gates")
        for dst, name in ((CAUS, "causal"), (CMPV, "cmpvis"), (ROPP, "ropep"), (BD, "bd"), (SAME, "same"),
                          (TOB, "toblk"), (EARL, "earlier")):
            sp.dma_start(dst[:], io["k_" + name]).then_inc(ld_masks, 16)
        sp.dma_start(W1P[:, :, :], w1[0].rearrange("t d h -> d t h")).then_inc(ld_taps, 16)
        sp.dma_start(W1Q[:, :, :], w1[1].rearrange("t d h -> d t h")).then_inc(ld_taps, 16)
        sp.dma_start(W2P[:, 0, :], io["cmp_k_w2"]).then_inc(ld_taps, 16)
        sp.dma_start(W2P[:, 1, 0:64], io["cmp_k_w2"][:, 64:128]).then_inc(ld_taps, 16)
        sp.dma_start(W2P[:, 1, 64:128], io["cmp_k_w2"][:, 0:64]).then_inc(ld_taps, 16)
        sp.dma_start(W2P[:, 2, :], io["cmp_v_w2"]).then_inc(ld_taps, 16)
    L_MASKS, L_TAPS = 16 * 7, 16 * 6

    def cache_pages_sp(sp, name, branch):
        view = io[name].rearrange("n r g d -> n r (g d)")

        def body(i, first):
            for u in range(PAGES // 2):
                pages = [sp.value_load(PT[0:1, ds(i * PAGES + (2 * u + k), 1)], min_val=0, max_val=POOL - 1) for k in range(2)]
                if first and u < RING:
                    sp.wait_ge(rest_done, by_name["o"].base + RING)
                else:
                    sp.wait_ge(att_used, BRANCH[branch] + i * PAGES + (2 * u - 6))
                for k, page in enumerate(pages):
                    sp.dma_start(RAW[:, u % RING, k * 512:(k + 1) * 512],
                                 view[ds(page, 1)].rearrange("o r n -> (o r) n")).then_inc(att_ready[u % RING], 16)

        if BRANCH[branch] == 0:
            body(0, True)
            with sp.Fori(1, TS) as i:
                body(i, False)
        else:
            with sp.Fori(0, TS) as i:
                body(i, False)

    def window_pages_sp(sp, name, branch):
        view = io[name].rearrange("b (u t p) g d -> (b u) p t (g d)", u=2, p=P)
        with sp.Fori(0, TS // 2) as i:
            for u in range(4):
                sp.wait_ge(att_used, BRANCH[branch] + i * 8 + (2 * u - 6))
                sp.dma_start(RAW[:, u, :].rearrange("p (t n) -> p t n", t=2),
                             view[ds(4 * i + u, 1)].rearrange("o p t n -> (o p) t n")).then_inc(att_ready[u], 32)

    def wait_page(pe, n_base, i, per, j):
        u = j // 2
        turns = 32 * (n_base // 8) + 32 * (per // 8) * i + 32 * (u // RING) + 32
        pe.wait_ge(att_ready[u % RING], turns)

    gate_pe = Steps("gate_pe", ["gates"])
    at_const, wg_zero, wg_head, wg_split, gate_sig = (sem(n) for n in ("at_const", "wg_zero", "wg_head", "wg_split", "gate_sig"))
    sw_done, sw_used, rope_cos, rope_done, new_done = (sem(n) for n in ("sw_done", "sw_used", "rope_cos", "rope_done", "new_done"))
    nt_done, nt_used = sem("nt_done"), sem("nt_used")
    nat_stored = [sem(f"nat_stored{k}") for k in range(2)]
    ROPED = [KVT[:, 2, :, :], KVT[:, 4, :, :]] + [QT[:, 4 * j:4 * j + 4, :] for j in range(4)]
    NT_JOBS = 15
    KEPT = {3: 0, 5: 1}

    def rotate_pe(pe):
        ph = by_name["o"]
        pe.wait_ge(at_const, 1)
        for j, src in enumerate(ROPED):
            if j == 0:
                pe.wait_ge(free_a, ph.groups)
            if j == 1:
                pe.wait_ge(free_b, ph.groups)
            if j >= 2:
                pe.wait_ge(sw_used, j - 1)
            for h in range(4):
                last = nc.tensor.matmul(PSUM[:, 4 * (j % 2) + h, 0:T], SWAP[:, :], src[:, h, :], start=True, stop=True)
            last.then_inc(sw_done, 1)
        pe.wait_ge(wg_split, 1)
        pe.wait_ge(sw_used, 5)
        for k in range(KC):
            nc.tensor.matmul(PSUM[:, 0, 0:T], WGH[:, k, :], XH[:, k, :], start=k == 0, stop=False)
            nc.tensor.matmul(PSUM[:, 0, 0:T], WGH[:, k, :], XL[:, k, :], start=False, stop=False)
            last = nc.tensor.matmul(PSUM[:, 0, 0:T], WGL[:, k, :], XH[:, k, :], start=False, stop=k == KC - 1)
        gate_pe.made_by(last, "gates")
        pe.wait_ge(rope_done, 6)
        for j in range(NT_JOBS):
            bank = 1 + j % 7
            if j >= 7:
                pe.wait_ge(nt_used, j - 6)
            if j < 12:
                t, qt = divmod(j, 2)
                for g in range(G):
                    last = nc.tensor.transpose(PSUM[:, bank, g * DH:(g + 1) * DH], KVT[:, t, g, qt * P:(qt + 1) * P], IDENT[:, :])
            elif j < 14:
                pe.wait_ge(new_done, 1)
                for m in range(4 if j == 12 else 2):
                    t = 4 * (j - 12) + m
                    last = nc.tensor.transpose(PSUM[0:TS * G, bank, m * DH:(m + 1) * DH], KS6[:, t, :], IDENT[:, :])
            else:
                pe.wait_ge(gate_sig, 1)
                for qt in range(2):
                    nc.tensor.transpose(PSUM[:, bank, qt * 48:(qt + 1) * 48], GT[0:48, qt * P:(qt + 1) * P], IDENT[0:48, 0:48])
                last = nc.tensor.transpose(PSUM[0:TS, bank, 96:144], GT[0:48, TP:T], IDENT[0:48, 0:48])
            last.then_inc(nt_done, 1)

    def rotate_dve_all(dve):
        V.tensor_copy(SWAP[:, 0:64], IDENT[:, 64:128])
        V.tensor_copy(SWAP[:, 64:128], IDENT[:, 0:64]).then_inc(at_const, 1)
        V.memset(WGH[:, :, :].bitcast(F32), 0.0)
        V.memset(WGL[:, :, :].bitcast(F32), 0.0).then_inc(wg_zero, 1)
        for j, dst in enumerate(ROPED):
            cos, sin = (ROPET[:, k, :].unsqueeze(1).to_broadcast([P, 4, T]) for k in range(2))
            dve.wait_ge(sw_done, j + 1)
            if j >= 2:
                dve.wait_ge(rope_done, j - 1)
            part = (ZA, ZB)[j % 2]
            V.tensor_tensor(part[:, :, :], PSUM[:, 4 * (j % 2):4 * (j % 2) + 4, 0:T], sin, ALU.mult).then_inc(sw_used, 1)
            V.tensor_tensor(dst, dst, cos, ALU.mult).then_inc(rope_cos, 1)
            dve.wait_ge(rope_cos, j + 1)
            V.tensor_tensor(dst, dst, part[:, :, :], ALU.add).then_inc(rope_done, 1)
            if j == 1:
                dve.wait_ge(wg_head, 1)
                V.tensor_tensor(WGL[:, :, 0:48], WGR[:, :, :], WGH[:, :, 0:48].bitcast(F32), ALU.subtract).then_inc(wg_split, 1)
        dve.wait_ge(rope_done, 6)
        V.tensor_copy(KS6[:, :, :].rearrange("p t (b g) -> p t b g", g=G), KVT[:, :, :, TP:T].rearrange("p t g b -> p t b g")).then_inc(new_done, 1)
        V.tensor_copy(QS[:, :].rearrange("p (b h) -> p b h", h=NH), QT[:, :, TP:T].rearrange("p h b -> p b h")).then_inc(new_done, 1)
        stores = 0
        for j in range(NT_JOBS):
            bank = 1 + j % 7
            dve.wait_ge(nt_done, j + 1)
            if j < 12:
                t, qt = divmod(j, 2)
                if t in KEPT:
                    dst = VNAT[:, KEPT[t], qt, :]
                else:
                    dst = NAT[:, stores % 2, :]
                    if stores >= 2:
                        dve.wait_ge(nat_stored[stores % 2], 16 * (stores // 2))
                    stores += 1
                V.tensor_copy(dst, PSUM[:, bank, :]).then_inc(nt_used, 1)
            elif j < 14:
                m = 4 if j == 12 else 2
                V.tensor_copy(SNAT[:, 4 * (j - 12):4 * (j - 12) + m, :].rearrange("p t d -> p (t d)"), PSUM[0:TS * G, bank, 0:m * DH]).then_inc(nt_used, 1)
            else:
                V.tensor_copy(GNS[:, :], PSUM[0:TS, bank, 96:144])
                V.tensor_copy(GN[:, :, :].rearrange("p q n -> p (q n)"), PSUM[:, bank, 0:96]).then_inc(nt_used, 1)

    ROW_NAMES = ["cmp_k", "cmp_v", "slc_k", "slc_v", "win_k", "win_v"]
    PASSING = [j for j in range(12) if j // 2 not in KEPT]

    def rotate_act_all(act):
        act.wait_ge(ld_gate, 32)
        act.wait_ge(wg_zero, 1)
        nc.scalar.activation(WGH[:, :, 0:48], WGR[:, :, :], ACT.Copy).then_inc(wg_head, 1)
        gate_pe.wait(act, "gates")
        nc.scalar.activation(GT[0:48, :], PSUM[0:48, 0, 0:T], ACT.Sigmoid, bias=BGATE[0:48, 0:1]).then_inc(gate_sig, 1)

    def rows_sp(sp):
        for j in range(12):
            t, qt = divmod(j, 2)
            sp.wait_ge(nt_used, j + 1)
            slot = None if t in KEPT else PASSING.index(j) % 2
            src = VNAT[:, KEPT[t], qt, :] if slot is None else NAT[:, slot, :]
            dst = out[ROW_NAMES[t] + "_prompt"][0].rearrange("(q p) g d -> q p (g d)", p=P)[qt]
            sp.dma_start(dst, src).then_inc(rows_stored if slot is None else nat_stored[slot], 16)
        sp.wait_ge(nt_used, NT_JOBS)
        for t in range(4):
            sp.dma_start(out[ROW_NAMES[t] + "_sample"].rearrange("b o g d -> (b o g) d"), SNAT[:, t, :]).then_inc(rows_stored, 16)
        for t in (4, 5):
            for b in range(TS):
                sp.dma_start(out[ROW_NAMES[t] + "_sample"][b, WIN - 1], SNAT[G * b:G * b + G, t, :]).then_inc(rows_stored, 16)
        for br in range(3):
            sp.dma_start(GSM[:, br:br + 1], GNS[:, NH * br:NH * br + NH]).then_inc(gates_moved, 16)
    ROWS_STORED = 16 * (4 + 4 + 2 * TS)
    NAT_STORED = 16 * 4

    def shift_sp(sp):
        for k, n in enumerate(("state_win_k", "state_win_v")):
            o = out[("win_k", "win_v")[k] + "_sample"]
            sp.dma_start(o[:, 0:WIN - 1].rearrange("b w g d -> b (w g d)"), io[n][:, 1:WIN].rearrange("b w g d -> b (w g d)")).then_inc(shift_stored, 16)
    SHIFT_STORED = 32

    pc_pe = Steps("pc_pe", ["k hidden", "v hidden", "k second", "v second"])
    pc_act = Steps("pc_act", ["k gelu", "v gelu", "v rows"])
    pc_dve = Steps("pc_dve", ["k cos", "k rows"])
    NPC = G * NCMPP

    def prompt_cmp_pe(pe):
        pe.wait_ge(nt_used, NT_JOBS)
        pe.wait_ge(ld_taps, L_TAPS)
        for kv, taps in enumerate((W1P, W1Q)):
            rows = KVT[:, kv, :, 0:TP].rearrange("p g (n s) -> p s g n", s=STRIDE)
            for t in range(TAPS):
                j, s = divmod(t, STRIDE)
                last = nc.tensor.matmul(PSUM[:, 1 + kv, 0:NPC], taps[:, t, :], rows[:, s, :, j:j + NCMPP],
                                        start=t == 0, stop=t == TAPS - 1)
            pc_pe.made_by(last, "kv"[kv] + " hidden")
        pc_act.wait(pe, "k gelu")
        for k in range(2):
            last = nc.tensor.matmul(PSUM[:, 3, 64 * k:64 * k + NPC], W2P[:, k, :], GEP[:, 0, 0:NPC], start=True, stop=True)
        pc_pe.made_by(last, "k second")
        pc_act.wait(pe, "v gelu")
        for g in range(G):
            last = nc.tensor.matmul(PSUM[0:NCMPP, 4, g * P:(g + 1) * P], GEP[:, 1, g * NCMPP:(g + 1) * NCMPP], W2P[:, 2, :], start=True, stop=True)
        pc_pe.made_by(last, "v second")

    def prompt_cmp_act(act):
        for kv in range(2):
            pc_pe.wait(act, "kv"[kv] + " hidden")
            pc_act.made_by(nc.scalar.activation(GEP[:, kv, 0:NPC], PSUM[:, 1 + kv, 0:NPC], ACT.Gelu_apprx_tanh,
                                                bias=GW[:, 48 + kv:49 + kv]), "kv"[kv] + " gelu")
        pc_pe.wait(act, "v second")
        pc_act.made_by(nc.scalar.activation(VCP[0:NCMPP, :, :].rearrange("p g d -> p (g d)"), PSUM[0:NCMPP, 4, :], ACT.Copy), "v rows")

    def prompt_cmp_dve(dve):
        pc_pe.wait(dve, "k second")
        dve.wait_ge(ld_masks, L_MASKS)
        V.tensor_tensor(RTP[:, 0:NPC], PSUM[:, 3, 64:64 + NPC], ROPP[:, 1, :], ALU.mult)
        pc_dve.made_by(V.tensor_tensor(KCP[:, 0:NPC], PSUM[:, 3, 0:NPC], ROPP[:, 0, :], ALU.mult), "k cos")
        pc_dve.wait(dve, "k cos")
        pc_dve.made_by(V.tensor_tensor(KCP[:, 0:NPC], KCP[:, 0:NPC], RTP[:, 0:NPC], ALU.add), "k rows")

    ITEMS = [(qt, g, br) for qt in range(2) for g in range(G) for br in range(3)]
    sc_done, sc_used, mx_done, nm_done, ex_done, vis_done, rs_done, rc_done, fg_done, pr_done = (
        sem("ap_" + n) for n in ("scores", "scores_used", "max", "negmax", "exp", "visible", "sum", "recip", "factor", "probs"))
    pt_done, pt_taken, pv_done, po_used = (sem("ap_" + n) for n in ("t_done", "t_taken", "pv", "out_used"))

    def keys_of(item):
        qt, g, br = item
        return NCMPP if br == 0 else P * (qt + 1)

    def score_banks(k):
        return PSUM[:, 2 * (k % 2):2 * (k % 2) + 2, :].rearrange("p b (r n) -> p (b r) n", r=2)

    def prompt_scores_pe(pe, k):
        qt, g, br = item = ITEMS[k]
        if k >= 2:
            pe.wait_ge(sc_used, k - 1)
        for r in range(HREP):
            keys = KCP[:, g * NCMPP:(g + 1) * NCMPP] if br == 0 else KVT[:, 2 * br, g, 0:keys_of(item)]
            last = nc.tensor.matmul(score_banks(k)[:, r, 0:keys_of(item)], QT[:, HREP * g + r, qt * P:(qt + 1) * P], keys, start=True, stop=True)
        last.then_inc(sc_done, 1)

    def prompt_att_pe(pe):
        pc_dve.wait(pe, "k rows")
        pc_act.wait(pe, "v rows")
        prompt_scores_pe(pe, 0)
        for k, item in enumerate(ITEMS):
            if k + 1 < len(ITEMS):
                prompt_scores_pe(pe, k + 1)
            qt, g, br = item
            n = keys_of(item)
            parts = [(kc, min(P, n - kc * P)) for kc in range(-(-n // P))]
            pe.wait_ge(pr_done, k + 1)
            if k >= 1:
                pe.wait_ge(pt_taken, k)
            for kc, w in parts:
                for r in range(HREP):
                    last = nc.tensor.transpose(PSUM[0:w, 4 + kc, r * P:(r + 1) * P], SP2[:, k % 2, r, kc * P:kc * P + w], IDENT[:, :])
            last.then_inc(pt_done, 1)
            pe.wait_ge(pt_taken, k + 1)
            o = k // 3
            if br == 0 and o >= 2:
                pe.wait_ge(po_used, o - 1)
            for kc, w in parts:
                v = VCP[0:w, g, :] if br == 0 else VNAT[0:w, br - 1, kc, g * DH:(g + 1) * DH]
                last = nc.tensor.matmul(PSUM[:, 6 + o % 2, :], v, PTP[0:w, k % 2, kc, :], start=br == 0 and kc == 0,
                                        stop=br == 2 and kc == len(parts) - 1)
            last.then_inc(pv_done, 1)

    def prompt_mask_dve(dve, k):
        qt, g, br = item = ITEMS[k]
        n = keys_of(item)
        s = SP2[:, k % 2, :, 0:n]
        mask = CMPV[:, qt, :] if br == 0 else CAUS[:, qt, 0:n]
        dve.wait_ge(sc_done, k + 1)
        if k >= 2:
            dve.wait_ge(pt_done, k - 1)
        V.tensor_tensor(s, score_banks(k)[:, :, 0:n], mask.unsqueeze(1).to_broadcast([P, HREP, n]), ALU.add).then_inc(sc_used, 1)
        dve.wait_ge(sc_used, k + 1)
        V.tensor_reduce(SM[:, 16 * (k % 2):16 * (k % 2) + 4], s, AX.X, ALU.max).then_inc(mx_done, 1)
        dve.wait_ge(mx_done, k + 1)
        V.tensor_scalar(SM[:, 16 * (k % 2) + 4:16 * (k % 2) + 8], SM[:, 16 * (k % 2):16 * (k % 2) + 4], -1e20, -SCALE, ALU.max, ALU.mult).then_inc(nm_done, 1)

    def prompt_att_dve(dve):
        dve.wait_ge(ld_masks, L_MASKS)
        prompt_mask_dve(dve, 0)
        for k, item in enumerate(ITEMS):
            qt, g, br = item
            n = keys_of(item)
            if k + 1 < len(ITEMS):
                prompt_mask_dve(dve, k + 1)
            s = SP2[:, k % 2, :, 0:n]
            at = 16 * (k % 2)
            dve.wait_ge(ex_done, 4 * k + 4)
            if br == 0:
                vis = CMPV[:, 2 + qt, :].unsqueeze(1).to_broadcast([P, HREP, n])
                V.tensor_tensor(s, s, vis, ALU.mult).then_inc(vis_done, 1)
                dve.wait_ge(vis_done, k // 3 + 1)
                V.tensor_reduce(SM[:, at + 8:at + 12], s, AX.X, ALU.add).then_inc(rs_done, 1)
                dve.wait_ge(rs_done, k // 3 + 1)
            V.tensor_scalar(SM[:, at:at + 4], SM[:, at + 8:at + 12], 1e-30, None, ALU.max).then_inc(rc_done, 1)
            dve.wait_ge(rc_done, 2 * k + 1)
            V.reciprocal(SM[:, at:at + 4], SM[:, at:at + 4]).then_inc(rc_done, 1)
            dve.wait_ge(rc_done, 2 * k + 2)
            h = NH * br + HREP * g
            V.tensor_tensor(SM[:, at + 12:at + 16], SM[:, at:at + 4], GN[:, qt, h:h + 4], ALU.mult).then_inc(fg_done, 1)
            dve.wait_ge(fg_done, k + 1)
            V.tensor_tensor(s, s, SM[:, at + 12:at + 16].unsqueeze(2).to_broadcast([P, HREP, n]), ALU.mult).then_inc(pr_done, 1)
            if br == 2 and k >= 5:
                prompt_out_dve(dve, k // 3 - 1)
        prompt_out_dve(dve, len(ITEMS) // 3 - 1)

    def prompt_out_dve(dve, o):
        qt, g, _ = ITEMS[3 * o]
        dve.wait_ge(pv_done, 3 * o + 3)
        V.tensor_copy(QT[:, HREP * g:HREP * g + 4, qt * P:(qt + 1) * P], PSUM[:, 6 + o % 2, :].rearrange("p (r t) -> p r t", r=4)).then_inc(po_used, 1)

    def prompt_exp_act(act, k):
        qt, g, br = item = ITEMS[k]
        n = keys_of(item)
        act.wait_ge(nm_done, k + 1)
        for r in range(HREP):
            s = SP2[:, k % 2, r, 0:n]
            at = 16 * (k % 2)
            nc.scalar.activation(s, s, ACT.Exp, scale=SCALE, bias=SM[:, at + 4 + r:at + 5 + r],
                                 accum_out=SM[:, at + 8 + r:at + 9 + r]).then_inc(ex_done, 1)

    def prompt_att_act(act):
        prompt_exp_act(act, 0)
        for k, item in enumerate(ITEMS):
            if k + 1 < len(ITEMS):
                prompt_exp_act(act, k + 1)
            n = keys_of(item)
            act.wait_ge(pt_done, k + 1)
            if k >= 2:
                act.wait_ge(pv_done, k - 1)
            w, m = min(n, P), -(-n // P)
            nc.scalar.activation(PTP[0:w, k % 2, 0:m, :], PSUM[0:w, 4:4 + m, :], ACT.Copy).then_inc(pt_taken, 1)

    kt_tp, kt_act, kt_dve, ks_done = (sem(n) for n in ("kt_tp", "kt_act", "kt_dve", "ks_done"))
    sp_pe = Steps("sp_pe", ["cmp scores", "cmp rows", "cmp turned", "block scores", "block sums", "cmp gated turned",
                            "slc rows", "win rows", "new turned", "slc turned", "win turned", "cmp out", "new out"])
    sp_act = Steps("sp_act", ["cmp copied", "cmp exp", "cmp turned kept", "block scores kept", "cmp gated kept",
                              "slc copied", "win copied", "slc exp", "slc new exp", "win exp", "win new exp", "slc kept", "win kept"])
    sp_dve = Steps("sp_dve", ["cmp negmax", "cmp probs", "cmp gated", "slc taken", "slc copied", "slc negmax", "win negmax",
                              "slc probs", "win probs", "new probs", "new kept", "slc kept", "out"])
    ch_dve = sem("ch_dve")
    chain = [0]
    N_PAGES = SLC_PAGES + WIN_PAGES

    def key_banks(branch, j):
        return (PSUM[:, 2 + j // 4, :], (j % 4) * P) if branch == "sk" else (PSUM[:, 6, :], (j % 4) * P)

    def key_pages_pe(pe, branch, steps, per):
        base = BRANCH[branch]

        def body(i, first):
            n = lambda j: base + per * i + j

            def turn(j):
                if j % 2 == 0:
                    wait_page(pe, base, i, per, j)
                if not (first and j < 2):
                    pe.wait_ge((kt_act, kt_dve)[j % 2], base // 2 + (per // 2) * i + j // 2)
                for g in range(G):
                    last = nc.tensor.transpose(PSUM[:, j % 2, g * P:(g + 1) * P],
                                               RAW[:, (j // 2) % RING, (j % 2) * 512 + g * DH:(j % 2) * 512 + (g + 1) * DH], IDENT[:, :])
                last.then_inc(att_used, 1)

            def score(j):
                pe.wait_ge((kt_act, kt_dve)[j % 2], base // 2 + (per // 2) * i + j // 2 + 1)
                row, pg = (0, j) if branch == "sk" else divmod(j, 4)
                bank, at = key_banks(branch, pg)
                seq = i if branch == "sk" else 2 * i + row
                for g in range(G):
                    last = nc.tensor.matmul(bank[:, ds(seq * NH + (at + g * HREP), HREP)], KT[:, j % 2, g * P:(g + 1) * P],
                                            QS[:, ds(seq * NH + g * HREP, HREP)], start=True, stop=True)
                last.then_inc(ks_done, 1)

            turn(0)
            for j in range(per):
                if j + 1 < per:
                    turn(j + 1)
                score(j)

        if base == 0:
            body(0, True)
            with pe.Fori(1, steps) as i:
                body(i, False)
        else:
            with pe.Fori(0, steps) as i:
                body(i, False)

    def key_pages_evac(eng, parity, branch, steps, per):
        base = BRANCH[branch]

        def body(i, first):
            for j in range(parity, per, 2):
                eng.wait_ge(att_used, base + per * i + (j + 1))
                if not (first and j < 2):
                    eng.wait_ge(ks_done, base + per * i + (j - 1))
                if parity == 0:
                    nc.scalar.activation(KT[:, 0, :], PSUM[:, 0, :], ACT.Copy).then_inc(kt_act, 1)
                else:
                    nc.vector.tensor_copy(KT[:, 1, :], PSUM[:, 1, :]).then_inc(kt_dve, 1)

        if base == 0:
            body(0, True)
            with eng.Fori(1, steps) as i:
                body(i, False)
        else:
            with eng.Fori(0, steps) as i:
                body(i, False)

    def value_pages_pe(pe, branch, steps, per):
        base = BRANCH[branch]
        with pe.Fori(0, steps) as i:
            for j in range(per):
                if j % 2 == 0:
                    wait_page(pe, base, i, per, j)
                row, pg = (0, j) if branch == "sv" else divmod(j, 4)
                seq = i if branch == "sv" else 2 * i + row
                probs = SCT if branch == "sv" else STW
                for g in range(G):
                    cols = ds(seq * NH + g * HREP, HREP)
                    last = nc.tensor.matmul(PSUM[:, 7, cols], RAW[:, (j // 2) % RING, (j % 2) * 512 + g * DH:(j % 2) * 512 + (g + 1) * DH],
                                            probs[:, pg, cols], start=False, stop=False, skip_group_check=True)
                last.then_inc(att_used, 1)

    def decode_pe(pe):
        pe.wait_ge(po_used, 2 * G)
        pe.wait_ge(ld_kc, 16)
        pe.wait_ge(new_done, 2)
        for b in range(TS):
            for g in range(G):
                keys = KCS[:, 2 * b + g // 2, :].rearrange("p (n g) -> p g n", g=2)[:, g % 2, :]
                nc.tensor.matmul(PSUM[0:NCMP, 7, b * NH + g * HREP:b * NH + (g + 1) * HREP], keys,
                                 QS[:, b * NH + g * HREP:b * NH + (g + 1) * HREP], start=True, stop=True)
        for k in range(2):
            last = nc.tensor.matmul(PSUM[:, 7, P + 32 * k:P + 32 * k + 32], QS[:, :], KS6[:, 2 + 2 * k, :], start=True, stop=True)
        sp_pe.made_by(last, "cmp scores")
        sp_act.wait(pe, "cmp copied")
        sp_pe.made_by(nc.tensor.transpose(PSUM[:, 0, 0:NCMP], PCS[0:NCMP, 0, :], IDENT[0:NCMP, 0:NCMP]), "cmp rows")
        sp_dve.wait(pe, "cmp probs")
        sp_pe.made_by(nc.tensor.transpose(PSUM[0:NCMP, 1, 0:P], PCS[:, 1, 0:NCMP], IDENT[:, :]), "cmp turned")
        sp_act.wait(pe, "cmp turned kept")
        sp_pe.made_by(nc.tensor.matmul(PSUM[:, 2, 0:30], PCS[0:NCMP, 0, :], TOB[0:NCMP, :], start=True, stop=True), "block scores")
        sp_act.wait(pe, "block scores kept")
        sp_pe.made_by(nc.tensor.matmul(PSUM[:, 3, 0:30], SAME[:, :], SM[:, 32:62], start=True, stop=True), "block sums")
        sp_dve.wait(pe, "cmp gated")
        sp_pe.made_by(nc.tensor.transpose(PSUM[0:NCMP, 1, P:2 * P], PCS[:, 1, 0:NCMP], IDENT[:, :]), "cmp gated turned")
        sp_act.wait(pe, "cmp gated kept")
        sp_dve.wait(pe, "slc taken")
        key_pages_pe(pe, "sk", TS, PAGES)
        key_pages_pe(pe, "wk", TS // 2, 8)
        sp_act.wait(pe, "slc copied")
        sp_dve.wait(pe, "slc copied")
        for j in range(PAGES):
            last = nc.tensor.transpose(PSUM[:, 2 + j // 4, (j % 4) * P:(j % 4 + 1) * P], SCT[:, j, :], IDENT[:, :])
        sp_pe.made_by(last, "slc rows")
        sp_act.wait(pe, "win copied")
        for j in range(4):
            last = nc.tensor.transpose(PSUM[:, 6, j * P:(j + 1) * P], STW[:, j, :], IDENT[:, :])
        sp_pe.made_by(last, "win rows")
        sp_dve.wait(pe, "new probs")
        for k in range(2):
            last = nc.tensor.transpose(PSUM[0:32, 0, k * P:(k + 1) * P], RTW[:, k, :], IDENT[:, :])
        sp_pe.made_by(last, "new turned")
        for j in range(PAGES):
            last = nc.tensor.transpose(PSUM[:, 2 + j // 4, (j % 4) * P:(j % 4 + 1) * P], S2[:, j * P:(j + 1) * P], IDENT[:, :])
        sp_pe.made_by(last, "slc turned")
        for j in range(4):
            last = nc.tensor.transpose(PSUM[:, 6, j * P:(j + 1) * P], S2W[:, j * P:(j + 1) * P], IDENT[:, :])
        sp_pe.made_by(last, "win turned")
        sp_dve.wait(pe, "new kept")
        for k in range(2):
            last = nc.tensor.matmul(PSUM[:, 7, 0:P], SNAT[:, 3 + 2 * k, :], RTK[0:32, k, :], start=k == 0, stop=False, skip_group_check=True)
        pe.wait_ge(ld_vc, 16)
        for b in range(TS):
            for g in range(G):
                cols = slice(b * NH + g * HREP, b * NH + (g + 1) * HREP)
                last = nc.tensor.matmul(PSUM[:, 7, cols], VCS[0:NCMP, 2 * b + g // 2, (g % 2) * DH:(g % 2 + 1) * DH],
                                        PCS[0:NCMP, 2, cols], start=False, stop=False, skip_group_check=True)
        sp_pe.made_by(last, "cmp out")
        sp_act.wait(pe, "slc kept")
        sp_dve.wait(pe, "slc kept")
        value_pages_pe(pe, "sv", TS, PAGES)
        sp_act.wait(pe, "win kept")
        value_pages_pe(pe, "wv", TS // 2, 8)
        sp_pe.made_by(nc.tensor.matmul(PSUM[:, 7, 0:P], ZERO[:, :], QS[:, :], start=False, stop=True, skip_group_check=True), "new out")

    def decode_act(act):
        A = nc.scalar.activation
        sp_pe.wait(act, "cmp scores")
        sp_act.made_by(A(PCS[0:NCMP, 0, :], PSUM[0:NCMP, 7, 0:P], ACT.Copy), "cmp copied")
        sp_dve.wait(act, "cmp negmax")
        sp_act.made_by(A(PCS[:, 1, 0:NCMP], PSUM[:, 0, 0:NCMP], ACT.Exp, scale=SCALE, bias=SM[:, 1:2], accum_out=SM[:, 2:3]), "cmp exp")
        sp_pe.wait(act, "cmp turned")
        sp_act.made_by(A(PCS[0:NCMP, 0, :], PSUM[0:NCMP, 1, 0:P], ACT.Copy), "cmp turned kept")
        sp_pe.wait(act, "block scores")
        sp_act.made_by(A(SM[:, 32:62], PSUM[:, 2, 0:30], ACT.Copy), "block scores kept")
        sp_pe.wait(act, "cmp gated turned")
        sp_act.made_by(A(PCS[0:NCMP, 2, :], PSUM[0:NCMP, 1, P:2 * P], ACT.Copy), "cmp gated kept")
        key_pages_evac(act, 0, "sk", TS, PAGES)
        key_pages_evac(act, 0, "wk", TS // 2, 8)
        act.wait_ge(ks_done, N_PAGES)
        sp_act.made_by(A(SCT[:, 0:8, :].rearrange("p (b j) c -> p b (j c)", b=2), PSUM[:, 2:4, :], ACT.Copy), "slc copied")
        sp_act.made_by(A(STW[:, :, :].rearrange("p j c -> p (j c)"), PSUM[:, 6, :], ACT.Copy), "win copied")
        sp_dve.wait(act, "slc negmax")
        sp_act.made_by(A(S2[:, :], S2[:, :], ACT.Exp, scale=SCALE, bias=SM[:, 5:6], accum_out=SM[:, 6:7]), "slc exp")
        sp_act.made_by(A(SM[:, 24:25], SM[:, 20:21], ACT.Exp, scale=SCALE, bias=SM[:, 5:6]), "slc new exp")
        sp_dve.wait(act, "win negmax")
        sp_act.made_by(A(S2W[:, 1:WIN], S2W[:, 1:WIN], ACT.Exp, scale=SCALE, bias=SM[:, 9:10], accum_out=SM[:, 10:11]), "win exp")
        sp_act.made_by(A(SM[:, 25:26], SM[:, 21:22], ACT.Exp, scale=SCALE, bias=SM[:, 9:10]), "win new exp")
        sp_pe.wait(act, "slc turned")
        sp_act.made_by(A(SCT[:, 0:8, :].rearrange("p (b j) c -> p b (j c)", b=2), PSUM[:, 2:4, :], ACT.Copy), "slc kept")
        sp_pe.wait(act, "win turned")
        sp_act.made_by(A(STW[:, :, :].rearrange("p j c -> p (j c)"), PSUM[:, 6, :], ACT.Copy), "win kept")

    def decode_dve(dve):
        def link(ins):
            chain[0] += 1
            ins.then_inc(ch_dve, 1)
            dve.wait_ge(ch_dve, chain[0])

        dve.wait_ge(po_used, 2 * G)
        dve.wait_ge(gates_moved, 48)
        link(V.memset(ZERO[:, :], 0.0))
        sp_act.wait(dve, "cmp copied")
        for k in range(2):
            link(V.tensor_tensor(RTW[:, k, :], PSUM[:, 7, P + 32 * k:P + 32 * k + 32], BD[:, :], ALU.mult))
            link(V.tensor_reduce(SM[:, 20 + k:21 + k], RTW[:, k, :], AX.X, ALU.add))
        sp_pe.wait(dve, "cmp rows")
        link(V.tensor_reduce(SM[:, 0:1], PSUM[:, 0, 0:NCMP], AX.X, ALU.max))
        sp_dve.made_by(V.tensor_scalar(SM[:, 1:2], SM[:, 0:1], -SCALE, None, ALU.mult), "cmp negmax")
        sp_act.wait(dve, "cmp exp")
        link(V.tensor_scalar(SM[:, 2:3], SM[:, 2:3], 1e-30, None, ALU.max))
        link(V.reciprocal(SM[:, 3:4], SM[:, 2:3]))
        sp_dve.made_by(V.tensor_scalar(PCS[:, 1, 0:NCMP], PCS[:, 1, 0:NCMP], SM[:, 3:4], None, ALU.mult), "cmp probs")
        sp_pe.wait(dve, "cmp turned")
        sp_dve.made_by(V.tensor_scalar(PCS[:, 1, 0:NCMP], PCS[:, 1, 0:NCMP], GSM[:, 0:1], None, ALU.mult), "cmp gated")
        sp_pe.wait(dve, "block sums")
        link(V.tensor_copy(SM[:, 32:62], PSUM[:, 3, 0:30]))
        one = SM[:, 32:62].unsqueeze(2).to_broadcast([P, 30, 30])
        other = SM[:, 32:62].unsqueeze(1).to_broadcast([P, 30, 30])
        link(V.tensor_tensor(RK[:, 0, :, :], other, one, ALU.is_equal))
        link(V.tensor_tensor(RK[:, 0, :, :], RK[:, 0, :, :], EARL[:, :, :], ALU.mult))
        link(V.tensor_tensor(RK[:, 1, :, :], other, one, ALU.is_gt))
        link(V.tensor_tensor(RK[:, 0, :, :], RK[:, 0, :, :], RK[:, 1, :, :], ALU.add))
        link(V.memset(BLK[:, :], 0.0))
        link(V.tensor_reduce(BLK[:, 1:31], RK[:, 0, :, :], AX.X, ALU.add))
        link(V.tensor_scalar(BLK[:, 1:31], BLK[:, 1:31], 12.5, NEG, ALU.is_gt, ALU.mult))
        sp_dve.made_by(V.memset(S2W[:, 0:1], 0.0), "slc taken")
        key_pages_evac(dve, 1, "sk", TS, PAGES)
        key_pages_evac(dve, 1, "wk", TS // 2, 8)
        dve.wait_ge(ks_done, N_PAGES)
        sp_dve.made_by(V.tensor_copy(SCT[:, 8:16, :].rearrange("p (b j) c -> p b (j c)", b=2), PSUM[:, 4:6, :]), "slc copied")
        sp_pe.wait(dve, "slc rows")
        link(V.tensor_tensor(S2[:, :].rearrange("p (b k) -> p b k", k=64), PSUM[:, 2:6, :].rearrange("p b (j k) -> p (b j) k", k=64),
                             BLK[:, :].unsqueeze(2).to_broadcast([P, 32, 64]), ALU.add))
        link(V.tensor_reduce(SM[:, 4:5], S2[:, :], AX.X, ALU.max))
        link(V.tensor_tensor(SM[:, 4:5], SM[:, 4:5], SM[:, 20:21], ALU.max))
        sp_dve.made_by(V.tensor_scalar(SM[:, 5:6], SM[:, 4:5], -SCALE, None, ALU.mult), "slc negmax")
        sp_pe.wait(dve, "win rows")
        link(V.tensor_copy(S2W[:, 1:WIN], PSUM[:, 6, 1:WIN]))
        link(V.tensor_reduce(SM[:, 8:9], S2W[:, 1:WIN], AX.X, ALU.max))
        link(V.tensor_tensor(SM[:, 8:9], SM[:, 8:9], SM[:, 21:22], ALU.max))
        sp_dve.made_by(V.tensor_scalar(SM[:, 9:10], SM[:, 8:9], -SCALE, None, ALU.mult), "win negmax")
        for k, (name, rows, at) in enumerate((("slc", S2[:, :], 6), ("win", S2W[:, 1:WIN], 10))):
            sp_act.wait(dve, name + " new exp")
            link(V.tensor_tensor(SM[:, at:at + 1], SM[:, at:at + 1], SM[:, 24 + k:25 + k], ALU.add))
            link(V.reciprocal(SM[:, at + 1:at + 2], SM[:, at:at + 1]))
            link(V.tensor_tensor(SM[:, at + 1:at + 2], SM[:, at + 1:at + 2], GSM[:, 1 + k:2 + k], ALU.mult))
            link(V.tensor_tensor(SM[:, 24 + k:25 + k], SM[:, 24 + k:25 + k], SM[:, at + 1:at + 2], ALU.mult))
            sp_dve.made_by(V.tensor_scalar(rows, rows, SM[:, at + 1:at + 2], None, ALU.mult), name + " probs")
        link(V.tensor_scalar(RTW[:, 0, :], BD[:, :], SM[:, 24:25], None, ALU.mult))
        sp_dve.made_by(V.tensor_scalar(RTW[:, 1, :], BD[:, :], SM[:, 25:26], None, ALU.mult), "new probs")
        sp_pe.wait(dve, "new turned")
        sp_dve.made_by(V.tensor_copy(RTK[0:32, :, :].rearrange("p k c -> p (k c)"), PSUM[0:32, 0, 0:2 * P]), "new kept")
        sp_pe.wait(dve, "slc turned")
        sp_dve.made_by(V.tensor_copy(SCT[:, 8:16, :].rearrange("p (b j) c -> p b (j c)", b=2), PSUM[:, 4:6, :]), "slc kept")
        sp_pe.wait(dve, "new out")
        sp_dve.made_by(V.tensor_copy(QT[:, :, TP:T].rearrange("p h b -> p b h"), PSUM[:, 7, 0:P].rearrange("p (b h) -> p b h", h=NH)), "out")

    def decode_sp_keys(sp):
        pc_pe.wait(sp, "v hidden")
        sp.dma_start(KCS[:, :, :], kscr.rearrange("b g p n -> p (b g) n")).then_inc(ld_kc, 16)
        cache_pages_sp(sp, "cache_slc_k", "sk")
        window_pages_sp(sp, "state_win_k", "wk")
        sp_pe.wait(sp, "cmp scores")
        sp.dma_start(VCS[0:NCMP, :, :], vscr.rearrange("b g p n -> p (b g) n")).then_inc(ld_vc, 16)
        cache_pages_sp(sp, "cache_slc_v", "sv")
        window_pages_sp(sp, "state_win_v", "wv")

    def out_heads_act(act):
        sp_dve.wait(act, "out")
        for c in range(KC):
            nc.scalar.activation(XH[:, c, :], QT[:, c, :], ACT.Copy).then_inc(xh_done, 1)

    def out_rests_dve(dve):
        for c in range(KC):
            dve.wait_ge(xh_done, XLS["att"] + c + 1)
            V.tensor_tensor(XL[:, c, :], QT[:, c, :], XH[:, c, :].bitcast(F32), ALU.subtract).then_inc(xl_done, 1)

    fin_tp, fin_used = sem("fin_tp"), sem("fin_used")

    def final_pe(pe):
        rms_pe(pe, "fin")
        ph = by_name["ple1"]
        for c in range(KC):
            pe.wait_ge(hn_done, 16 * HNS["fin"] + c + 1)
            if c >= 4:
                pe.wait_ge(fin_used, c - 3)
            bank = c % 4
            for k in range(2):
                nc.tensor.transpose(PSUM[:, bank, k * P:(k + 1) * P], HN[:, c % 4, k * P:(k + 1) * P], IDENT[:, :])
            nc.tensor.transpose(PSUM[0:TS, bank, TP:TP + P], HN[:, c % 4, TP:T], IDENT[:, :]).then_inc(fin_tp, 1)

    def final_dve(dve):
        rms_dve(dve, "fin")

        def gained(c):
            if c >= 4:
                dve.wait_ge(fin_tp, c - 3)
            V.scalar_tensor_tensor(out=HN[:, c % 4, :], in0=X[:, c, :], scalar=GV[:, 16 * NFIN + c:16 * NFIN + c + 1],
                                   in1=RSTD[:, :], op0=ALU.mult, op1=ALU.mult).then_inc(hn_done, 1)

        for c in range(KC):
            gained(c)
            if c >= 1:
                take(dve, c - 1)
        take(dve, KC - 1)

    def take(dve, c):
        dve.wait_ge(fin_tp, c + 1)
        V.tensor_copy(YN[:, :, c * P:(c + 1) * P], PSUM[:, c % 4, 0:TP].rearrange("p (q d) -> p q d", q=2))
        V.tensor_copy(YS[:, c * P:(c + 1) * P], PSUM[0:TS, c % 4, TP:TP + P]).then_inc(fin_used, 1)

    def final_sp(sp):
        y = out["y_prompt"][0].rearrange("(q p) d -> p q d", p=P)
        for h in range(4):
            sl = slice(h * 512, (h + 1) * 512)
            sp.wait_ge(fin_used, 4 * h + 4)
            sp.dma_start(y[:, :, sl], YN[:, :, sl]).then_inc(stored, 16)
        sp.dma_start(out["y_sample"].rearrange("b o d -> (b o) d"), YS[:, :]).then_inc(stored, 16)

    block = stack.enter_context(nc.Block())

    @block.sync
    def _(sp):
        start_sp(sp)
        stage1_sp(sp)
        states_sp(sp)
        phase_sp(sp, "glu", skip=RING)
        ffn_sp(sp, 0)
        before_kv_sp(sp)
        phase_sp(sp, "kv")
        phase_sp(sp, "q")
        phase_sp(sp, "o", only=RING)
        attention_small_sp(sp)
        rows_sp(sp)
        decode_sp_keys(sp)
        sp.wait_ge(att_used, ATT_PAGES)
        phase_sp(sp, "o", skip=RING)
        shift_sp(sp)
        ffn_sp(sp, 1)
        final_sp(sp)
        sp.wait_ge(stored, STATES_STORED + 16 * 5)
        sp.wait_ge(rows_stored, ROWS_STORED)
        for k in range(2):
            sp.wait_ge(nat_stored[k], NAT_STORED)
        sp.wait_ge(shift_stored, SHIFT_STORED)
        sp.wait_ge(cmp_kept, 16 * 4 * NKV)

    @block.tensor
    def _(pe):
        start_pe(pe)
        stage1_pe(pe)
        states_pe(pe)
        phase_pe(pe, "glu", XH, XL, None)
        ffn_pe(pe, 0)
        rms_pe(pe, "kv")
        phase_pe(pe, "kv", XH, XL, normed_ready(pe, "kv"))
        phase_pe(pe, "q", XH, XL, normed_ready(pe, "mix1"))
        rotate_pe(pe)
        prompt_cmp_pe(pe)
        prompt_att_pe(pe)
        decode_pe(pe)
        phase_pe(pe, "o", XH, XL, normed_ready(pe, "att"))
        ffn_pe(pe, 1)
        final_pe(pe)

    @block.scalar
    def _(act):
        start_act(act)
        stage1_act(act)
        glu_act(act)
        ffn_act(act, 0)
        rms_act(act, "kv")
        norm_act(act, "kv")
        keep_groups_act(act, "kv", lambda g: KVT[:, ds(g, 1), :, :].rearrange("p o h t -> p (o h) t"))
        norm_act(act, "mix1", by_name["q"].base - TAP_UNITS)
        keep_groups_act(act, "q", lambda g: QT[:, ds(4 * g, 4), :])
        rotate_act_all(act)
        prompt_cmp_act(act)
        prompt_att_act(act)
        decode_act(act)
        out_heads_act(act)
        add_act(act, "o", True)
        ffn_act(act, 1)
        rms_act(act, "fin")

    @block.vector
    def _(dve):
        start_dve(dve)
        stage1_dve(dve)
        states_dve(dve)
        glu_dve(dve)
        ffn_dve(dve, 0)
        rms_dve(dve, "kv")
        norm_dve(dve, "kv", NKV_GAIN)
        only_split_dve(dve, "kv")
        norm_dve(dve, "mix1", NMIX[1])
        only_split_dve(dve, "q")
        rotate_dve_all(dve)
        prompt_cmp_dve(dve)
        prompt_att_dve(dve)
        decode_dve(dve)
        out_rests_dve(dve)
        add_dve(dve, "o", True)
        ffn_dve(dve, 1)
        final_dve(dve)

    @block.gpsimd
    def _(pool):
        nc.gpsimd.memset(EPSB[:, 2:3], 0.0).then_inc(hl_done, 1)
        stage1_pool(pool)
        ffn_pool(pool, 0)
        ffn_pool(pool, 1)

    stack.close()


_INS = ['x_prompt', 'x_sample', 'state_ssm_re', 'state_ssm_im', 'cache_cmp_k', 'cache_cmp_v', 'cache_slc_k',
        'cache_slc_v', 'state_win_k', 'state_win_v', 'page_table', 'p_prompt', 'p_sample', 'norm_mix_g',
        'norm_ffn_g', 'norm_ple_g', 'norm_kv_g', 'norm_final_g', 'ssm_a_re', 'ssm_a_im', 'ssm_log_dt',
        'ssm_b_re', 'ssm_b_im', 'ssm_c_re', 'ssm_c_im', 'ssm_d', 'ssm_w_glu', 'ssm_b_glu', 'kv_w', 'cmp_k_w1',
        'cmp_k_b1', 'cmp_k_w2', 'cmp_v_w1', 'cmp_v_b1', 'cmp_v_w2', 'nsa_w_q', 'nsa_w_gate', 'nsa_b_gate',
        'nsa_w_o', 'ffn_w_gate', 'ffn_w_up', 'ffn_w_down', 'ple_w_gate', 'ple_w_proj']
_ROWS_P, _ROWS_S = (1, TP, G, DH), (TS, 1, G, DH)
_OUTS = [('y_prompt', (1, TP, D)), ('y_sample', (TS, 1, D)),
         ('ssm_re_prompt', (1, 1, 128, ST)), ('ssm_im_prompt', (1, 1, 128, ST)),
         ('cmp_k_prompt', _ROWS_P), ('cmp_v_prompt', _ROWS_P), ('slc_k_prompt', _ROWS_P), ('slc_v_prompt', _ROWS_P),
         ('win_k_prompt', _ROWS_P), ('win_v_prompt', _ROWS_P),
         ('ssm_re_sample', (1, TS, 128, ST)), ('ssm_im_sample', (1, TS, 128, ST)),
         ('cmp_k_sample', _ROWS_S), ('cmp_v_sample', _ROWS_S), ('slc_k_sample', _ROWS_S), ('slc_v_sample', _ROWS_S),
         ('win_k_sample', (TS, WIN, G, DH)), ('win_v_sample', (TS, WIN, G, DH))]


def kernel(**inputs):
    import numpy as _np
    import concourse.bacc as _bacc
    from concourse.bass_utils import run_bass_kernel_spmd as _run

    nc = _bacc.Bacc("TRN2", target_bir_lowering=False, num_devices=1)
    arrays, io, out = {}, {}, {}

    def add(name, a):
        arrays[f"in_{name}"] = a
        io[name] = nc.dram_tensor(f"in_{name}", a.shape, mybir.dt.from_np(a.dtype), kind="ExternalInput").ap()

    for name in _INS:
        add(name, _np.ascontiguousarray(inputs[name]))
    for name, a in shape_constants().items():
        add("k_" + name, _np.ascontiguousarray(a))
    for name, shape in _OUTS:
        out[name] = nc.dram_tensor(f"out_{name}", shape, F32, kind="ExternalOutput").ap()
    trunk_kernel(nc, io, out)
    r = _run(nc, [arrays], core_ids=[0])
    return tuple(r.results[0][f"out_{name}"] for name, _ in _OUTS)
```

```python
from contextlib import ExitStack

import concourse.bass as bass
import numpy as np
from concourse import mybir

F32, F32R, I32 = mybir.dt.float32, mybir.dt.float32r, mybir.dt.int32
ALU, ACT, AX = mybir.AluOpType, mybir.ActivationFunctionType, mybir.AxisListType
ds = bass.ds

P = 128
D, TP, TS, DEPTH = 2048, 256, 8, 2
T = TP + TS
KC = D // P
FF = 5632
PLE = 256
G, HREP, DH, NH = 4, 4, 128, 16
PAGE, PAGES, POOL, PAST = 128, 16, 160, 2048
GRP, ST = 16, 64
NQ = 64
STRIDE, TAPS = 16, 32
NCMP, NCMPP = PAST // STRIDE - 1, TP // STRIDE - 1
WIN = 512
EPS = 1e-6
SCALE = DH ** -0.5
NEG = -1e30
MAGIC = 12582912.0
INV2PI = float(np.float32(1 / (2 * np.pi)))
TWOPI_A = 6.28125
TWOPI_B = float(np.float32(2 * np.pi - 6.28125))
TWOPI_IN = 6.2831845
HALFPI = float(np.float32(np.pi / 2))
QSTEP = P + HREP
RING = 4
UK = 2
UN = 512
FC1, FC2 = 24, 20
SLOT = UK * UN


def shape_constants():
    f = np.float32
    half = DH // 2
    inv = (f(10000.0) ** (-np.arange(half, dtype=f) / f(half))).astype(f)

    def turn(pos):
        ang = pos.astype(f)[None, :] * inv[:, None]
        c, s = np.cos(ang).astype(f), np.sin(ang).astype(f)
        return np.concatenate([c, c]), np.concatenate([-s, s])

    tok = np.concatenate([np.arange(TP), np.full(TS, PAST)])
    out = {}
    out["ident"] = np.eye(P, dtype=f)
    out["ropet"] = np.stack(turn(tok), 1)
    cmp_pos = np.arange(NCMP) * STRIDE + TAPS - 1
    out["ropec"] = np.stack([np.repeat(a, 2, axis=1) for a in turn(cmp_pos)], 1)
    out["ropep"] = np.stack([np.tile(a[:, :NCMPP], (1, G)) for a in turn(cmp_pos)], 1)
    out["iota"] = np.tile(np.arange(16, dtype=f), (P, 1))
    par = (np.arange(P) // GRP) % 2
    cm = np.zeros((P, 2, 2, ST), f)
    cm[np.arange(P), 0, par], cm[np.arange(P), 1, par] = 1, -1
    out["cmask"] = cm.reshape(P, 2, P)
    t, k = np.arange(P)[:, None], np.arange(TP)[None, :]
    out["causal"] = np.stack([np.where(k <= t, 0, NEG), np.where(k <= t + P, 0, NEG)], 1).astype(f)
    vis = np.stack([(cmp_pos[:NCMPP][None, :] <= t + P * qt) for qt in range(2)], 1)
    out["cmpvis"] = np.concatenate([np.where(vis, 0, NEG), vis], 1).astype(f)
    row = np.arange(P) // HREP
    out["bd"] = (row[:, None] == np.arange(P // HREP)[None, :]).astype(f)
    out["same"] = (row[:, None] == row[None, :]).astype(f)
    m = np.zeros((P, 33), f)
    for n in range(NCMP):
        for j in range(2):
            m[n, (n + j) * STRIDE // 64] += 1
    out["toblk"] = m[:, 1:31].copy()
    lt = np.arange(30)
    out["earlier"] = np.broadcast_to((lt[None, None, :] < lt[None, :, None]), (P, 30, 30)).astype(f).copy()
    return out


class Sbuf:

    def __init__(self, nc, base):
        self.nc, self.at = nc, base

    def __call__(self, name, shape, dtype=F32, at=None):
        size = int(np.prod(shape[1:])) * 4
        size = -(-size // 32) * 32
        where = self.at if at is None else at
        if at is None:
            self.at += size
        assert where + size <= 229344, (name, where + size)
        return self.nc.alloc_sbuf_tensor_at(name, list(shape), dtype, offset=where)


def trunk_kernel(nc, io, out):
    sem_of = {}
    stack = ExitStack()

    def sem(name):
        if name not in sem_of:
            sem_of[name] = stack.enter_context(nc.semaphore(name))
        return sem_of[name]

    sb = Sbuf(nc, 16512)
    X = sb("x_res", [P, KC, T])
    XH = sb("act_head", [P, KC, T], F32R)
    xl_at = sb.at
    XL = sb("act_rest", [P, KC, T], F32R)
    RAW = sb("w_raw", [P, RING, SLOT])
    WH = sb("w_head", [P, RING, SLOT], F32R)
    WL = sb("w_rest", [P, RING, SLOT], F32R)
    PH = sb("ple_head", [P, DEPTH, 2, T], F32R)
    PL = sb("ple_rest", [P, DEPTH, 2, T], F32R)
    HN = sb("normed", [P, 4, T])
    za_at = sb.at
    ZA = sb("gate_val", [P, 4, T])
    zb_at = sb.at
    ZB = sb("prod_val", [P, 4, T])
    ssq_at = sb.at
    SSQ = sb("sumsq", [P, 4, T])
    RT = sb("rms", [P, T])
    RSTD = sb("rstd", [P, T])
    GV = sb("gains_t", [P, P])
    GW = sb("biases_t", [P, 50])
    ONES = sb("ones", [P, P])
    IDENT = sb("ident", [P, P])
    ROPET = sb("ropet", [P, 2, T])
    EPSB = sb("eps_bias", [P, 8])
    PT = sb("page_table", [1, P], I32)
    region = sb.at
    NMIX, NFFN, NPLE, NKV_GAIN, NFIN = (0, 1), (2, 3), (4, 5), 6, 7

    RH = sb("rows_head", [P, TAPS // 2, P, 2], F32R)
    rl_at = sb.at
    RL = sb("rows_rest", [P, TAPS // 2, P, 2], F32R)
    W2K = sb("w2k", [P, 2, P])
    W2V = sb("w2v", [P, P])
    GEL = sb("cmp_hidden", [P, 2 * NCMP])
    CMPO = sb("cmp_out", [P, 2 * P])
    RTMP = sb("rope_tmp", [P, 2 * NCMP])
    ROPC = sb("ropec", [P, 2, 2 * NCMP])
    ARGA = sb("turns_hi", [P, NQ + 2, 16])
    ARGB = sb("turns_lo", [P, NQ + 2, 16])
    PR = sb("ssm_par", [P, 16, NQ])
    W0 = sb("carry_in", [P, 2, NQ, TS])
    fin_at = sb.at
    FIN = sb("ssm_last", [P, 2, NQ, 1 + TS])
    BN = sb("b_raw", [P, 2, 4, GRP])
    CN_ = sb("c_raw", [P, 2, ST])
    BP = sb("b_prod", [P, 4, 4, GRP])
    BPAD = sb("b_pad", [P, 2, P])
    CPAD = sb("c_pad", [P, 2, P])
    BCT = sb("bc_t", [P, 4, P])
    CMASK = sb("cmask", [P, 2, P])
    IOTA = sb("iota16", [P, 16])
    T1 = sb("turns", [P, TP])
    KS = sb("round_s", [P, TP])
    KCR = sb("round_c", [P, TP])
    FS = sb("frac_s", [P, TP])
    FCO = sb("frac_c", [P, TP])
    SN = sb("sin_t", [P, 2, TP], at=ssq_at)
    CS = sb("cos_t", [P, 2, TP], at=ssq_at + 2 * TP * 4)
    XRI = sb("x_ri", [P, 2, 2, T])
    SRI = sb("s_ri", [P, 2, TP])
    M12 = sb("prod_pool", [P, 2, TP], at=za_at)
    N12 = sb("prod_dve", [P, 2, TP], at=za_at + 2 * TP * 4)
    H = sb("state", [P, 2, 2, T], at=za_at + 4 * TP * 4)
    OUTS = sb("states_out", [NQ, 2 * (1 + TS), P], at=region)
    XN = sb("x_nat", [P, 2, D], at=region)
    XS = sb("x_nat_s", [TS, D], at=rl_at)
    PN = sb("p_nat", [P, DEPTH, 2, PLE], at=rl_at + 8192)
    PS_ = sb("p_nat_s", [TS, DEPTH, PLE], at=rl_at + 12288)
    VEC = sb("vec_nat", [P, 2, P], at=rl_at + 14336)
    AN = sb("a_nat", [NQ, 3, P], at=xl_at)
    LD = sb("logdt_nat", [NQ, 2], at=xl_at + 1536)
    S0 = sb("s0_nat", [P, 2, 4, P], at=xl_at + 2048)
    H0 = sb("s0_t", [P, 2, NQ, TS], at=fin_at)
    PTMP = sb("par_tmp", [P, 4, NQ * 16], at=xl_at)
    PSF = sb("par_small", [P, 8, NQ], at=region)

    HH = sb("hid_head", [P, FC1, T], F32R, at=region)
    HL = sb("hid_rest", [P, FC1, T], F32R, at=region + FC1 * T * 4)

    att_at = region + 6 * 4 * T * 4 + KC * T * 4
    KVT = sb("kv_t", [P, 6, G, T], at=region)
    QT = sb("q_t", [P, NH, T], at=region + 6 * 4 * T * 4)
    sb.at = att_at
    VNAT = sb("v_rows", [P, 2, 2, G * DH])
    KCP = sb("k_cmp_p", [P, 64])
    VCP = sb("v_cmp_p", [16, G, DH])
    KS6 = sb("new_t", [P, 6, TS * G])
    SNAT = sb("new_rows", [TS * G, 6, DH])
    GT = sb("gates_t", [P, T])
    GN = sb("gates_rows", [P, 2, 48])
    GNS = sb("gates_rows_s", [TS, 48])
    GSM = sb("gates_s", [P, 8])
    QS = sb("q_s", [P, P])
    SWAP = sb("swap_halves", [P, P])
    BGATE = sb("b_gate", [P, 8])
    SM = sb("soft_small", [P, 64])
    scratch = sb.at
    WGR = sb("wg_raw", [P, KC, 48])
    WGH = sb("wg_head", [P, KC, P], F32R)
    WGL = sb("wg_rest", [P, KC, P], F32R)
    sb.at = scratch
    W1P = sb("taps_p", [P, TAPS, P])
    W2P = sb("w2_p", [P, 3, P])
    GEP = sb("hid_p", [P, 2, 64])
    RTP = sb("rope_p", [P, 64])
    sb.at = scratch
    SP2 = sb("scores_p", [P, 2, HREP, TP])
    PTP = sb("probs_t_p", [P, 2, 2, HREP * P])
    sb.at = scratch
    S2 = sb("scores_s", [P, PAST])
    SCT = sb("scores_st", [P, PAGES, P])
    PRL = sb("probs_seq", [P, 2, PAGES, NH])
    DACC = sb("decode_out", [P, P])
    KT = sb("k_t", [P, 2, G * P], at=zb_at)
    VO = sb("v_out", [NH, 2, G * DH], at=zb_at)
    QPAD = sb("q_spread", [P, 2, G * QSTEP + TS * NH], at=zb_at + 4096)
    NAT = sb("rows_out", [P, 2, G * DH], at=za_at)
    at = sb.at
    sb.at = 16512 + KC * T * 4
    CAUS = sb("causal", [P, 2, TP])
    CMPV = sb("cmpvis", [P, 4, NCMPP])
    ROPP = sb("ropep", [P, 2, G * NCMPP])
    BD = sb("own_head", [P, TS * G])
    SAME = sb("same_group", [P, P])
    TOB = sb("to_block", [P, 30])
    EARL = sb("earlier", [P, 30, 30])
    S2W = sb("scores_w", [P, WIN])
    STW = sb("scores_wt", [P, 4, P])
    PCS = sb("cmp_probs", [P, 3, P])
    assert sb.at <= xl_at
    W1Q = sb("taps_v", [P, TAPS, P], at=xl_at)
    KCS = sb("cmp_rows", [P, TS * 2, 2 * NCMP], at=xl_at)
    RTW = sb("new_scores", [P, 2, TS * G], at=region + 8192)
    RTK = sb("new_probs_t", [32, 2, P], at=region + 4 * T * 4 * 3)
    ZERO = sb("zeros", [P, P], at=region + 4 * T * 4 * 3 + 1024)
    BLK = sb("block_mask", [P, 32], at=region + 4 * T * 4 * 3 + 1536)
    YN = sb("y_rows", [P, 2, D], at=region)
    YS = sb("y_rows_s", [TS, D], at=region + 2 * D * 4)
    VCS = sb("cmp_rows_v", [P, TS * 2, 2 * P], at=xl_at)
    RK = sb("rank_pairs", [P, 2, 30, 30], at=region)
    sb.at = at

    PSUM = stack.enter_context(nc.psum_tensor("psum", [P, 8, 512], F32))
    kscr = nc.dram_tensor("cmp_k_scratch", [TS, 2, P, 2 * NCMP], F32).ap()
    vscr = nc.dram_tensor("cmp_v_scratch", [TS, 2, NCMP, 2 * P], F32).ap()

    class Phase:

        def __init__(self, name, steps, ka, kb, unrolled=False):
            self.name, self.steps, self.ka, self.kb, self.unrolled = name, steps, ka, kb, unrolled
            self.per = ka + kb

    phases = [Phase("glu", 4, 8, 8)]

    def layer_tail(l):
        return [Phase(f"gu1{l}", FC1 // 4, 8, 8), Phase(f"dn1{l}", 2, FC1 // 2, FC1 // 2),
                Phase(f"gu2{l}", FC2 // 4, 8, 8), Phase(f"dn2{l}", 2, FC2 // 2, FC2 // 2),
                Phase(f"ple{l}", 4, 8, 1, True)]

    phases += layer_tail(0) + [Phase("kv", 3, 8, 8), Phase("q", 2, 8, 8), Phase("o", 2, 8, 8)] + layer_tail(1)
    TAP_UNITS = 2 * RING
    s, ngr = TAP_UNITS, 0
    for ph in phases:
        ph.base, ph.groups = s, ngr
        s += ph.per * ph.steps
        ngr += ph.steps
    NUNITS = s
    by_name = {ph.name: ph for ph in phases}
    nsq = 4
    for ph in phases:
        ph.sq = nsq
        if ph.name in ("glu", "o") or ph.name[:3] in ("dn2", "ple"):
            nsq += 4

    def steps_of(ph, eng, body):
        if ph.unrolled:
            for i in range(ph.steps):
                body(i)
        else:
            with eng.Fori(0, ph.steps) as i:
                body(i)

    class Unit:

        def __init__(self, base, per=0, i=0, c=0):
            if isinstance(i, int):
                n = base + per * i + c
                self.n, self.slot, self.turn = n, n % RING, n // RING + 1
            else:
                self.n, self.slot = per * i + (base + c), (base + c) % RING
                self.turn = (per // RING) * i + ((base + c) // RING + 1)
            self.known = isinstance(i, int)

    raw_ready = [sem(f"raw_ready{k}") for k in range(RING)]
    units_used, head_done, rest_done = sem("units_used"), sem("head_done"), sem("rest_done")
    free_a, free_b = sem("free_a"), sem("free_b")
    x_done, sq_done, ssq_done = sem("x_done"), sem("sq_done"), sem("ssq_done")
    norm_sum, rt_done, rstd_done = sem("norm_sum"), sem("rt_done"), sem("rstd_done")
    hn_done, xh_done, xl_done = sem("hn_done"), sem("xh_done"), sem("xl_done")
    glu_sig, prod_done, hh_done, hl_done = (sem(n) for n in ("glu_sig", "prod_done", "hh_done", "hl_done"))
    tp_done, tp_evac = sem("tp_done"), sem("tp_evac")
    ld = {n: sem("ld_" + n) for n in ("const", "vec", "x", "ssm", "p", "late")}
    ph_done, par_act, par_dve = sem("ph_done"), sem("par_act"), sem("par_dve")
    page_ready = [sem(f"page_ready{k}") for k in range(RING)]
    bc_loaded, bc_ready, bct_tp, bct_done = (sem(n) for n in ("bc_loaded", "bc_ready", "bct_tp", "bct_done"))
    cmp_tp, cmp_head, cmp_rest, cmp_acc, cmp_gelu, cmp_mm2, cmp_out, cmp_kept, rope_part = (
        sem(n) for n in ("cmp_tp", "cmp_head", "cmp_rest", "cmp_acc", "cmp_gelu", "cmp_mm2", "cmp_out", "cmp_kept", "rope_part"))
    pool_t1, dve_ks, dve_kc, dve_fc, pool_fs, act_tab = (sem(n) for n in ("pool_t1", "dve_ks", "dve_kc", "dve_fc", "pool_fs", "act_tab"))
    hn_chunk, pe_bu, act_x, pool_rot, dve_n, dve_rot, dve_scan, pool_der, dve_n2, dve_h, pe_y, pool_fin = (
        sem(n) for n in ("hn_chunk", "pe_bu", "act_x", "pool_rot", "dve_n", "dve_rot", "dve_scan", "pool_der", "dve_n2", "dve_h", "pe_y", "pool_fin"))
    y_sum, y_gelu, b_prod, arg_ready, stored = (sem(n) for n in ("y_sum", "y_gelu", "b_prod", "arg_ready", "stored"))

    def load_unit(sp, u, src, first=False):
        if not (u.known and u.n < RING) and not first:
            sp.wait_ge(rest_done, u.n - (RING - 1))
        sp.dma_start(RAW[:, u.slot, :].rearrange("p (k n) -> p k n", k=src.shape[1]), src).then_inc(raw_ready[u.slot], 16)

    def split_head(act, u):
        act.wait_ge(raw_ready[u.slot], 16 * u.turn)
        if not (u.known and u.n < TAP_UNITS + RING):
            act.wait_ge(units_used, u.n - (RING - 1) - TAP_UNITS)
        nc.scalar.activation(WH[:, u.slot, :], RAW[:, u.slot, :], ACT.Copy).then_inc(head_done, 1)

    def split_rest(dve, u):
        dve.wait_ge(head_done, u.n + 1)
        nc.vector.tensor_tensor(WL[:, u.slot, :], RAW[:, u.slot, :], WH[:, u.slot, :].bitcast(F32),
                                ALU.subtract).then_inc(rest_done, 1)

    def group_matmuls(pe, ph, i, c0, kunits, bank, heads, rests, ready):
        for ku in range(kunits):
            u = Unit(ph.base, ph.per, i, c0 + ku)
            pe.wait_ge(rest_done, u.n + 1)
            for kk in range(UK):
                k = UK * ku + kk
                if ready is not None:
                    ready(k)
                for n in range(4):
                    w = slice(kk * UN + n * P, kk * UN + (n + 1) * P)
                    o = PSUM[:, bank + n, 0:T]
                    nc.tensor.matmul(o, WH[:, u.slot, w], heads[:, k, :], start=k == 0, stop=False)
                    nc.tensor.matmul(o, WH[:, u.slot, w], rests[:, k, :], start=False, stop=False)
                    last = nc.tensor.matmul(o, WL[:, u.slot, w], heads[:, k, :], start=False,
                                            stop=k == UK * kunits - 1)
            last.then_inc(units_used, 1)

    NORMS = {"mix0": 0, "ffn0": 1, "ple0": 2, "kv": 3, "ffn1": 4, "ple1": 5, "fin": 6}
    HNS = {"ffn0": 0, "ple0": 1, "kv": 2, "mix1": 3, "ffn1": 4, "ple1": 5, "fin": 6}
    XLS = {"ffn0": 16, "ple0": 32, "kv": 48, "mix1": 64, "att": 80, "ffn1": 96, "ple1": 112}

    NEXT_PHASE = {"ffn0": "gu10", "ple0": "ple0", "kv": "kv", "ffn1": "gu11", "ple1": "ple1"}

    def norm_bank(name):
        return PSUM[:, 4 if name == "mix0" else 0, 0:T]

    def rms_pe(pe, name):
        k = NORMS[name]
        if name != "mix0":
            pe.wait_ge(free_a, by_name[NEXT_PHASE[name]].groups if name in NEXT_PHASE else ngr)
        for j in range(4):
            pe.wait_ge(ssq_done, 4 * k + j + 1)
            last = nc.tensor.matmul(norm_bank(name), ONES[:, :], SSQ[:, j, :], start=j == 0, stop=j == 3)
        last.then_inc(norm_sum, 1)

    def rms_act(act, name):
        k = NORMS[name]
        nc.scalar.activation(EPSB[:, 3:4], EPSB[:, 0:1], ACT.Sqrt)
        act.wait_ge(norm_sum, k + 1)
        nc.scalar.activation(RT[:, :], norm_bank(name), ACT.Sqrt, scale=1.0 / D, bias=EPSB[:, 0:1]).then_inc(rt_done, 1)

    def rms_dve(dve, name):
        k = NORMS[name]
        dve.wait_ge(rt_done, k + 1)
        nc.vector.reciprocal(RSTD[:, :], RT[:, :]).then_inc(rstd_done, 1)
        dve.wait_ge(rstd_done, k + 1)

    def norm_act(act, name, used=None):
        n = 16 * HNS[name]
        if used is not None:
            act.wait_ge(units_used, used)
        for c in range(KC):
            act.wait_ge(hn_done, n + c + 1)
            nc.scalar.activation(XH[:, c, :], HN[:, c % 4, :], ACT.Copy).then_inc(xh_done, 1)

    def norm_dve(dve, name, gain):
        m = XLS.get(name)

        def rest(c):
            dve.wait_ge(xh_done, m + c + 1)
            nc.vector.tensor_tensor(XL[:, c, :], HN[:, c % 4, :], XH[:, c, :].bitcast(F32),
                                    ALU.subtract).then_inc(xl_done, 1)

        for c in range(KC):
            if c >= 4:
                dve.wait_ge(xl_done, m + c - 3)
            nc.vector.scalar_tensor_tensor(out=HN[:, c % 4, :], in0=X[:, c, :], scalar=GV[:, 16 * gain + c:16 * gain + c + 1],
                                           in1=RSTD[:, :], op0=ALU.mult, op1=ALU.mult).then_inc(hn_done, 1)
            if c >= 1:
                rest(c - 1)
        rest(KC - 1)

    def normed_ready(pe, name):
        return lambda k: pe.wait_ge(xl_done, XLS[name] + k + 1)

    def square_act(act, k, chunks, done, count):
        act.wait_ge(done, count)
        act.wait_ge(ssq_done, k)
        nc.scalar.activation(HN[:, :, :], X[:, chunks, :], ACT.Square).then_inc(sq_done, 1)

    def square_dve(dve, k, dst):
        dve.wait_ge(sq_done, k + 1)
        nc.vector.tensor_reduce(dst if len(dst.shape) == 2 else dst.rearrange("p o t -> p (o t)"), HN[:, :, :].rearrange("p c t -> p t c"), AX.X, ALU.add).then_inc(ssq_done, 1)

    def weight(name, i, half):
        def cols(w, at, rows=None):
            w = w if rows is None else w[rows]
            return w.rearrange("(k p) n -> p k n", p=P)[:, :, ds(at, UN)]
        l = int(name[-1]) if name[-1] in "01" else 0
        if name == "glu":
            return cols(io["ssm_w_glu"][0], i * UN + half * D)
        if name[:2] == "gu":
            at = (FC1 * P if name[2] == "2" else 0)
            return cols(io["ffn_w_up" if half else "ffn_w_gate"][l], i * UN + at)
        if name[:2] == "dn":
            rows = slice(0, FC1 * P) if name[2] == "1" else slice(FC1 * P, FF)
            return cols(io["ffn_w_down"][l], i * (2 * UN) + half * UN, rows)
        if name[:3] == "ple":
            return cols(io["ple_w_proj" if half else "ple_w_gate"][l], i * UN)
        w = {"kv": io["kv_w"], "q": io["nsa_w_q"][0], "o": io["nsa_w_o"][0]}[name]
        return cols(w, i * (2 * UN) + half * UN)

    def phase_sp(sp, name, skip=0, only=None):
        ph = by_name[name]
        if only is not None:
            for c in range(only):
                load_unit(sp, Unit(ph.base, ph.per, 0, c), weight(name, 0, 0)[:, UK * c:UK * (c + 1), :])
            return

        def body(i):
            for half, kn, c0 in ((0, ph.ka, 0), (1, ph.kb, ph.ka)):
                src = weight(name, i, half)
                for ku in range(kn):
                    if isinstance(i, int) and i == 0 and c0 + ku < skip:
                        continue
                    load_unit(sp, Unit(ph.base, ph.per, i, c0 + ku), src[:, UK * ku:UK * (ku + 1), :])

        if skip:
            body(0)
            with sp.Fori(1, ph.steps) as i:
                body(i)
        else:
            steps_of(ph, sp, body)

    def phase_pe(pe, name, heads, rests, ready, heads_b=None, rests_b=None):
        ph = by_name[name]

        def body(i, wait=True):
            if wait:
                pe.wait_ge(free_a, i + ph.groups)
            group_matmuls(pe, ph, i, 0, ph.ka, 0, heads, rests, ready)
            if wait:
                pe.wait_ge(free_b, i + ph.groups)
            group_matmuls(pe, ph, i, ph.ka, ph.kb, 4, heads_b or heads, rests_b or rests, None)

        if ph.groups == 0:
            body(0, False)
            with pe.Fori(1, ph.steps) as i:
                body(i)
        else:
            steps_of(ph, pe, body)

    def after_units(eng, name, split, evac_a, evac_b):
        ph = by_name[name]

        def body(i):
            for c in range(ph.per):
                u = Unit(ph.base, ph.per, i, c)
                if c == ph.ka - 1:
                    eng.wait_ge(units_used, u.n + 1 - TAP_UNITS)
                    evac_a(i)
                if c == ph.per - 1:
                    eng.wait_ge(units_used, u.n + 1 - TAP_UNITS)
                    evac_b(i)
                if not (u.known and u.n + RING >= NUNITS):
                    split(eng, Unit(ph.base + RING, ph.per, i, c))

        steps_of(ph, eng, body)

    nothing = lambda i: None
    A4, B4 = PSUM[:, 0:4, 0:T], PSUM[:, 4:8, 0:T]

    def four(t, g):
        return t[:, ds(4 * g, 4), :] if not isinstance(g, int) else t[:, 4 * g:4 * g + 4, :]

    NKV = TS
    caches = [io["cache_cmp_k"], io["cache_cmp_v"]]
    cache_views = [c.rearrange("n r g d -> n r (g d)") for c in caches]
    w1 = [io["cmp_k_w1"], io["cmp_v_w1"]]
    L_CONST = 16 * 2
    L_VEC = 16 * 9
    L_SSM = 16 * 5
    L_LATE = 16 * 8

    def start_sp(sp):
        def rows(x, n):
            return x.rearrange("(c p) -> c p", p=P) if n == 1 else x.rearrange("l (c p) -> (l c) p", p=P)
        sp.dma_start(IDENT[:, :], io["k_ident"]).then_inc(ld["const"], 16)
        sp.dma_start(ROPET[:, :, :], io["k_ropet"]).then_inc(ld["const"], 16)
        for name, at in (("norm_mix_g", 0), ("norm_ffn_g", 32), ("norm_ple_g", 64)):
            sp.dma_start(VEC[at:at + 32, 0, :], rows(io[name], 2)).then_inc(ld["vec"], 16)
        for name, at in (("norm_kv_g", 96), ("norm_final_g", 112)):
            sp.dma_start(VEC[at:at + 16, 0, :], rows(io[name], 1)).then_inc(ld["vec"], 16)
        for name, at, n in (("ssm_d", 0, 16), ("ssm_b_glu", 16, 32)):
            sp.dma_start(VEC[at:at + n, 1, :], rows(io[name], 2)).then_inc(ld["vec"], 16)
        for name, at in (("cmp_k_b1", 48), ("cmp_v_b1", 49)):
            sp.dma_start(VEC[at:at + 1, 1, :], io[name].rearrange("(a p) -> a p", a=1)).then_inc(ld["vec"], 16)
        sp.dma_start(XN[:, :, :], io["x_prompt"][0].rearrange("(q p) d -> p q d", p=P)).then_inc(ld["x"], 16)
        sp.dma_start(XS[:, :], io["x_sample"].rearrange("b o d -> (b o) d")).then_inc(ld["x"], 16)
        for k, name in enumerate(("ssm_a_re", "ssm_a_im")):
            sp.dma_start(AN[:, k, :], io[name][0].rearrange("(q e) p -> q (e p)", e=2)).then_inc(ld["ssm"], 16)
        sp.dma_start(LD[:, :], io["ssm_log_dt"][0].rearrange("(q e) -> q e", e=2)).then_inc(ld["ssm"], 16)
        for k, name in enumerate(("state_ssm_re", "state_ssm_im")):
            sp.dma_start(S0[:, k, :, :], io[name][0].rearrange("(k b) (q e) p -> (b q) k (e p)", b=2, e=2)).then_inc(ld["ssm"], 16)
        for u in range(RING):
            load_taps(sp, 0, u)
        sp.dma_start(PN[:, :, :, :], io["p_prompt"].rearrange("l o (q p) d -> p l (o q) d", p=P)).then_inc(ld["p"], 16)
        sp.dma_start(PS_[:, :, :], io["p_sample"].rearrange("l b o d -> b l (o d)")).then_inc(ld["p"], 16)
        sp.dma_start(PT[:, :], io["page_table"].rearrange("(o b) n -> o (b n)", o=1)).then_inc(ld["late"], 16)
        sp.dma_start(W2K[:, 0, :], io["cmp_k_w2"]).then_inc(ld["late"], 16)
        sp.dma_start(W2K[:, 1, 0:64], io["cmp_k_w2"][:, 64:128]).then_inc(ld["late"], 16)
        sp.dma_start(W2K[:, 1, 64:128], io["cmp_k_w2"][:, 0:64]).then_inc(ld["late"], 16)
        sp.dma_start(W2V[:, :], io["cmp_v_w2"]).then_inc(ld["late"], 16)
        sp.dma_start(ROPC[:, :, :], io["k_ropec"]).then_inc(ld["late"], 16)
        sp.dma_start(CMASK[:, :, :], io["k_cmask"]).then_inc(ld["late"], 16)
        sp.dma_start(IOTA[:, :], io["k_iota"]).then_inc(ld["late"], 16)

    def load_taps(sp, kv, u):
        load_unit(sp, Unit(RING * kv + u), w1[kv][8 * u:8 * u + 8].rearrange("t d h -> d t h"))

    def body_sp(sp, kv, i, first):
        c = i + NKV * kv
        if not (first and kv == 0):
            sp.wait_ge(bc_ready, c)
        for k, name in enumerate(("ssm_b_re", "ssm_b_im")):
            b = io[name][0].rearrange("(c j e) p h -> c (e p) j h", j=4, e=2)
            sp.dma_start(BN[:, k, :, :], b[ds(c, 1)].rearrange("o s j h -> (o s) j h")).then_inc(bc_loaded, 16)
        for k, name in enumerate(("ssm_c_re", "ssm_c_im")):
            cc = io[name][0].rearrange("(c g) h p -> c (g h) p", g=8)
            sp.dma_start(CN_[:, k, :], cc[ds(c, 1)].rearrange("o s p -> (o s) p")).then_inc(bc_loaded, 16)
        for gp in range(2):
            for u in range(4):
                pages = [sp.value_load(PT[0:1, ds(i * PAGES + (4 * u + k), 1)], min_val=0, max_val=POOL - 1) for k in range(4)]
                if first and gp == 0:
                    sp.wait_ge(rest_done, RING * kv + u + 1)
                else:
                    sp.wait_ge(cmp_tp, 8 * (2 * c + gp - 1) + 2 * u + 2)
                for k, page in enumerate(pages):
                    src = cache_views[kv][ds(page, 1), :, 2 * gp * DH:(2 * gp + 2) * DH]
                    sp.dma_start(RAW[:, u, k * 256:(k + 1) * 256], src.rearrange("o r n -> (o r) n")).then_inc(page_ready[u], 16)

    P0_JOBS = 3 + KC + 2 + 4

    def bank_of(j):
        return PSUM[:, j % 8, :]

    def start_pe(pe):
        j = 0

        def job(ins, wait=None):
            nonlocal j
            if wait:
                pe.wait_ge(*wait)
            if j >= 8:
                pe.wait_ge(tp_evac, j - 7)
            for src, at in ins:
                n, m = src.shape[0], int(np.prod(src.shape[1:]))
                last = nc.tensor.transpose(PSUM[0:m, j % 8, at:at + n], src, IDENT[0:n, 0:n])
            last.then_inc(tp_done, 1)
            j += 1

        pe.wait_ge(ld["const"], L_CONST)
        job([(VEC[:, 0, :], 0)], (ld["vec"], L_VEC))
        job([(VEC[0:50, 1, :], 0)])
        pe.wait_ge(ld["ssm"], L_SSM)
        job([(AN[:, k, :], k * NQ) for k in range(3)], (par_dve, 1))
        pe.wait_ge(ld["x"], 32)
        for c in range(KC):
            sl = slice(c * P, (c + 1) * P)
            job([(XN[:, 0, sl], 0), (XN[:, 1, sl], P), (XS[:, sl], 2 * P)])
        for k in range(2):
            job([(S0[:, k, m, :], m * P) for m in range(4)])
        for l in range(DEPTH):
            for c in range(2):
                sl = slice(c * P, (c + 1) * P)
                job([(PN[:, l, 0, sl], 0), (PN[:, l, 1, sl], P), (PS_[:, l, sl], 2 * P)],
                    (ld["p"], 32) if l == c == 0 else None)

    def start_dve(dve):
        nc.vector.memset(ONES[:, :], 1.0)
        nc.vector.memset(EPSB[:, 0:1], EPS)
        nc.vector.memset(EPSB[:, 1:2], HALFPI)
        nc.vector.memset(ARGA[:, NQ:NQ + 2, :], 0.0)
        nc.vector.memset(ARGB[:, NQ:NQ + 2, :], 0.0)
        nc.vector.memset(BPAD[:, :, :], 0.0)
        dve.wait_ge(ld["ssm"], L_SSM)
        nc.vector.tensor_copy(AN[:, 2, :].rearrange("q (e p) -> q e p", e=2),
                              LD[:, :].unsqueeze(2).to_broadcast([NQ, 2, ST])).then_inc(par_dve, 1)
        j = 0

        def evac(dst, src_cols=None, rows=P):
            nonlocal j
            dve.wait_ge(tp_done, j + 1)
            src = bank_of(j)[0:rows]
            src = src_cols(src)
            nc.vector.tensor_copy(dst, src).then_inc(tp_evac, 1)
            j += 1

        evac(GV[:, :], lambda b: b[:, 0:P])
        evac(GW[:, :], lambda b: b[:, 0:50])
        evac(PR[:, 0:3, :], lambda b: b[:, 0:3 * NQ].rearrange("p (k q) -> p k q", k=3))
        for c in range(KC):
            evac(X[:, c, :], lambda b: b[:, 0:T])
        for u in range(RING):
            split_rest(dve, Unit(u))
        for k in range(2):
            evac(H0[:, k, :, :].rearrange("p q b -> p b q"), lambda b: b[:, :].rearrange("p (b q) -> p b q", q=NQ))
        for l in range(DEPTH):
            for c in range(2):
                evac(ZA[:, 2 * l + c, :], lambda b: b[:, 0:T])
        dve.wait_ge(ph_done, 1)
        dve.wait_ge(tp_evac, P0_JOBS)
        nc.vector.tensor_tensor(PL[:, :, :, :].rearrange("p l c t -> p (l c) t"), ZA[:, :, :],
                                PH[:, :, :, :].rearrange("p l c t -> p (l c) t").bitcast(F32), ALU.subtract).then_inc(ph_done, 1)
        for g in range(4):
            square_dve(dve, g, SSQ[:, g, :])
        rms_dve(dve, "mix0")
        ssm_parameters_dve(dve)

    def start_act(act):
        for u in range(RING):
            split_head(act, Unit(u))
        act.wait_ge(tp_evac, P0_JOBS)
        nc.scalar.activation(PH[:, :, :, :].rearrange("p l c t -> p (l c) t"), ZA[:, :, :], ACT.Copy).then_inc(ph_done, 1)
        for g in range(4):
            if g:
                act.wait_ge(ssq_done, g)
            nc.scalar.activation(HN[:, :, :], X[:, 4 * g:4 * g + 4, :], ACT.Square).then_inc(sq_done, 1)
        rms_act(act, "mix0")
        act.wait_ge(tp_evac, 3)
        nc.scalar.activation(PR[:, 3, :], PR[:, 2, :], ACT.Exp).then_inc(par_act, 1)
        act.wait_ge(par_dve, 2)
        nc.scalar.activation(PR[:, 4, :], PSF[:, 0, :], ACT.Exp).then_inc(par_act, 1)
        act.wait_ge(par_dve, 3)
        nc.scalar.activation(PR[:, 5, :], PSF[:, 4, :], ACT.Sin, scale=TWOPI_IN).then_inc(par_act, 1)
        nc.scalar.activation(PR[:, 6, :], PSF[:, 5, :], ACT.Sin, scale=TWOPI_IN).then_inc(par_act, 1)

    def ssm_parameters_dve(dve):
        V = nc.vector
        n = [0]

        def link(ins):
            n[0] += 1
            ins.then_inc(arg_ready, 1)
            dve.wait_ge(arg_ready, n[0])

        def tt(o, a, b, op):
            link(V.tensor_tensor(o, a, b, op))

        def rounded(o, a, tmp):
            link(V.tensor_scalar(tmp, a, MAGIC, -MAGIC, ALU.add, ALU.add))
            tt(o, a, tmp, ALU.subtract)

        s = lambda k: PSF[:, k, :]
        r = lambda k: PR[:, k, :]
        dve.wait_ge(par_act, 1)
        V.tensor_tensor(s(0), r(3), r(0), ALU.mult).then_inc(par_dve, 1)
        tt(s(1), r(3), r(1), ALU.mult)
        link(V.tensor_scalar(s(2), s(1), INV2PI, MAGIC, ALU.mult, ALU.add))
        link(V.tensor_scalar(s(2), s(2), -MAGIC, None, ALU.add))
        link(V.scalar_tensor_tensor(out=s(3), in0=s(2), scalar=-TWOPI_A, in1=s(1), op0=ALU.mult, op1=ALU.add))
        link(V.scalar_tensor_tensor(out=s(3), in0=s(2), scalar=-TWOPI_B, in1=s(3), op0=ALU.mult, op1=ALU.add))
        link(V.tensor_scalar(s(4), s(3), INV2PI, None, ALU.mult))
        link(V.tensor_scalar(s(4), s(4), 0.5, -0.5, ALU.min, ALU.max))
        link(V.tensor_scalar(s(6), s(4), 0.25, None, ALU.add))
        link(V.tensor_scalar(s(7), s(6), MAGIC, -MAGIC, ALU.add, ALU.add))
        V.tensor_tensor(s(5), s(6), s(7), ALU.subtract).then_inc(par_dve, 1)
        it = IOTA[:, :].unsqueeze(1).to_broadcast([P, NQ, 16])
        dve.wait_ge(ld["late"], L_LATE)
        t0 = PTMP[:, 0, :].rearrange("p (q b) -> p q b", b=16)
        t1 = PTMP[:, 1, :].rearrange("p (q b) -> p q b", b=16)
        tt(t0, s(4).unsqueeze(2).to_broadcast([P, NQ, 16]), it, ALU.mult)
        rounded(ARGB[:, 0:NQ, :], t0, t1)
        link(V.tensor_scalar(s(6), s(4), 16.0, None, ALU.mult))
        rounded(s(1), s(6), s(7))
        tt(t0, s(1).unsqueeze(2).to_broadcast([P, NQ, 16]), it, ALU.mult)
        rounded(ARGA[:, 0:NQ, :], t0, t1)
        dve.wait_ge(par_act, 4)
        tt(r(7), r(4), r(6), ALU.mult)
        tt(r(8), r(4), r(5), ALU.mult)
        link(V.tensor_scalar(s(1), r(7), -1.0, None, ALU.add))
        tt(s(2), r(0), r(0), ALU.mult)
        tt(s(3), r(1), r(1), ALU.mult)
        tt(s(2), s(2), s(3), ALU.add)
        link(V.reciprocal(s(2), s(2)))
        tt(s(3), s(1), r(0), ALU.mult)
        tt(s(6), r(8), r(1), ALU.mult)
        tt(s(3), s(3), s(6), ALU.add)
        tt(r(9), s(3), s(2), ALU.mult)
        tt(s(3), r(8), r(0), ALU.mult)
        tt(s(6), s(1), r(1), ALU.mult)
        tt(s(3), s(3), s(6), ALU.subtract)
        tt(r(10), s(3), s(2), ALU.mult)
        re, im = (r(k).unsqueeze(2).to_broadcast([P, NQ, TS]) for k in (7, 8))
        t2 = PTMP[:, 0, 0:NQ * TS].rearrange("p (q b) -> p q b", b=TS)
        t3 = PTMP[:, 1, 0:NQ * TS].rearrange("p (q b) -> p q b", b=TS)
        tt(t2, re, H0[:, 0, :, :], ALU.mult)
        tt(t3, im, H0[:, 1, :, :], ALU.mult)
        tt(W0[:, 0, :, :], t2, t3, ALU.subtract)
        tt(t2, re, H0[:, 1, :, :], ALU.mult)
        tt(t3, im, H0[:, 0, :, :], ALU.mult)
        tt(W0[:, 1, :, :], t2, t3, ALU.add)
        assert n[0] == N_PAR, n[0]
    N_PAR = 39

    def tile(c, j):
        return 4 * c + j

    TP_BANKS = (0, 1, 7, 0, 1, 0, 1, 0, 1, 0, 7, 1, 0, 7, 1, 0)
    BCT_AT = 4

    def bank_back(m):
        back = [d for d in range(1, 17) if TP_BANKS[(m - d) % 16] == TP_BANKS[m]][0]
        return back

    def page_rows(bank):
        return PSUM[:, bank, :].rearrange("p (g n s) -> p g n s", g=2, s=16)

    def rows_of(tensor, m):
        return tensor[:, :, 16 * m:16 * m + 16, :].rearrange("p s n g -> p g n s")

    def body_pe(pe, kv, i, first, last=False):
        c = i + NKV * kv
        item = lambda gp: 2 * c + gp

        def bct():
            pe.wait_ge(bc_ready, c + 1)
            if not (first and kv == 0):
                pe.wait_ge(bct_done, c)
            pe.wait_ge(cmp_rest, 8 * item(0) + 3)
            for k in range(2):
                nc.tensor.transpose(PSUM[:, 7, k * P:(k + 1) * P], BPAD[:, k, :], IDENT[:, :])
            for k in range(2):
                last_ = nc.tensor.transpose(PSUM[:, 7, (2 + k) * P:(3 + k) * P], CPAD[:, k, :], IDENT[:, :])
            last_.then_inc(bct_tp, 1)

        def bu(j):
            if j == 0:
                pe.wait_ge(bct_done, c + 1)
                pe.wait_ge(hn_chunk, c + 1)
            if not (first and kv == 0 and j == 0):
                pe.wait_ge(act_x, tile(c, j))
            r = slice(32 * j, 32 * j + 32)
            for k in range(2):
                last_ = nc.tensor.matmul(PSUM[:, 4 + k, 0:T], BCT[r, k, :], HN[r, 0, :], start=True, stop=True)
            last_.then_inc(pe_bu, 1)

        def y(j):
            pe.wait_ge(dve_h, tile(c, j) + 1)
            pe.wait_ge(pool_rot, tile(c, j) + 1)
            if j == 0 and not (first and kv == 0):
                pe.wait_ge(y_sum, c)
            r = slice(32 * j, 32 * j + 32)
            nc.tensor.matmul(PSUM[r, 6, 0:T], BCT[:, 2, r], H[:, j % 2, 0, :], start=True, stop=False)
            nc.tensor.matmul(PSUM[r, 6, 0:T], BCT[:, 3, r], H[:, j % 2, 1, :], start=False, stop=True).then_inc(pe_y, 1)

        def tp(gp, lo, hi):
            for m in range(lo, hi):
                u = m // 2
                pe.wait_ge(page_ready[u], 64 * item(gp) + 64)
                n = 8 * item(gp) + m
                at = 8 * gp + m
                bank, back = TP_BANKS[at], bank_back(at)
                if not (first and kv == 0 and at < back):
                    pe.wait_ge(cmp_rest, n + (1 - back))
                if bank == 7 and BCT_AT <= at and back > at - BCT_AT:
                    pe.wait_ge(bct_done, c + 1)
                for g in range(2):
                    for pg in range(2):
                        src = RAW[:, u, (2 * (m % 2) + pg) * 256 + g * DH:(2 * (m % 2) + pg) * 256 + (g + 1) * DH]
                        last_ = nc.tensor.transpose(PSUM[:, bank, (2 * g + pg) * P:(2 * g + pg + 1) * P], src, IDENT[:, :])
                last_.then_inc(cmp_tp, 1)

        def mm(gp, part):
            if part == 0:
                pe.wait_ge(cmp_rest, 8 * item(gp) + 8)
                if not (first and kv == 0 and gp == 0):
                    pe.wait_ge(cmp_gelu, item(gp))
                if first and gp == 0:
                    pe.wait_ge(rest_done, RING * kv + RING)
            for t in range(8 * part, 8 * part + 8):
                u, k = part, t % 8
                w = slice(k * P, (k + 1) * P)
                sh = 2 * (part // 2)
                hi, lo = (r[:, t % 16, :, :].rearrange("p n g -> p (n g)")[:, sh:sh + 2 * NCMP] for r in (RH, RL))
                o = PSUM[:, 2, 0:2 * NCMP]
                nc.tensor.matmul(o, WH[:, u, w], hi, start=t == 0, stop=False)
                nc.tensor.matmul(o, WH[:, u, w], lo, start=False, stop=False)
                last_ = nc.tensor.matmul(o, WL[:, u, w], hi, start=False, stop=t == TAPS - 1)
            if part == 3:
                last_.then_inc(cmp_acc, 1)

        tp(0, 0, 4)
        if not first:
            second_pe(pe, kv, item(0) - 1)
        bct()
        tp(0, 4, 7)
        bu(0)
        tp(0, 7, 8)
        bu(1)
        mm(0, 0)
        mm(0, 1)
        y(0)
        mm(0, 2)
        bu(2)
        mm(0, 3)
        y(1)
        tp(1, 0, 4)
        second_pe(pe, kv, item(0), first and kv == 0)
        tp(1, 4, 8)
        bu(3)
        mm(1, 0)
        mm(1, 1)
        y(2)
        mm(1, 2)
        mm(1, 3)
        y(3)

    def second_pe(pe, kv, item, very_first=False):
        pe.wait_ge(cmp_gelu, item + 1)
        if not very_first:
            pe.wait_ge(cmp_out, item)
        if kv == 0:
            for k in range(2):
                last = nc.tensor.matmul(PSUM[:, 3, 256 * k:256 * k + 2 * NCMP], W2K[:, k, :], GEL[:, :], start=True, stop=True)
        else:
            for g in range(2):
                hid = GEL[:, :].rearrange("p (n g) -> p g n", g=2)[:, g, :]
                last = nc.tensor.matmul(PSUM[0:NCMP, 3, g * P:(g + 1) * P], hid, W2V[:, :], start=True, stop=True)
        last.then_inc(cmp_mm2, 1)

    def body_act(act, kv, i, first):
        c = i + NKV * kv
        item = lambda gp: 2 * c + gp

        def take_x(j):
            q = tile(c, j)
            act.wait_ge(pe_bu, q + 1)
            if not (first and kv == 0 and j < 2):
                act.wait_ge(dve_rot, q - 1)
                act.wait_ge(pool_rot, q - 1)
            nc.scalar.activation(XRI[:, j % 2, :, :], PSUM[:, 4:6, 0:T], ACT.Copy).then_inc(act_x, 1)

        def heads(gp, lo, hi):
            for m in range(lo, hi):
                n = 8 * item(gp) + m
                act.wait_ge(cmp_tp, n + 1)
                if m == 0 and not (first and kv == 0 and gp == 0):
                    act.wait_ge(cmp_acc, item(gp))
                nc.scalar.activation(rows_of(RH, m), page_rows(TP_BANKS[8 * gp + m]), ACT.Copy).then_inc(cmp_head, 1)

        heads(0, 0, 4)
        act.wait_ge(bct_tp, c + 1)
        if not (first and kv == 0):
            act.wait_ge(pe_y, 4 * c)
        nc.scalar.activation(BCT[:, :, :], PSUM[:, 7, :].rearrange("p (k n) -> p k n", k=4), ACT.Copy).then_inc(bct_done, 1)
        heads(0, 4, 7)
        take_x(0)
        heads(0, 7, 8)
        if not first:
            keep_act(act, kv, item(0) - 1, i - 1, 1)
        tables_act(act, tile(c, 1), 1, first and kv == 0)
        take_x(1)
        take_x(2)
        tables_act(act, tile(c, 2), 0)
        gelu_act(act, kv, item(0), first and kv == 0)
        heads(1, 0, 8)
        keep_act(act, kv, item(0), i, 0)
        tables_act(act, tile(c, 3), 1)
        take_x(3)
        tables_act(act, tile(c, 4), 0)
        gelu_act(act, kv, item(1))
        act.wait_ge(y_sum, c + 1)
        nc.scalar.activation(HN[:, 3, :], HN[:, 3, :], ACT.Gelu_apprx_tanh).then_inc(y_gelu, 1)
        act.wait_ge(y_gelu, c + 1)
        nc.scalar.activation(XH[:, ds(c, 1), :].rearrange("p o t -> p (o t)"), HN[:, 3, :], ACT.Copy).then_inc(xh_done, 1)

    def tables_act(act, q, par_, very_first=False):
        act.wait_ge(pool_fs, q + 1)
        act.wait_ge(dve_fc, q + 1)
        if not very_first:
            act.wait_ge(dve_h, q - 1)
            act.wait_ge(pool_der, q - 1)
        nc.scalar.activation(SN[:, par_, :], FS[:, :], ACT.Sin, scale=TWOPI_IN)
        nc.scalar.activation(CS[:, par_, :], FCO[:, :], ACT.Sin, scale=-TWOPI_IN, bias=EPSB[:, 1:2]).then_inc(act_tab, 1)

    def gelu_act(act, kv, item, very_first=False):
        act.wait_ge(cmp_acc, item + 1)
        if not very_first:
            act.wait_ge(cmp_mm2, item)
        nc.scalar.activation(GEL[:, :], PSUM[:, 2, 0:2 * NCMP], ACT.Gelu_apprx_tanh,
                             bias=GW[:, 48 + kv:49 + kv]).then_inc(cmp_gelu, 1)

    def keep_act(act, kv, item, b, gp):
        if kv == 0:
            act.wait_ge(cmp_out, item + 1)
            src, dst = CMPO[:, 0:2 * NCMP], kscr
        else:
            act.wait_ge(cmp_mm2, item + 1)
            act.wait_ge(cmp_kept, 16 * item)
            nc.scalar.activation(CMPO[0:NCMP, :], PSUM[0:NCMP, 3, 0:2 * P], ACT.Copy).then_inc(cmp_out, 1)
            act.wait_ge(cmp_out, item + 1)
            src, dst = CMPO[0:NCMP, :], vscr
        act.dma_start(dst[ds(b, 1), gp].rearrange("o p n -> (o p) n"), src).then_inc(cmp_kept, 16)

    def turns_dve(dve, q, very_first=False):
        dve.wait_ge(pool_t1, q + 1)
        if not very_first:
            dve.wait_ge(pool_fs, q)
        nc.vector.tensor_scalar(KS[:, :], T1[:, :], MAGIC, -MAGIC, ALU.add, ALU.add).then_inc(dve_ks, 1)
        nc.vector.tensor_scalar(KCR[:, :], T1[:, :], 0.25, MAGIC, ALU.add, ALU.add).then_inc(dve_kc, 1)

    def cosine_dve(dve, q, very_first=False):
        dve.wait_ge(dve_kc, q + 1)
        if not very_first:
            dve.wait_ge(act_tab, q)
        nc.vector.scalar_tensor_tensor(out=FCO[:, :], in0=KCR[:, :], scalar=-MAGIC, in1=T1[:, :],
                                       op0=ALU.add, op1=ALU.subtract).then_inc(dve_fc, 1)

    def prologue_dve(dve):
        for q in range(2):
            turns_dve(dve, q, q == 0)
            cosine_dve(dve, q, q == 0)

    def body_dve(dve, kv, i, first):
        c = i + NKV * kv
        V = nc.vector
        item = lambda gp: 2 * c + gp

        def rests(gp, lo, hi):
            for m in range(lo, hi):
                dve.wait_ge(cmp_head, 8 * item(gp) + m + 1)
                V.tensor_tensor(rows_of(RL, m), page_rows(TP_BANKS[8 * gp + m]), rows_of(RH, m).bitcast(F32), ALU.subtract).then_inc(cmp_rest, 1)

        rests(0, 0, 2)
        if not (first and kv == 0):
            dve.wait_ge(pe_bu, 4 * c)
            dve.wait_ge(y_sum, c)
        V.scalar_tensor_tensor(out=HN[:, 0, :], in0=X[:, ds(c, 1), :].rearrange("p o t -> p (o t)"),
                               scalar=GV[:, ds(c, 1)], in1=RSTD[:, :], op0=ALU.mult, op1=ALU.mult).then_inc(hn_chunk, 1)
        rests(0, 2, 4)

        def state_tile(j):
            q, b = tile(c, j), j % 2
            x, sn, cs = XRI[:, b, :, 0:TP], SN[:, b, :], CS[:, b, :]
            G2 = HN[:, 1:3, 0:TP]
            dve.wait_ge(act_tab, q + 1)
            dve.wait_ge(act_x, q + 1)
            if not (first and kv == 0 and j == 0):
                dve.wait_ge(dve_h, q)
            V.tensor_tensor(N12[:, :, :], x, cs.unsqueeze(1).to_broadcast([P, 2, TP]), ALU.mult).then_inc(dve_n, 1)
            dve.wait_ge(dve_n, q + 1)
            dve.wait_ge(pool_rot, q + 1)
            V.tensor_tensor(G2[:, 0], N12[:, 0, :], M12[:, 0, :], ALU.add)
            V.tensor_tensor(G2[:, 1], N12[:, 1, :], M12[:, 1, :], ALU.subtract).then_inc(dve_rot, 1)
            dve.wait_ge(dve_rot, q + 1)
            m = PR[:, 4:5, ds(q, 1)].rearrange("p o q -> p (o q)").to_broadcast([P, TP])
            for k in range(2):
                last_ = V.tensor_tensor_scan(SRI[:, k, :], m, G2[:, k], 0.0, ALU.mult, ALU.add)
            last_.then_inc(dve_scan, 1)
            turns_dve(dve, q + 2)
            dve.wait_ge(dve_scan, q + 1)
            V.tensor_tensor(N12[:, :, :], SRI[:, :, :], cs.unsqueeze(1).to_broadcast([P, 2, TP]), ALU.mult).then_inc(dve_n2, 1)
            dve.wait_ge(dve_n2, q + 1)
            dve.wait_ge(pool_der, q + 1)
            if not (first and kv == 0 and j < 2):
                dve.wait_ge(pe_y, q - 1)
                dve.wait_ge(pool_fin, q - 1)
            V.tensor_tensor(H[:, b, 0, 0:TP], N12[:, 0, :], M12[:, 0, :], ALU.subtract)
            V.tensor_tensor(H[:, b, 1, 0:TP], N12[:, 1, :], M12[:, 1, :], ALU.add).then_inc(dve_h, 1)
            cosine_dve(dve, q + 2)

        rests(0, 4, 8)
        if not first:
            rotate_dve(dve, kv, item(0) - 1)
        state_tile(0)
        state_tile(1)
        rests(1, 0, 8)
        rotate_dve(dve, kv, item(0), first and kv == 0)
        state_tile(2)
        state_tile(3)
        dve.wait_ge(pe_y, 4 * c + 4)
        if not (first and kv == 0):
            dve.wait_ge(xl_done, c)
        V.scalar_tensor_tensor(out=HN[:, 3, :], in0=HN[:, 0, :], scalar=GW[:, ds(c, 1)], in1=PSUM[:, 6, 0:T],
                               op0=ALU.mult, op1=ALU.add).then_inc(y_sum, 1)
        dve.wait_ge(xh_done, c + 1)
        V.tensor_tensor(XL[:, ds(c, 1), :].rearrange("p o t -> p (o t)"), HN[:, 3, :],
                        XH[:, ds(c, 1), :].rearrange("p o t -> p (o t)").bitcast(F32), ALU.subtract).then_inc(xl_done, 1)

    def rotate_dve(dve, kv, item, very_first=False):
        if kv:
            return
        V = nc.vector
        dve.wait_ge(cmp_mm2, item + 1)
        V.tensor_tensor(RTMP[:, :], PSUM[:, 3, 256:256 + 2 * NCMP], ROPC[:, 1, :], ALU.mult)
        if not very_first:
            dve.wait_ge(cmp_kept, 16 * item)
        V.tensor_tensor(CMPO[:, 0:2 * NCMP], PSUM[:, 3, 0:2 * NCMP], ROPC[:, 0, :], ALU.mult).then_inc(rope_part, 1)
        dve.wait_ge(rope_part, item + 1)
        V.tensor_tensor(CMPO[:, 0:2 * NCMP], CMPO[:, 0:2 * NCMP], RTMP[:, :], ALU.add).then_inc(cmp_out, 1)

    def turns_pool(pool, q, very_first=False):
        if not very_first:
            pool.wait_ge(dve_fc, q)
            pool.wait_ge(pool_fs, q)
        shape = [P, 16, 16]
        a = ARGA[:, ds(q, 1), :].rearrange("p o b -> p (o b)").unsqueeze(2).to_broadcast(shape)
        b = ARGB[:, ds(q, 1), :].rearrange("p o b -> p (o b)").unsqueeze(1).to_broadcast(shape)
        nc.gpsimd.tensor_tensor(T1[:, :].rearrange("p (a b) -> p a b", b=16), a, b, ALU.add).then_inc(pool_t1, 1)

    def parts_pool(pool, q, very_first=False):
        pool.wait_ge(dve_ks, q + 1)
        pool.wait_ge(pool_t1, q + 1)
        if not very_first:
            pool.wait_ge(act_tab, q)
        nc.gpsimd.tensor_tensor(FS[:, :], T1[:, :], KS[:, :], ALU.subtract).then_inc(pool_fs, 1)

    def prologue_pool(pool):
        pool.wait_ge(arg_ready, N_PAR)
        for q in range(2):
            turns_pool(pool, q, q == 0)
            parts_pool(pool, q, q == 0)

    def body_pool(pool, kv, i, first):
        c = i + NKV * kv
        Q = nc.gpsimd
        pool.wait_ge(bc_loaded, 64 * c + 64)
        cf = [PR[:, k:k + 1, ds(4 * c, 4)].rearrange("p o q -> p (o q)").unsqueeze(2).to_broadcast([P, 4, GRP]) for k in (9, 10)]
        if not (first and kv == 0):
            pool.wait_ge(bct_tp, c)
        for k in range(2):
            Q.tensor_tensor(CPAD[:, k, :].rearrange("p (e s) -> p e s", e=2), CN_[:, k, :].unsqueeze(1).to_broadcast([P, 2, ST]),
                            CMASK[:, k, :].rearrange("p (e s) -> p e s", e=2), ALU.mult)
        Q.tensor_tensor(BP[:, 0, :, :], cf[0], BN[:, 0, :, :], ALU.mult)
        Q.tensor_tensor(BP[:, 1, :, :], cf[1], BN[:, 1, :, :], ALU.mult)
        Q.tensor_tensor(BP[:, 2, :, :], cf[0], BN[:, 1, :, :], ALU.mult)
        Q.tensor_tensor(BP[:, 3, :, :], cf[1], BN[:, 0, :, :], ALU.mult).then_inc(b_prod, 1)
        pool.wait_ge(b_prod, c + 1)
        bp = BPAD[:, :, :].rearrange("p k (j e h) -> p k e j h", j=4, e=2)
        for e in range(2):
            r = slice(ST * e, ST * e + ST)
            Q.tensor_tensor(bp[r, 0, e], BP[r, 0], BP[r, 1], ALU.subtract)
            last = Q.tensor_tensor(bp[r, 1, e], BP[r, 2], BP[r, 3], ALU.add)
        last.then_inc(bc_ready, 1)
        pool.wait_ge(bc_ready, c + 1)
        for j in range(4):
            q, b = tile(c, j), j % 2
            very_first = first and kv == 0
            pool.wait_ge(act_tab, q + 1)
            pool.wait_ge(act_x, q + 1)
            if not (very_first and j == 0):
                pool.wait_ge(dve_h, q)
            if not (very_first and j < 2):
                pool.wait_ge(pe_y, q - 1)
                pool.wait_ge(pool_fin, q - 1)
            Q.tensor_tensor(M12[:, 0, :], XRI[:, b, 1, 0:TP], SN[:, b, :], ALU.mult)
            Q.tensor_tensor(M12[:, 1, :], XRI[:, b, 0, 0:TP], SN[:, b, :], ALU.mult)
            w0 = W0[:, :, ds(q, 1), :].rearrange("p k o b -> p k (o b)")
            Q.tensor_tensor(H[:, b, :, TP:T], w0, XRI[:, b, :, TP:T], ALU.add).then_inc(pool_rot, 1)
            turns_pool(pool, q + 2)
            pool.wait_ge(dve_scan, q + 1)
            Q.tensor_tensor(M12[:, 0, :], SRI[:, 1, :], SN[:, b, :], ALU.mult)
            Q.tensor_tensor(M12[:, 1, :], SRI[:, 0, :], SN[:, b, :], ALU.mult).then_inc(pool_der, 1)
            parts_pool(pool, q + 2)
            pool.wait_ge(dve_h, q + 1)
            pool.wait_ge(pool_rot, q + 1)
            last = H[:, b, :, TP - 1:T]
            Q.tensor_tensor(FIN[:, :, ds(q, 1), :].rearrange("p k o b -> p k (o b)"), last,
                            ONES[:, 0:2 * (1 + TS)].rearrange("p (k b) -> p k b", k=2), ALU.mult).then_inc(pool_fin, 1)


    def sequences(eng, body):
        def run(kv):
            body(eng, kv, 0, True)
            with eng.Fori(1, NKV) as i:
                body(eng, kv, i, False)
        return run

    def stage1_sp(sp):
        run = sequences(sp, body_sp)
        sp.wait_ge(ld["late"], L_LATE)
        run(0)
        for u in range(RING):
            sp.wait_ge(cmp_tp, 8 * (2 * NKV - 1) + 2 * u + 2)
            load_taps(sp, 1, u)
        run(1)
        for u in range(RING):
            sp.wait_ge(cmp_tp, 8 * (4 * NKV - 1) + 2 * u + 2)
            load_unit(sp, Unit(TAP_UNITS + u), weight("glu", 0, 0)[:, UK * u:UK * (u + 1), :])

    def stage1_pe(pe):
        rms_pe(pe, "mix0")
        run = sequences(pe, body_pe)
        pe.wait_ge(ld["late"], L_LATE)
        for kv in range(2):
            run(kv)
            second_pe(pe, kv, 2 * NKV * (kv + 1) - 1)

    def stage1_act(act):
        tables_act(act, 0, 0, True)
        run = sequences(act, body_act)
        for kv in range(2):
            run(kv)
            n = 2 * NKV * (kv + 1)
            keep_act(act, kv, n - 1, NKV - 1, 1)
            act.wait_ge(cmp_acc, n)
            for u in range(RING):
                split_head(act, Unit(RING * (kv + 1) + u))

    def stage1_dve(dve):
        prologue_dve(dve)
        run = sequences(dve, body_dve)
        for kv in range(2):
            run(kv)
            rotate_dve(dve, kv, 2 * NKV * (kv + 1) - 1)
            for u in range(RING):
                split_rest(dve, Unit(RING * (kv + 1) + u))
        dve.wait_ge(pool_fin, NQ)
        dve.wait_ge(pool_fs, NQ + 2)
        dve.wait_ge(act_tab, NQ + 1)
        dve.wait_ge(cmp_kept, 16 * 4 * NKV)

    def stage1_pool(pool):
        prologue_pool(pool)
        run = sequences(pool, body_pool)
        for kv in range(2):
            run(kv)

    V = nc.vector

    X_ADDS = {"glu": 0, "ple0": 4, "ple1": 8}
    HID_USES, at = {}, 1
    for n in ("gu10", "gu20", "gu11", "gu21"):
        HID_USES[n] = at
        at += by_name[n].steps

    def add_to_x(dve, name, i):
        ph = by_name[name]
        xs = X[:, ds(4 * i, 4), :]
        V.tensor_tensor(xs, xs, ZB[:, :, :], ALU.add).then_inc(x_done, 1)
        square_dve(dve, ph.sq + i, SSQ[:, ds(i, 1), :])

    def glu_act(act):
        ph = by_name["glu"]

        def b(i):
            act.wait_ge(free_b, i + 1)
            nc.scalar.activation(ZB[:, :, :], ZB[:, :, :], ACT.Sigmoid).then_inc(glu_sig, 1)
            square_act(act, ph.sq + i, ds(4 * i, 4), x_done, i + 1)
        after_units(act, "glu", split_head, nothing, b)

    def glu_dve(dve):
        def bias(i, half):
            return GW[:, ds(4 * i + (16 + 16 * half), 4)].unsqueeze(2).to_broadcast([P, 4, T])

        def a(i):
            V.tensor_tensor(ZA[:, :, :], A4, bias(i, 0), ALU.add).then_inc(free_a, 1)

        def b(i):
            V.tensor_tensor(ZB[:, :, :], B4, bias(i, 1), ALU.add).then_inc(free_b, 1)
            dve.wait_ge(glu_sig, i + 1)
            V.tensor_tensor(ZB[:, :, :], ZA[:, :, :], ZB[:, :, :], ALU.mult).then_inc(prod_done, 1)
            dve.wait_ge(prod_done, i + 1)
            add_to_x(dve, "glu", i)
        after_units(dve, "glu", split_rest, a, b)

    def gate_act(act, name, func, hidden):
        ph = by_name[name]

        def a(i):
            act.wait_ge(free_b, ph.groups + i)
            nc.scalar.activation(ZA[:, :, :], A4, func).then_inc(free_a, 1)

        def b(i):
            if hidden:
                act.wait_ge(free_b, ph.groups + i + 1)
                nc.scalar.activation(HH[:, ds(4 * i, 4), :], ZB[:, :, :], ACT.Copy).then_inc(hh_done, 1)
            else:
                square_act(act, ph.sq + i, ds(4 * i, 4), x_done, X_ADDS[name] + i + 1)
        after_units(act, name, split_head, a, b)

    def gate_dve(dve, name, hidden):
        ph = by_name[name]

        def b(i):
            if hidden:
                dve.wait_ge(hl_done, HID_USES[name] + i)
            dve.wait_ge(free_a, ph.groups + i + 1)
            V.tensor_tensor(ZB[:, :, :], ZA[:, :, :], B4, ALU.mult).then_inc(free_b, 1)
            if not hidden:
                dve.wait_ge(free_b, ph.groups + i + 1)
                add_to_x(dve, name, i)
        after_units(dve, name, split_rest, nothing, b)

    def hidden_pool(pool, name):
        ph = by_name[name]
        with pool.Fori(0, ph.steps) as i:
            pool.wait_ge(hh_done, HID_USES[name] + i)
            pool.wait_ge(free_b, ph.groups + i + 1)
            nc.gpsimd.tensor_tensor(HL[:, ds(4 * i, 4), :], ZB[:, :, :], HH[:, ds(4 * i, 4), :].bitcast(F32),
                                    ALU.subtract).then_inc(hl_done, 1)

    def add_dve(dve, name, squares):
        ph = by_name[name]

        def part(half, bank, free):
            def f(i):
                xs = X[:, ds(8 * i + 4 * half, 4), :]
                V.tensor_tensor(xs, xs, bank, ALU.add).then_inc(free, 1)
                if squares:
                    square_dve(dve, ph.sq + 2 * i + half, SSQ[:, ds(2 * i + half, 1), :])
            return f
        after_units(dve, name, split_rest, part(0, A4, free_a), part(1, B4, free_b))

    def add_act(act, name, squares):
        ph = by_name[name]

        def part(half, free):
            def f(i):
                if squares:
                    square_act(act, ph.sq + 2 * i + half, ds(8 * i + 4 * half, 4), free, ph.groups + i + 1)
            return f
        after_units(act, name, split_head, part(0, free_a), part(1, free_b))

    def keep_groups_act(act, name, dst):
        def part(half, bank, free):
            return lambda i: nc.scalar.activation(dst(2 * i + half), bank, ACT.Copy).then_inc(free, 1)
        after_units(act, name, split_head, part(0, A4, free_a), part(1, B4, free_b))

    def only_split_dve(dve, name):
        after_units(dve, name, split_rest, nothing, nothing)

    def ffn_sp(sp, l):
        for n in ("gu1", "dn1", "gu2", "dn2", "ple"):
            phase_sp(sp, n + str(l))

    def ffn_pe(pe, l):
        rms_pe(pe, f"ffn{l}")
        for part in "12":
            gu, dn = f"gu{part}{l}", f"dn{part}{l}"
            phase_pe(pe, gu, XH, XL, normed_ready(pe, f"ffn{l}") if part == "1" else None)
            phase_pe(pe, dn, HH, HL, lambda k: pe.wait_ge(hl_done, HID_USES[gu] + k // 4 + 1))
        rms_pe(pe, f"ple{l}")
        phase_pe(pe, f"ple{l}", XH, XL, normed_ready(pe, f"ple{l}"), PH[:, l], PL[:, l])

    def ffn_act(act, l):
        rms_act(act, f"ffn{l}")
        norm_act(act, f"ffn{l}")
        for part in "12":
            gate_act(act, f"gu{part}{l}", ACT.Silu, True)
            add_act(act, f"dn{part}{l}", part == "2")
        rms_act(act, f"ple{l}")
        norm_act(act, f"ple{l}")
        gate_act(act, f"ple{l}", ACT.Sigmoid, False)

    def ffn_dve(dve, l):
        rms_dve(dve, f"ffn{l}")
        norm_dve(dve, f"ffn{l}", NFFN[l])
        for part in "12":
            gate_dve(dve, f"gu{part}{l}", True)
            add_dve(dve, f"dn{part}{l}", part == "2")
        rms_dve(dve, f"ple{l}")
        norm_dve(dve, f"ple{l}", NPLE[l])
        gate_dve(dve, f"ple{l}", False)

    def ffn_pool(pool, l):
        for part in "12":
            hidden_pool(pool, f"gu{part}{l}")

    class Steps:

        def __init__(self, name, steps):
            self.sem, self.steps, self.made = sem(name), steps, 0

        def made_by(self, ins, step):
            assert self.steps[self.made] == step, (step, self.steps[self.made])
            self.made += 1
            ins.then_inc(self.sem, 1)

        def wait(self, eng, step):
            eng.wait_ge(self.sem, self.steps.index(step) + 1)

    fs_tp, fs_used = sem("fs_tp"), sem("fs_used")
    FS_BANKS = 5

    def states_pe(pe):
        pe.wait_ge(pool_fin, NQ)
        pe.wait_ge(y_sum, KC)
        pe.wait_ge(act_x, NQ)
        pe.wait_ge(cmp_out, 4 * NKV)
        pe.wait_ge(cmp_rest, 32 * NKV)
        n = 2 * (1 + TS)
        for j in range(n):
            k, b = divmod(j, 1 + TS)
            last = nc.tensor.transpose(PSUM[0:NQ, j // 4, (j % 4) * P:(j % 4 + 1) * P], FIN[:, k, :, b], IDENT[:, :])
            if j % 4 == 3 or j == n - 1:
                last.then_inc(fs_tp, 1)
        pe.wait_ge(fs_used, FS_BANKS)

    def states_dve(dve):
        for j in range(FS_BANKS):
            m = min(4, 2 * (1 + TS) - 4 * j)
            dve.wait_ge(fs_tp, j + 1)
            V.tensor_copy(OUTS[:, 4 * j:4 * j + m, :], PSUM[0:NQ, j, 0:m * P].rearrange("q (b s) -> q b s", s=P)).then_inc(fs_used, 1)

    def states_sp(sp):
        sp.wait_ge(fs_used, FS_BANKS)
        for k, n in enumerate(("ssm_re", "ssm_im")):
            at = k * (1 + TS)
            view = lambda name: out[name][0].rearrange("b (q e) s -> q b (e s)", e=2)
            sp.dma_start(view(n + "_prompt"), OUTS[:, at:at + 1, :]).then_inc(stored, 16)
            sp.dma_start(view(n + "_sample"), OUTS[:, at + 1:at + 1 + TS, :]).then_inc(stored, 16)
    STATES_STORED = 64

    att_ready = [sem(f"att_ready{k}") for k in range(RING)]
    att_used = sem("att_used")
    ld_gate, ld_masks, ld_taps, ld_kc, ld_vc, gates_moved = (
        sem(n) for n in ("ld_gate", "ld_masks", "ld_taps", "ld_kc", "ld_vc", "gates_moved"))
    rows_stored, shift_stored = sem("rows_stored"), sem("shift_stored")
    SLC_PAGES, WIN_PAGES = TS * PAGES, TS * WIN // PAGE
    BRANCH = {"sk": 0, "wk": SLC_PAGES, "sv": SLC_PAGES + WIN_PAGES, "wv": 2 * SLC_PAGES + WIN_PAGES}
    ATT_PAGES = 2 * (SLC_PAGES + WIN_PAGES)

    def before_kv_sp(sp):
        sp.wait_ge(ssq_done, by_name["ple0"].sq)
        sp.dma_start(WGR[:, :, :], io["nsa_w_gate"][0].rearrange("(k p) n -> p k n", p=P)).then_inc(ld_gate, 16)
        sp.dma_start(BGATE[0:48, 0:1], io["nsa_b_gate"][0].rearrange("(p a) -> p a", a=1)).then_inc(ld_gate, 16)

    def attention_small_sp(sp):
        gate_pe.wait(sp, "gates")
        for dst, name in ((CAUS, "causal"), (CMPV, "cmpvis"), (ROPP, "ropep"), (BD, "bd"), (SAME, "same"),
                          (TOB, "toblk"), (EARL, "earlier")):
            sp.dma_start(dst[:], io["k_" + name]).then_inc(ld_masks, 16)
        sp.dma_start(W1P[:, :, :], w1[0].rearrange("t d h -> d t h")).then_inc(ld_taps, 16)
        sp.dma_start(W1Q[:, :, :], w1[1].rearrange("t d h -> d t h")).then_inc(ld_taps, 16)
        sp.dma_start(W2P[:, 0, :], io["cmp_k_w2"]).then_inc(ld_taps, 16)
        sp.dma_start(W2P[:, 1, 0:64], io["cmp_k_w2"][:, 64:128]).then_inc(ld_taps, 16)
        sp.dma_start(W2P[:, 1, 64:128], io["cmp_k_w2"][:, 0:64]).then_inc(ld_taps, 16)
        sp.dma_start(W2P[:, 2, :], io["cmp_v_w2"]).then_inc(ld_taps, 16)
    L_MASKS, L_TAPS = 16 * 7, 16 * 6

    PER = {"s": PAGES, "w": WIN // PAGE}

    def page_number(branch, i, k, j):
        per = PER[branch[0]]
        return i * (2 * per) + (BRANCH[branch] + per * k + j)

    def load_pages(eng, name, branch, i, odd, first=False):
        per = PER[branch[0]]
        for u in range(per):
            mine = odd == 0 if first and u < RING else u % 2 == odd
            if not mine:
                continue
            dst = RAW[:, u % RING, :].rearrange("p (t n) -> p t n", t=2)
            if branch[0] == "s":
                view = io[name].rearrange("n r g d -> n r (g d)")
                pages = [eng.value_load(PT[0:1, ds(i * (2 * PAGES) + (2 * u + m), 1)], min_val=0, max_val=POOL - 1) for m in range(2)]
            if first and u < RING:
                eng.wait_ge(rest_done, by_name["o"].base + RING)
            else:
                eng.wait_ge(att_used, page_number(branch, i, 0, 2 * u - 6))
            if branch[0] == "s":
                for m, page in enumerate(pages):
                    eng.dma_start(dst[:, m, :], view[ds(page, 1)].rearrange("o r n -> (o r) n")).then_inc(att_ready[u % RING], 16)
            else:
                view = io[name].rearrange("b (u t p) g d -> (b u) p t (g d)", u=2, p=P)
                eng.dma_start(dst, view[ds(i * 4 + u, 1)].rearrange("o p t n -> (o p) t n")).then_inc(att_ready[u % RING], 32)

    def branch_loads(eng, name, branch, odd):
        if branch == "sk":
            load_pages(eng, name, branch, 0, odd, True)
        with eng.Fori(1 if branch == "sk" else 0, TS // 2) as i:
            load_pages(eng, name, branch, i, odd)

    def wait_page(pe, branch, i, k, j):
        n = BRANCH[branch] + PER[branch[0]] * k + j
        pe.wait_ge(att_ready[n // 2 % RING], i * (8 * PER[branch[0]]) + 32 * (n // 8 + 1))

    gate_pe = Steps("gate_pe", ["gates"])
    at_const, wg_zero, wg_head, wg_split, gate_sig = (sem(n) for n in ("at_const", "wg_zero", "wg_head", "wg_split", "gate_sig"))
    sw_done, sw_used, rope_cos, rope_done, new_done = (sem(n) for n in ("sw_done", "sw_used", "rope_cos", "rope_done", "new_done"))
    nt_done, nt_used = sem("nt_done"), sem("nt_used")
    nat_stored = [sem(f"nat_stored{k}") for k in range(2)]
    ROPED = [KVT[:, 2, :, :], KVT[:, 4, :, :]] + [QT[:, 4 * j:4 * j + 4, :] for j in range(4)]
    NT_JOBS = 15
    KEPT = {3: 0, 5: 1}

    def rotate_pe(pe):
        ph = by_name["o"]
        pe.wait_ge(at_const, 1)
        for j, src in enumerate(ROPED):
            if j == 0:
                pe.wait_ge(free_a, ph.groups)
            if j == 1:
                pe.wait_ge(free_b, ph.groups)
            if j >= 2:
                pe.wait_ge(sw_used, j - 1)
            for h in range(4):
                last = nc.tensor.matmul(PSUM[:, 4 * (j % 2) + h, 0:T], SWAP[:, :], src[:, h, :], start=True, stop=True)
            last.then_inc(sw_done, 1)
        pe.wait_ge(wg_split, 1)
        pe.wait_ge(sw_used, 5)
        for k in range(KC):
            nc.tensor.matmul(PSUM[:, 0, 0:T], WGH[:, k, :], XH[:, k, :], start=k == 0, stop=False)
            nc.tensor.matmul(PSUM[:, 0, 0:T], WGH[:, k, :], XL[:, k, :], start=False, stop=False)
            last = nc.tensor.matmul(PSUM[:, 0, 0:T], WGL[:, k, :], XH[:, k, :], start=False, stop=k == KC - 1)
        gate_pe.made_by(last, "gates")
        pe.wait_ge(rope_done, 6)
        for j in range(NT_JOBS):
            bank = 1 + j % 7
            if j >= 7:
                pe.wait_ge(nt_used, j - 6)
            if j < 12:
                t, qt = divmod(j, 2)
                for g in range(G):
                    last = nc.tensor.transpose(PSUM[:, bank, g * DH:(g + 1) * DH], KVT[:, t, g, qt * P:(qt + 1) * P], IDENT[:, :])
            elif j < 14:
                pe.wait_ge(new_done, 1)
                for m in range(4 if j == 12 else 2):
                    t = 4 * (j - 12) + m
                    last = nc.tensor.transpose(PSUM[0:TS * G, bank, m * DH:(m + 1) * DH], KS6[:, t, :], IDENT[:, :])
            else:
                pe.wait_ge(gate_sig, 1)
                for qt in range(2):
                    nc.tensor.transpose(PSUM[:, bank, qt * 48:(qt + 1) * 48], GT[0:48, qt * P:(qt + 1) * P], IDENT[0:48, 0:48])
                last = nc.tensor.transpose(PSUM[0:TS, bank, 96:144], GT[0:48, TP:T], IDENT[0:48, 0:48])
            last.then_inc(nt_done, 1)

    def rotate_dve_all(dve):
        V.tensor_copy(SWAP[:, 0:64], IDENT[:, 64:128])
        V.tensor_copy(SWAP[:, 64:128], IDENT[:, 0:64]).then_inc(at_const, 1)
        V.memset(WGH[:, :, :].bitcast(F32), 0.0)
        V.memset(WGL[:, :, :].bitcast(F32), 0.0).then_inc(wg_zero, 1)
        for j, dst in enumerate(ROPED):
            cos, sin = (ROPET[:, k, :].unsqueeze(1).to_broadcast([P, 4, T]) for k in range(2))
            dve.wait_ge(sw_done, j + 1)
            if j >= 2:
                dve.wait_ge(rope_done, j - 1)
            part = (ZA, ZB)[j % 2]
            V.tensor_tensor(part[:, :, :], PSUM[:, 4 * (j % 2):4 * (j % 2) + 4, 0:T], sin, ALU.mult).then_inc(sw_used, 1)
            V.tensor_tensor(dst, dst, cos, ALU.mult).then_inc(rope_cos, 1)
            dve.wait_ge(rope_cos, j + 1)
            V.tensor_tensor(dst, dst, part[:, :, :], ALU.add).then_inc(rope_done, 1)
            if j == 1:
                dve.wait_ge(wg_head, 1)
                V.tensor_tensor(WGL[:, :, 0:48], WGR[:, :, :], WGH[:, :, 0:48].bitcast(F32), ALU.subtract).then_inc(wg_split, 1)
        dve.wait_ge(rope_done, 6)
        V.tensor_copy(KS6[:, :, :].rearrange("p t (b g) -> p t b g", g=G), KVT[:, :, :, TP:T].rearrange("p t g b -> p t b g")).then_inc(new_done, 1)
        V.tensor_copy(QS[:, :].rearrange("p (b h) -> p b h", h=NH), QT[:, :, TP:T].rearrange("p h b -> p b h")).then_inc(new_done, 1)
        stores = 0
        for j in range(NT_JOBS):
            bank = 1 + j % 7
            dve.wait_ge(nt_done, j + 1)
            if j < 12:
                t, qt = divmod(j, 2)
                if t in KEPT:
                    dst = VNAT[:, KEPT[t], qt, :]
                else:
                    dst = NAT[:, stores % 2, :]
                    if stores >= 2:
                        dve.wait_ge(nat_stored[stores % 2], 16 * (stores // 2))
                    stores += 1
                V.tensor_copy(dst, PSUM[:, bank, :]).then_inc(nt_used, 1)
            elif j < 14:
                m = 4 if j == 12 else 2
                V.tensor_copy(SNAT[:, 4 * (j - 12):4 * (j - 12) + m, :].rearrange("p t d -> p (t d)"), PSUM[0:TS * G, bank, 0:m * DH]).then_inc(nt_used, 1)
            else:
                V.tensor_copy(GNS[:, :], PSUM[0:TS, bank, 96:144])
                V.tensor_copy(GN[:, :, :].rearrange("p q n -> p (q n)"), PSUM[:, bank, 0:96]).then_inc(nt_used, 1)

    ROW_NAMES = ["cmp_k", "cmp_v", "slc_k", "slc_v", "win_k", "win_v"]
    PASSING = [j for j in range(12) if j // 2 not in KEPT]

    def rotate_act_all(act):
        act.wait_ge(ld_gate, 32)
        act.wait_ge(wg_zero, 1)
        nc.scalar.activation(WGH[:, :, 0:48], WGR[:, :, :], ACT.Copy).then_inc(wg_head, 1)
        gate_pe.wait(act, "gates")
        nc.scalar.activation(GT[0:48, :], PSUM[0:48, 0, 0:T], ACT.Sigmoid, bias=BGATE[0:48, 0:1]).then_inc(gate_sig, 1)

    def rows_sp(sp):
        for j in range(12):
            t, qt = divmod(j, 2)
            sp.wait_ge(nt_used, j + 1)
            slot = None if t in KEPT else PASSING.index(j) % 2
            src = VNAT[:, KEPT[t], qt, :] if slot is None else NAT[:, slot, :]
            dst = out[ROW_NAMES[t] + "_prompt"][0].rearrange("(q p) g d -> q p (g d)", p=P)[qt]
            sp.dma_start(dst, src).then_inc(rows_stored if slot is None else nat_stored[slot], 16)
        sp.wait_ge(nt_used, NT_JOBS)
        for t in range(4):
            sp.dma_start(out[ROW_NAMES[t] + "_sample"].rearrange("b o g d -> (b o g) d"), SNAT[:, t, :]).then_inc(rows_stored, 16)
        for t in (4, 5):
            for b in range(TS):
                sp.dma_start(out[ROW_NAMES[t] + "_sample"][b, WIN - 1], SNAT[G * b:G * b + G, t, :]).then_inc(rows_stored, 16)
        for br in range(3):
            sp.dma_start(GSM[:, br:br + 1], GNS[:, NH * br:NH * br + NH]).then_inc(gates_moved, 16)
    ROWS_STORED = 16 * (4 + 4 + 2 * TS)
    NAT_STORED = 16 * 4

    def shift_sp(sp):
        for k, n in enumerate(("state_win_k", "state_win_v")):
            o = out[("win_k", "win_v")[k] + "_sample"]
            sp.dma_start(o[:, 0:WIN - 1].rearrange("b w g d -> b (w g d)"), io[n][:, 1:WIN].rearrange("b w g d -> b (w g d)")).then_inc(shift_stored, 16)
    SHIFT_STORED = 32

    pc_pe = Steps("pc_pe", ["k hidden", "v hidden", "k second", "v second"])
    pc_act = Steps("pc_act", ["k gelu", "v gelu", "v rows"])
    pc_dve = Steps("pc_dve", ["k cos", "k rows"])
    NPC = G * NCMPP

    def prompt_cmp_pe(pe):
        pe.wait_ge(nt_used, NT_JOBS)
        pe.wait_ge(ld_taps, L_TAPS)
        for kv, taps in enumerate((W1P, W1Q)):
            rows = KVT[:, kv, :, 0:TP].rearrange("p g (n s) -> p s g n", s=STRIDE)
            for t in range(TAPS):
                j, s = divmod(t, STRIDE)
                last = nc.tensor.matmul(PSUM[:, 1 + kv, 0:NPC], taps[:, t, :], rows[:, s, :, j:j + NCMPP],
                                        start=t == 0, stop=t == TAPS - 1)
            pc_pe.made_by(last, "kv"[kv] + " hidden")
        pc_act.wait(pe, "k gelu")
        for k in range(2):
            last = nc.tensor.matmul(PSUM[:, 3, 64 * k:64 * k + NPC], W2P[:, k, :], GEP[:, 0, 0:NPC], start=True, stop=True)
        pc_pe.made_by(last, "k second")
        pc_act.wait(pe, "v gelu")
        for g in range(G):
            last = nc.tensor.matmul(PSUM[0:NCMPP, 4, g * P:(g + 1) * P], GEP[:, 1, g * NCMPP:(g + 1) * NCMPP], W2P[:, 2, :], start=True, stop=True)
        pc_pe.made_by(last, "v second")

    def prompt_cmp_act(act):
        for kv in range(2):
            pc_pe.wait(act, "kv"[kv] + " hidden")
            pc_act.made_by(nc.scalar.activation(GEP[:, kv, 0:NPC], PSUM[:, 1 + kv, 0:NPC], ACT.Gelu_apprx_tanh,
                                                bias=GW[:, 48 + kv:49 + kv]), "kv"[kv] + " gelu")
        pc_pe.wait(act, "v second")
        pc_act.made_by(nc.scalar.activation(VCP[0:NCMPP, :, :].rearrange("p g d -> p (g d)"), PSUM[0:NCMPP, 4, :], ACT.Copy), "v rows")

    def prompt_cmp_dve(dve):
        pc_pe.wait(dve, "k second")
        dve.wait_ge(ld_masks, L_MASKS)
        V.tensor_tensor(RTP[:, 0:NPC], PSUM[:, 3, 64:64 + NPC], ROPP[:, 1, :], ALU.mult)
        pc_dve.made_by(V.tensor_tensor(KCP[:, 0:NPC], PSUM[:, 3, 0:NPC], ROPP[:, 0, :], ALU.mult), "k cos")
        pc_dve.wait(dve, "k cos")
        pc_dve.made_by(V.tensor_tensor(KCP[:, 0:NPC], KCP[:, 0:NPC], RTP[:, 0:NPC], ALU.add), "k rows")

    ITEMS = [(qt, g, br) for qt in range(2) for g in range(G) for br in range(3)]
    sc_done, sc_used, mx_done, nm_done, ex_done, vis_done, rs_done, rc_done, fg_done, pr_done = (
        sem("ap_" + n) for n in ("scores", "scores_used", "max", "negmax", "exp", "visible", "sum", "recip", "factor", "probs"))
    pt_done, pt_taken, pv_done, po_used = (sem("ap_" + n) for n in ("t_done", "t_taken", "pv", "out_used"))

    def keys_of(item):
        qt, g, br = item
        return NCMPP if br == 0 else P * (qt + 1)

    def score_banks(k):
        return PSUM[:, 2 * (k % 2):2 * (k % 2) + 2, :].rearrange("p b (r n) -> p (b r) n", r=2)

    def prompt_scores_pe(pe, k):
        qt, g, br = item = ITEMS[k]
        if k >= 2:
            pe.wait_ge(sc_used, k - 1)
        for r in range(HREP):
            keys = KCP[:, g * NCMPP:(g + 1) * NCMPP] if br == 0 else KVT[:, 2 * br, g, 0:keys_of(item)]
            last = nc.tensor.matmul(score_banks(k)[:, r, 0:keys_of(item)], QT[:, HREP * g + r, qt * P:(qt + 1) * P], keys, start=True, stop=True)
        last.then_inc(sc_done, 1)

    def prompt_att_pe(pe):
        pc_dve.wait(pe, "k rows")
        pc_act.wait(pe, "v rows")
        prompt_scores_pe(pe, 0)
        prompt_scores_pe(pe, 1)
        for k in range(len(ITEMS)):
            if k + 2 < len(ITEMS):
                prompt_scores_pe(pe, k + 2)
            pe.wait_ge(pr_done, k + 1)
            if k >= 1:
                pe.wait_ge(pt_taken, k)
            for kc, w in parts_of(k):
                for r in range(HREP):
                    last = nc.tensor.transpose(PSUM[0:w, 4 + kc, r * P:(r + 1) * P], SP2[:, k % 2, r, kc * P:kc * P + w], IDENT[:, :])
            last.then_inc(pt_done, 1)
            if k >= 1:
                prompt_outputs_pe(pe, k - 1)
        prompt_outputs_pe(pe, len(ITEMS) - 1)

    def parts_of(k):
        n = keys_of(ITEMS[k])
        return [(kc, min(P, n - kc * P)) for kc in range(-(-n // P))]

    def prompt_outputs_pe(pe, k):
        qt, g, br = ITEMS[k]
        parts = parts_of(k)
        pe.wait_ge(pt_taken, k + 1)
        o = k // 3
        if br == 0 and o >= 2:
            pe.wait_ge(po_used, o - 1)
        for kc, w in parts:
            v = VCP[0:w, g, :] if br == 0 else VNAT[0:w, br - 1, kc, g * DH:(g + 1) * DH]
            last = nc.tensor.matmul(PSUM[:, 6 + o % 2, :], v, PTP[0:w, k % 2, kc, :], start=br == 0 and kc == 0,
                                    stop=br == 2 and kc == len(parts) - 1)
        last.then_inc(pv_done, 1)

    def prompt_mask_dve(dve, k):
        qt, g, br = item = ITEMS[k]
        n = keys_of(item)
        s = SP2[:, k % 2, :, 0:n]
        mask = CMPV[:, qt, :] if br == 0 else CAUS[:, qt, 0:n]
        dve.wait_ge(sc_done, k + 1)
        if k >= 2:
            dve.wait_ge(pt_done, k - 1)
        V.tensor_tensor(s, score_banks(k)[:, :, 0:n], mask.unsqueeze(1).to_broadcast([P, HREP, n]), ALU.add).then_inc(sc_used, 1)
        dve.wait_ge(sc_used, k + 1)
        V.tensor_reduce(SM[:, 16 * (k % 2):16 * (k % 2) + 4], s, AX.X, ALU.max).then_inc(mx_done, 1)
        dve.wait_ge(mx_done, k + 1)
        V.tensor_scalar(SM[:, 16 * (k % 2) + 4:16 * (k % 2) + 8], SM[:, 16 * (k % 2):16 * (k % 2) + 4], -1e20, -SCALE, ALU.max, ALU.mult).then_inc(nm_done, 1)

    def prompt_att_dve(dve):
        dve.wait_ge(ld_masks, L_MASKS)
        prompt_mask_dve(dve, 0)
        for k, item in enumerate(ITEMS):
            qt, g, br = item
            n = keys_of(item)
            if k + 1 < len(ITEMS):
                prompt_mask_dve(dve, k + 1)
            s = SP2[:, k % 2, :, 0:n]
            at = 16 * (k % 2)
            dve.wait_ge(ex_done, 4 * k + 4)
            if br == 0:
                vis = CMPV[:, 2 + qt, :].unsqueeze(1).to_broadcast([P, HREP, n])
                V.tensor_tensor(s, s, vis, ALU.mult).then_inc(vis_done, 1)
                dve.wait_ge(vis_done, k // 3 + 1)
                V.tensor_reduce(SM[:, at + 8:at + 12], s, AX.X, ALU.add).then_inc(rs_done, 1)
                dve.wait_ge(rs_done, k // 3 + 1)
            V.tensor_scalar(SM[:, at:at + 4], SM[:, at + 8:at + 12], 1e-30, None, ALU.max).then_inc(rc_done, 1)
            dve.wait_ge(rc_done, 2 * k + 1)
            V.reciprocal(SM[:, at:at + 4], SM[:, at:at + 4]).then_inc(rc_done, 1)
            dve.wait_ge(rc_done, 2 * k + 2)
            h = NH * br + HREP * g
            V.tensor_tensor(SM[:, at + 12:at + 16], SM[:, at:at + 4], GN[:, qt, h:h + 4], ALU.mult).then_inc(fg_done, 1)
            dve.wait_ge(fg_done, k + 1)
            V.tensor_tensor(s, s, SM[:, at + 12:at + 16].unsqueeze(2).to_broadcast([P, HREP, n]), ALU.mult).then_inc(pr_done, 1)
            if br == 2 and k >= 5:
                prompt_out_dve(dve, k // 3 - 1)
        prompt_out_dve(dve, len(ITEMS) // 3 - 1)

    def prompt_out_dve(dve, o):
        qt, g, _ = ITEMS[3 * o]
        dve.wait_ge(pv_done, 3 * o + 3)
        V.tensor_copy(QT[:, HREP * g:HREP * g + 4, qt * P:(qt + 1) * P], PSUM[:, 6 + o % 2, :].rearrange("p (r t) -> p r t", r=4)).then_inc(po_used, 1)

    def prompt_exp_act(act, k):
        qt, g, br = item = ITEMS[k]
        n = keys_of(item)
        act.wait_ge(nm_done, k + 1)
        for r in range(HREP):
            s = SP2[:, k % 2, r, 0:n]
            at = 16 * (k % 2)
            nc.scalar.activation(s, s, ACT.Exp, scale=SCALE, bias=SM[:, at + 4 + r:at + 5 + r],
                                 accum_out=SM[:, at + 8 + r:at + 9 + r]).then_inc(ex_done, 1)

    def prompt_att_act(act):
        prompt_exp_act(act, 0)
        for k, item in enumerate(ITEMS):
            if k + 1 < len(ITEMS):
                prompt_exp_act(act, k + 1)
            n = keys_of(item)
            act.wait_ge(pt_done, k + 1)
            if k >= 2:
                act.wait_ge(pv_done, k - 1)
            w, m = min(n, P), -(-n // P)
            nc.scalar.activation(PTP[0:w, k % 2, 0:m, :], PSUM[0:w, 4:4 + m, :], ACT.Copy).then_inc(pt_taken, 1)

    kt_taken, ks_done, q_ready, pr_ready, vo_taken, q_clear, vo_tp, pv_added = (
        sem(n) for n in ("kt_taken", "ks_done", "q_ready", "pr_ready", "vo_taken", "q_clear", "vo_tp", "pv_added"))
    sp_pe = Steps("sp_pe", ["cmp scores", "cmp rows", "cmp turned", "block scores", "block sums", "cmp gated turned",
                            "slc rows", "win rows", "new turned", "slc turned", "win turned", "cmp out"])
    sp_act = Steps("sp_act", ["cmp copied", "cmp exp", "cmp turned kept", "block scores kept", "cmp gated kept",
                              "slc exp", "slc new exp", "win exp", "win new exp", "slc kept", "win kept"])
    sp_dve = Steps("sp_dve", ["cmp negmax", "cmp probs", "cmp gated", "slc taken", "slc negmax", "win negmax",
                              "slc probs", "win probs", "new probs", "new kept", "slc kept", "out"])
    ch_dve = sem("ch_dve")
    chain = [0]

    def sequences_of(eng, body):
        for k in range(2):
            body(0, k)
        with eng.Fori(1, TS // 2) as i:
            for k in range(2):
                body(i, k)

    def seq_number(branch, i, k):
        return i * 2 + (k + (0 if branch[0] == "s" else TS))

    def spread(k, n):
        row = QPAD[:, k, ds(n * NH, G * QSTEP)]
        return row.rearrange("p (g c) -> p g c", c=QSTEP)[:, :, 0:HREP]

    def known(s):
        return isinstance(s, int)

    def before(i, k, back):
        return (2 * i + k - back) % TS if known(i) else i * 2 + (k - back)

    def key_pages_pe(pe, branch):
        per = PER[branch[0]]

        def body(i, k):
            n = lambda j: page_number(branch, i, k, j)
            s = seq_number(branch, i, k)

            def turn(j):
                if j % 2 == 0:
                    wait_page(pe, branch, i, k, j)
                if not (known(s) and s == 0 and j < 2):
                    pe.wait_ge(kt_taken, n(j - 1))
                slot = (per * k + j) // 2 % RING
                for g in range(G):
                    at = (j % 2) * 512 + g * DH
                    last = nc.tensor.transpose(PSUM[:, j % 2, g * P:(g + 1) * P], RAW[:, slot, at:at + DH], IDENT[:, :])
                last.then_inc(att_used, 1)

            turn(0)
            pe.wait_ge(q_ready, s + 1)
            for j in range(per):
                if j + 1 < per:
                    turn(j + 1)
                pe.wait_ge(kt_taken, n(j + 1))
                bank = 2 + j // 4 if branch[0] == "s" else 6
                for g in range(G):
                    last = nc.tensor.matmul(PSUM[:, bank, (j % 4) * P:(j % 4 + 1) * P], QPAD[:, k, g * P:(g + 1) * P],
                                            KT[:, j % 2, g * P:(g + 1) * P], start=False, stop=False, skip_group_check=True)
                last.then_inc(ks_done, 1)

        sequences_of(pe, body)

    def zeros_pe(banks, **flags):
        for bank in banks:
            last = nc.tensor.matmul(PSUM[:, bank, :].rearrange("p (a b) -> p a b", a=4), ZERO[:, :],
                                    ZERO[:, :].unsqueeze(1).to_broadcast([P, 4, P]), skip_group_check=True, **flags)
        return last

    def key_pages_dve(dve, branch):
        per = PER[branch[0]]

        def body(i, k):
            n = lambda j: page_number(branch, i, k, j)
            s = seq_number(branch, i, k)
            if not (known(s) and s < 2):
                dve.wait_ge(q_clear, s + (-1))
            q = QS[:, ds((i * 2 + k) * NH, NH)].rearrange("p (g r) -> p g r", g=G)
            ones = ONES[:, 0:NH].rearrange("p (g r) -> p g r", g=G)
            nc.vector.tensor_tensor(spread(k, i * 2 + k), q, ones, ALU.mult).then_inc(q_ready, 1)
            for j in range(per):
                dve.wait_ge(att_used, n(j + 1))
                if not (known(s) and s == 0 and j < 2):
                    dve.wait_ge(ks_done, n(j - 1))
                nc.vector.tensor_copy(KT[:, j % 2, :], PSUM[:, j % 2, :]).then_inc(kt_taken, 1)
                if j == 1 and not (known(s) and s == 0):
                    dve.wait_ge(ks_done, n(0))
                    none = ZERO[:, 0:NH].rearrange("p (g r) -> p g r", g=G)
                    nc.vector.tensor_tensor(spread(1 - k, before(i, k, 1)), none, none, ALU.add).then_inc(q_clear, 1)

        sequences_of(dve, body)

    def value_pages_pe(pe, branch):
        per = PER[branch[0]]

        def body(i, k):
            s = seq_number(branch, i, k)
            pe.wait_ge(pr_ready, s + 1)
            if not (known(s) and s < 2):
                pe.wait_ge(vo_taken, s + (-1))
            for j in range(per):
                if j % 2 == 0:
                    wait_page(pe, branch, i, k, j)
                turning = j == 2 and not (known(s) and s == 0)
                if turning:
                    output_taken(pe, s + (-1))
                slot = (per * k + j) // 2 % RING
                last = nc.tensor.matmul(PSUM[0:NH, k, :], PRL[:, k, j, :], RAW[:, slot, (j % 2) * 512:(j % 2 + 1) * 512],
                                        start=j == 0, stop=j == per - 1)
                last.then_inc(att_used, 1)
                if turning:
                    turn_output(1 - k)

        sequences_of(pe, body)

    def output_taken(pe, s):
        pe.wait_ge(vo_taken, s + 1)
        if not (known(s) and s == 0):
            pe.wait_ge(pv_added, s)

    def turn_output(k):
        for g in range(G):
            last = nc.tensor.transpose(PSUM[:, 2, g * NH:(g + 1) * NH], VO[:, k, g * DH:(g + 1) * DH], IDENT[0:NH, 0:NH])
        last.then_inc(vo_tp, 1)

    def value_pages_dve(dve, branch):
        per = PER[branch[0]]
        probs = SCT if branch[0] == "s" else STW

        def body(i, k):
            s = seq_number(branch, i, k)
            ones = ONES[:, 0:NH].unsqueeze(1).to_broadcast([P, per, NH])
            nc.vector.tensor_tensor(PRL[:, k, 0:per, :], probs[:, :, ds((i * 2 + k) * NH, NH)], ones, ALU.mult).then_inc(pr_ready, 1)
            if not (known(s) and s == 0):
                dve.wait_ge(att_used, page_number(branch, i, k, 0))
                nc.vector.tensor_copy(VO[:, 1 - k, :], PSUM[0:NH, 1 - k, :]).then_inc(vo_taken, 1)
            if not (known(s) and s < 2):
                add_output(dve, s + (-2), before(i, k, 2))

        sequences_of(dve, body)

    def add_output(dve, s, seq):
        dve.wait_ge(vo_tp, s + 1)
        if not (known(s) and s == 0):
            dve.wait_ge(pv_added, s)
        cols = DACC[:, ds(seq * NH, NH)].rearrange("p (g r) -> p g r", g=G)
        own = PSUM[:, 2, 0:G * (NH + HREP)].rearrange("p (g c) -> p g c", c=NH + HREP)[:, :, 0:HREP]
        nc.vector.tensor_tensor(cols, cols, own, ALU.add).then_inc(pv_added, 1)

    def last_outputs_dve(dve):
        dve.wait_ge(att_used, ATT_PAGES)
        nc.vector.tensor_copy(VO[:, 1, :], PSUM[0:NH, 1, :]).then_inc(vo_taken, 1)
        for s in (2 * TS - 2, 2 * TS - 1):
            add_output(dve, s, s % TS)

    def decode_pe(pe):
        pe.wait_ge(po_used, 2 * G)
        pe.wait_ge(ld_kc, 16)
        pe.wait_ge(new_done, 2)
        for b in range(TS):
            for g in range(G):
                keys = KCS[:, 2 * b + g // 2, :].rearrange("p (n g) -> p g n", g=2)[:, g % 2, :]
                nc.tensor.matmul(PSUM[0:NCMP, 7, b * NH + g * HREP:b * NH + (g + 1) * HREP], keys,
                                 QS[:, b * NH + g * HREP:b * NH + (g + 1) * HREP], start=True, stop=True)
        for k in range(2):
            last = nc.tensor.matmul(PSUM[:, 7, P + 32 * k:P + 32 * k + 32], QS[:, :], KS6[:, 2 + 2 * k, :], start=True, stop=True)
        sp_pe.made_by(last, "cmp scores")
        sp_act.wait(pe, "cmp copied")
        sp_pe.made_by(nc.tensor.transpose(PSUM[:, 0, 0:NCMP], PCS[0:NCMP, 0, :], IDENT[0:NCMP, 0:NCMP]), "cmp rows")
        sp_dve.wait(pe, "cmp probs")
        sp_pe.made_by(nc.tensor.transpose(PSUM[0:NCMP, 1, 0:P], PCS[:, 1, 0:NCMP], IDENT[:, :]), "cmp turned")
        sp_act.wait(pe, "cmp turned kept")
        sp_pe.made_by(nc.tensor.matmul(PSUM[:, 2, 0:30], PCS[0:NCMP, 0, :], TOB[0:NCMP, :], start=True, stop=True), "block scores")
        sp_act.wait(pe, "block scores kept")
        sp_pe.made_by(nc.tensor.matmul(PSUM[:, 3, 0:30], SAME[:, :], SM[:, 32:62], start=True, stop=True), "block sums")
        sp_dve.wait(pe, "cmp gated")
        sp_pe.made_by(nc.tensor.transpose(PSUM[0:NCMP, 1, P:2 * P], PCS[:, 1, 0:NCMP], IDENT[:, :]), "cmp gated turned")
        sp_act.wait(pe, "cmp gated kept")
        sp_dve.wait(pe, "slc taken")
        zeros_pe(range(2, 7), start=True, stop=False)
        key_pages_pe(pe, "sk")
        key_pages_pe(pe, "wk")
        sp_pe.made_by(zeros_pe(range(2, 6), start=False, stop=True), "slc rows")
        sp_pe.made_by(zeros_pe([6], start=False, stop=True), "win rows")
        nc.tensor.matmul(PSUM[:, 7, 0:P], ZERO[:, :], QS[:, :], start=True, stop=False, skip_group_check=True)
        pe.wait_ge(ld_vc, 16)
        for b in range(TS):
            for g in range(G):
                cols = slice(b * NH + g * HREP, b * NH + (g + 1) * HREP)
                nc.tensor.matmul(PSUM[:, 7, cols], VCS[0:NCMP, 2 * b + g // 2, (g % 2) * DH:(g % 2 + 1) * DH],
                                 PCS[0:NCMP, 2, cols], start=False, stop=False, skip_group_check=True)
        sp_dve.wait(pe, "new probs")
        for k in range(2):
            last = nc.tensor.transpose(PSUM[0:32, 0, k * P:(k + 1) * P], RTW[:, k, :], IDENT[:, :])
        sp_pe.made_by(last, "new turned")
        for j in range(PAGES):
            last = nc.tensor.transpose(PSUM[:, 2 + j // 4, (j % 4) * P:(j % 4 + 1) * P], S2[:, j * P:(j + 1) * P], IDENT[:, :])
        sp_pe.made_by(last, "slc turned")
        for j in range(4):
            last = nc.tensor.transpose(PSUM[:, 6, j * P:(j + 1) * P], S2W[:, j * P:(j + 1) * P], IDENT[:, :])
        sp_pe.made_by(last, "win turned")
        sp_dve.wait(pe, "new kept")
        for k in range(2):
            nc.tensor.matmul(PSUM[:, 7, 0:P], SNAT[:, 3 + 2 * k, :], RTK[0:32, k, :], start=False, stop=False, skip_group_check=True)
        sp_pe.made_by(nc.tensor.matmul(PSUM[:, 7, 0:P], ZERO[:, :], QS[:, :], start=False, stop=True, skip_group_check=True), "cmp out")
        value_pages_pe(pe, "sv")
        value_pages_pe(pe, "wv")
        output_taken(pe, 2 * TS - 1)
        turn_output(1)

    def decode_act(act):
        A = nc.scalar.activation
        sp_pe.wait(act, "cmp scores")
        sp_act.made_by(A(PCS[0:NCMP, 0, :], PSUM[0:NCMP, 7, 0:P], ACT.Copy), "cmp copied")
        sp_dve.wait(act, "cmp negmax")
        sp_act.made_by(A(PCS[:, 1, 0:NCMP], PSUM[:, 0, 0:NCMP], ACT.Exp, scale=SCALE, bias=SM[:, 1:2], accum_out=SM[:, 2:3]), "cmp exp")
        sp_pe.wait(act, "cmp turned")
        sp_act.made_by(A(PCS[0:NCMP, 0, :], PSUM[0:NCMP, 1, 0:P], ACT.Copy), "cmp turned kept")
        sp_pe.wait(act, "block scores")
        sp_act.made_by(A(SM[:, 32:62], PSUM[:, 2, 0:30], ACT.Copy), "block scores kept")
        sp_pe.wait(act, "cmp gated turned")
        sp_act.made_by(A(PCS[0:NCMP, 2, :], PSUM[0:NCMP, 1, P:2 * P], ACT.Copy), "cmp gated kept")
        branch_loads(act, "cache_slc_k", "sk", 1)
        branch_loads(act, "state_win_k", "wk", 1)
        sp_dve.wait(act, "slc negmax")
        sp_act.made_by(A(S2[:, :], S2[:, :], ACT.Exp, scale=SCALE, bias=SM[:, 5:6], accum_out=SM[:, 6:7]), "slc exp")
        sp_act.made_by(A(SM[:, 24:25], SM[:, 20:21], ACT.Exp, scale=SCALE, bias=SM[:, 5:6]), "slc new exp")
        sp_dve.wait(act, "win negmax")
        sp_act.made_by(A(S2W[:, 1:WIN], S2W[:, 1:WIN], ACT.Exp, scale=SCALE, bias=SM[:, 9:10], accum_out=SM[:, 10:11]), "win exp")
        sp_act.made_by(A(SM[:, 25:26], SM[:, 21:22], ACT.Exp, scale=SCALE, bias=SM[:, 9:10]), "win new exp")
        sp_pe.wait(act, "slc turned")
        sp_act.made_by(A(SCT[:, 0:8, :].rearrange("p (b j) c -> p b (j c)", b=2), PSUM[:, 2:4, :], ACT.Copy), "slc kept")
        sp_pe.wait(act, "win turned")
        sp_act.made_by(A(STW[:, :, :].rearrange("p j c -> p (j c)"), PSUM[:, 6, :], ACT.Copy), "win kept")
        branch_loads(act, "cache_slc_v", "sv", 1)
        branch_loads(act, "state_win_v", "wv", 1)

    def decode_dve(dve):
        def link(ins):
            chain[0] += 1
            ins.then_inc(ch_dve, 1)
            dve.wait_ge(ch_dve, chain[0])

        dve.wait_ge(po_used, 2 * G)
        dve.wait_ge(gates_moved, 48)
        link(V.memset(ZERO[:, :], 0.0))
        link(V.memset(QPAD[:, :, :], 0.0))
        sp_act.wait(dve, "cmp copied")
        for k in range(2):
            link(V.tensor_tensor(RTW[:, k, :], PSUM[:, 7, P + 32 * k:P + 32 * k + 32], BD[:, :], ALU.mult))
            link(V.tensor_reduce(SM[:, 20 + k:21 + k], RTW[:, k, :], AX.X, ALU.add))
        sp_pe.wait(dve, "cmp rows")
        link(V.tensor_reduce(SM[:, 0:1], PSUM[:, 0, 0:NCMP], AX.X, ALU.max))
        sp_dve.made_by(V.tensor_scalar(SM[:, 1:2], SM[:, 0:1], -SCALE, None, ALU.mult), "cmp negmax")
        sp_act.wait(dve, "cmp exp")
        link(V.tensor_scalar(SM[:, 2:3], SM[:, 2:3], 1e-30, None, ALU.max))
        link(V.reciprocal(SM[:, 3:4], SM[:, 2:3]))
        sp_dve.made_by(V.tensor_scalar(PCS[:, 1, 0:NCMP], PCS[:, 1, 0:NCMP], SM[:, 3:4], None, ALU.mult), "cmp probs")
        sp_pe.wait(dve, "cmp turned")
        sp_dve.made_by(V.tensor_scalar(PCS[:, 1, 0:NCMP], PCS[:, 1, 0:NCMP], GSM[:, 0:1], None, ALU.mult), "cmp gated")
        sp_pe.wait(dve, "block sums")
        link(V.tensor_copy(SM[:, 32:62], PSUM[:, 3, 0:30]))
        one = SM[:, 32:62].unsqueeze(2).to_broadcast([P, 30, 30])
        other = SM[:, 32:62].unsqueeze(1).to_broadcast([P, 30, 30])
        link(V.tensor_tensor(RK[:, 0, :, :], other, one, ALU.is_equal))
        link(V.tensor_tensor(RK[:, 0, :, :], RK[:, 0, :, :], EARL[:, :, :], ALU.mult))
        link(V.tensor_tensor(RK[:, 1, :, :], other, one, ALU.is_gt))
        link(V.tensor_tensor(RK[:, 0, :, :], RK[:, 0, :, :], RK[:, 1, :, :], ALU.add))
        link(V.memset(BLK[:, :], 0.0))
        link(V.tensor_reduce(BLK[:, 1:31], RK[:, 0, :, :], AX.X, ALU.add))
        link(V.tensor_scalar(BLK[:, 1:31], BLK[:, 1:31], 12.5, NEG, ALU.is_gt, ALU.mult))
        sp_dve.made_by(V.memset(S2W[:, 0:1], 0.0), "slc taken")
        key_pages_dve(dve, "sk")
        key_pages_dve(dve, "wk")
        sp_pe.wait(dve, "slc rows")
        link(V.tensor_tensor(S2[:, :].rearrange("p (b k) -> p b k", k=64), PSUM[:, 2:6, :].rearrange("p b (j k) -> p (b j) k", k=64),
                             BLK[:, :].unsqueeze(2).to_broadcast([P, 32, 64]), ALU.add))
        link(V.tensor_reduce(SM[:, 4:5], S2[:, :], AX.X, ALU.max))
        link(V.tensor_tensor(SM[:, 4:5], SM[:, 4:5], SM[:, 20:21], ALU.max))
        sp_dve.made_by(V.tensor_scalar(SM[:, 5:6], SM[:, 4:5], -SCALE, None, ALU.mult), "slc negmax")
        sp_pe.wait(dve, "win rows")
        link(V.tensor_copy(S2W[:, 1:WIN], PSUM[:, 6, 1:WIN]))
        link(V.tensor_reduce(SM[:, 8:9], S2W[:, 1:WIN], AX.X, ALU.max))
        link(V.tensor_tensor(SM[:, 8:9], SM[:, 8:9], SM[:, 21:22], ALU.max))
        sp_dve.made_by(V.tensor_scalar(SM[:, 9:10], SM[:, 8:9], -SCALE, None, ALU.mult), "win negmax")
        for k, (name, rows, at) in enumerate((("slc", S2[:, :], 6), ("win", S2W[:, 1:WIN], 10))):
            sp_act.wait(dve, name + " new exp")
            link(V.tensor_tensor(SM[:, at:at + 1], SM[:, at:at + 1], SM[:, 24 + k:25 + k], ALU.add))
            link(V.reciprocal(SM[:, at + 1:at + 2], SM[:, at:at + 1]))
            link(V.tensor_tensor(SM[:, at + 1:at + 2], SM[:, at + 1:at + 2], GSM[:, 1 + k:2 + k], ALU.mult))
            link(V.tensor_tensor(SM[:, 24 + k:25 + k], SM[:, 24 + k:25 + k], SM[:, at + 1:at + 2], ALU.mult))
            sp_dve.made_by(V.tensor_scalar(rows, rows, SM[:, at + 1:at + 2], None, ALU.mult), name + " probs")
        link(V.tensor_scalar(RTW[:, 0, :], BD[:, :], SM[:, 24:25], None, ALU.mult))
        sp_dve.made_by(V.tensor_scalar(RTW[:, 1, :], BD[:, :], SM[:, 25:26], None, ALU.mult), "new probs")
        sp_pe.wait(dve, "new turned")
        sp_dve.made_by(V.tensor_copy(RTK[0:32, :, :].rearrange("p k c -> p (k c)"), PSUM[0:32, 0, 0:2 * P]), "new kept")
        sp_pe.wait(dve, "slc turned")
        sp_dve.made_by(V.tensor_copy(SCT[:, 8:16, :].rearrange("p (b j) c -> p b (j c)", b=2), PSUM[:, 4:6, :]), "slc kept")
        sp_pe.wait(dve, "cmp out")
        link(V.tensor_copy(DACC[:, :], PSUM[:, 7, 0:P]))
        sp_act.wait(dve, "win kept")
        value_pages_dve(dve, "sv")
        value_pages_dve(dve, "wv")
        last_outputs_dve(dve)
        dve.wait_ge(pv_added, 2 * TS)
        sp_dve.made_by(V.tensor_copy(QT[:, :, TP:T].rearrange("p h b -> p b h"), DACC[:, :].rearrange("p (b h) -> p b h", h=NH)), "out")

    def decode_sp_keys(sp):
        pc_pe.wait(sp, "v hidden")
        sp.dma_start(KCS[:, :, :], kscr.rearrange("b g p n -> p (b g) n")).then_inc(ld_kc, 16)
        branch_loads(sp, "cache_slc_k", "sk", 0)
        branch_loads(sp, "state_win_k", "wk", 0)
        sp_pe.wait(sp, "cmp scores")
        sp.dma_start(VCS[0:NCMP, :, :], vscr.rearrange("b g p n -> p (b g) n")).then_inc(ld_vc, 16)
        branch_loads(sp, "cache_slc_v", "sv", 0)
        branch_loads(sp, "state_win_v", "wv", 0)

    def out_heads_act(act):
        sp_dve.wait(act, "out")
        for c in range(KC):
            nc.scalar.activation(XH[:, c, :], QT[:, c, :], ACT.Copy).then_inc(xh_done, 1)

    def out_rests_dve(dve):
        for c in range(KC):
            dve.wait_ge(xh_done, XLS["att"] + c + 1)
            V.tensor_tensor(XL[:, c, :], QT[:, c, :], XH[:, c, :].bitcast(F32), ALU.subtract).then_inc(xl_done, 1)

    fin_tp, fin_used = sem("fin_tp"), sem("fin_used")

    def final_pe(pe):
        rms_pe(pe, "fin")
        for c in range(KC):
            pe.wait_ge(hn_done, 16 * HNS["fin"] + c + 1)
            if c >= 4:
                pe.wait_ge(fin_used, c - 3)
            bank = c % 4
            for k in range(2):
                nc.tensor.transpose(PSUM[:, bank, k * P:(k + 1) * P], HN[:, c % 4, k * P:(k + 1) * P], IDENT[:, :])
            nc.tensor.transpose(PSUM[0:TS, bank, TP:TP + P], HN[:, c % 4, TP:T], IDENT[:, :]).then_inc(fin_tp, 1)

    def final_dve(dve):
        rms_dve(dve, "fin")

        def gained(c):
            if c >= 4:
                dve.wait_ge(fin_tp, c - 3)
            V.scalar_tensor_tensor(out=HN[:, c % 4, :], in0=X[:, c, :], scalar=GV[:, 16 * NFIN + c:16 * NFIN + c + 1],
                                   in1=RSTD[:, :], op0=ALU.mult, op1=ALU.mult).then_inc(hn_done, 1)

        for c in range(KC):
            gained(c)
            if c >= 1:
                take(dve, c - 1)
        take(dve, KC - 1)

    def take(dve, c):
        dve.wait_ge(fin_tp, c + 1)
        V.tensor_copy(YN[:, :, c * P:(c + 1) * P], PSUM[:, c % 4, 0:TP].rearrange("p (q d) -> p q d", q=2))
        V.tensor_copy(YS[:, c * P:(c + 1) * P], PSUM[0:TS, c % 4, TP:TP + P]).then_inc(fin_used, 1)

    def final_sp(sp):
        y = out["y_prompt"][0].rearrange("(q p) d -> p q d", p=P)
        for h in range(4):
            sl = slice(h * 512, (h + 1) * 512)
            sp.wait_ge(fin_used, 4 * h + 4)
            sp.dma_start(y[:, :, sl], YN[:, :, sl]).then_inc(stored, 16)
        sp.dma_start(out["y_sample"].rearrange("b o d -> (b o) d"), YS[:, :]).then_inc(stored, 16)

    block = stack.enter_context(nc.Block())

    @block.sync
    def _(sp):
        start_sp(sp)
        stage1_sp(sp)
        states_sp(sp)
        phase_sp(sp, "glu", skip=RING)
        ffn_sp(sp, 0)
        before_kv_sp(sp)
        phase_sp(sp, "kv")
        phase_sp(sp, "q")
        phase_sp(sp, "o", only=RING)
        attention_small_sp(sp)
        rows_sp(sp)
        shift_sp(sp)
        decode_sp_keys(sp)
        sp.wait_ge(att_used, ATT_PAGES)
        phase_sp(sp, "o", skip=RING)
        ffn_sp(sp, 1)
        final_sp(sp)
        sp.wait_ge(stored, STATES_STORED + 16 * 5)
        sp.wait_ge(rows_stored, ROWS_STORED)
        for k in range(2):
            sp.wait_ge(nat_stored[k], NAT_STORED)
        sp.wait_ge(shift_stored, SHIFT_STORED)
        sp.wait_ge(cmp_kept, 16 * 4 * NKV)

    @block.tensor
    def _(pe):
        start_pe(pe)
        stage1_pe(pe)
        states_pe(pe)
        phase_pe(pe, "glu", XH, XL, None)
        ffn_pe(pe, 0)
        rms_pe(pe, "kv")
        phase_pe(pe, "kv", XH, XL, normed_ready(pe, "kv"))
        phase_pe(pe, "q", XH, XL, normed_ready(pe, "mix1"))
        rotate_pe(pe)
        prompt_cmp_pe(pe)
        prompt_att_pe(pe)
        decode_pe(pe)
        phase_pe(pe, "o", XH, XL, normed_ready(pe, "att"))
        ffn_pe(pe, 1)
        final_pe(pe)

    @block.scalar
    def _(act):
        start_act(act)
        stage1_act(act)
        glu_act(act)
        ffn_act(act, 0)
        rms_act(act, "kv")
        norm_act(act, "kv")
        keep_groups_act(act, "kv", lambda g: KVT[:, ds(g, 1), :, :].rearrange("p o h t -> p (o h) t"))
        norm_act(act, "mix1", by_name["q"].base - TAP_UNITS)
        keep_groups_act(act, "q", lambda g: QT[:, ds(4 * g, 4), :])
        rotate_act_all(act)
        prompt_cmp_act(act)
        prompt_att_act(act)
        decode_act(act)
        out_heads_act(act)
        add_act(act, "o", True)
        ffn_act(act, 1)
        rms_act(act, "fin")

    @block.vector
    def _(dve):
        start_dve(dve)
        stage1_dve(dve)
        states_dve(dve)
        glu_dve(dve)
        ffn_dve(dve, 0)
        rms_dve(dve, "kv")
        norm_dve(dve, "kv", NKV_GAIN)
        only_split_dve(dve, "kv")
        norm_dve(dve, "mix1", NMIX[1])
        only_split_dve(dve, "q")
        rotate_dve_all(dve)
        prompt_cmp_dve(dve)
        prompt_att_dve(dve)
        decode_dve(dve)
        out_rests_dve(dve)
        add_dve(dve, "o", True)
        ffn_dve(dve, 1)
        final_dve(dve)

    @block.gpsimd
    def _(pool):
        nc.gpsimd.memset(EPSB[:, 2:3], 0.0).then_inc(hl_done, 1)
        stage1_pool(pool)
        ffn_pool(pool, 0)
        ffn_pool(pool, 1)

    stack.close()


_INS = ['x_prompt', 'x_sample', 'state_ssm_re', 'state_ssm_im', 'cache_cmp_k', 'cache_cmp_v', 'cache_slc_k',
        'cache_slc_v', 'state_win_k', 'state_win_v', 'page_table', 'p_prompt', 'p_sample', 'norm_mix_g',
        'norm_ffn_g', 'norm_ple_g', 'norm_kv_g', 'norm_final_g', 'ssm_a_re', 'ssm_a_im', 'ssm_log_dt',
        'ssm_b_re', 'ssm_b_im', 'ssm_c_re', 'ssm_c_im', 'ssm_d', 'ssm_w_glu', 'ssm_b_glu', 'kv_w', 'cmp_k_w1',
        'cmp_k_b1', 'cmp_k_w2', 'cmp_v_w1', 'cmp_v_b1', 'cmp_v_w2', 'nsa_w_q', 'nsa_w_gate', 'nsa_b_gate',
        'nsa_w_o', 'ffn_w_gate', 'ffn_w_up', 'ffn_w_down', 'ple_w_gate', 'ple_w_proj']
_ROWS_P, _ROWS_S = (1, TP, G, DH), (TS, 1, G, DH)
_OUTS = [('y_prompt', (1, TP, D)), ('y_sample', (TS, 1, D)),
         ('ssm_re_prompt', (1, 1, 128, ST)), ('ssm_im_prompt', (1, 1, 128, ST)),
         ('cmp_k_prompt', _ROWS_P), ('cmp_v_prompt', _ROWS_P), ('slc_k_prompt', _ROWS_P), ('slc_v_prompt', _ROWS_P),
         ('win_k_prompt', _ROWS_P), ('win_v_prompt', _ROWS_P),
         ('ssm_re_sample', (1, TS, 128, ST)), ('ssm_im_sample', (1, TS, 128, ST)),
         ('cmp_k_sample', _ROWS_S), ('cmp_v_sample', _ROWS_S), ('slc_k_sample', _ROWS_S), ('slc_v_sample', _ROWS_S),
         ('win_k_sample', (TS, WIN, G, DH)), ('win_v_sample', (TS, WIN, G, DH))]


def kernel(**inputs):
    import numpy as _np
    import concourse.bacc as _bacc
    from concourse.bass_utils import run_bass_kernel_spmd as _run

    nc = _bacc.Bacc("TRN2", target_bir_lowering=False, num_devices=1)
    arrays, io, out = {}, {}, {}

    def add(name, a):
        arrays[f"in_{name}"] = a
        io[name] = nc.dram_tensor(f"in_{name}", a.shape, mybir.dt.from_np(a.dtype), kind="ExternalInput").ap()

    for name in _INS:
        add(name, _np.ascontiguousarray(inputs[name]))
    for name, a in shape_constants().items():
        add("k_" + name, _np.ascontiguousarray(a))
    for name, shape in _OUTS:
        out[name] = nc.dram_tensor(f"out_{name}", shape, F32, kind="ExternalOutput").ap()
    trunk_kernel(nc, io, out)
    r = _run(nc, [arrays], core_ids=[0])
    return tuple(r.results[0][f"out_{name}"] for name, _ in _OUTS)
```
